# Optimizing a Trainium2 kernel written in Bass

```python
import math
import jax
import jax.numpy as jnp
from jax import lax
import numpy as np
import jax, jax.numpy as jnp

D_MODEL = 1024
BATCH = 1
SEQ = 256
DEPTH = 1

CTX_LEN = 256
GRID_W = 64
N_HEADS = 8
HEAD_DIM = 64
D_ATTN = N_HEADS * 2 * HEAD_DIM
D_HYENA = D_MODEL
SHORT_CONV = 3
FILTER_EMB = 33
FILTER_ORDER = 64
DECAY_TARGET = 1e-2
FAST_DECAY_PCT = 0.3
SLOW_DECAY_PCT = 1.5
D_FF = 2816
ROPE_THETA = 10000.0
Q_BLOCK = 128
N_MOD = 9
N_PROJ = 3 * D_HYENA + 3 * D_ATTN + 2 * D_MODEL
SPLITS = (3 * D_HYENA, 3 * D_HYENA + D_ATTN, 3 * D_HYENA + 2 * D_ATTN, 3 * D_HYENA + 3 * D_ATTN)
EPS = 1e-6


def rmsnorm(x, g):
    xf = x.astype(jnp.float32)
    y = xf * lax.rsqrt(jnp.mean(xf * xf, axis=-1, keepdims=True) + EPS)
    return (y * g.astype(jnp.float32)).astype(x.dtype)

def modulate(x, shift, scale):
    return x * (1.0 + scale) + shift

def swiglu(x, w_in, w_out):
    gate, up = jnp.split(x @ w_in, 2, axis=-1)
    return (jax.nn.silu(gate) * up) @ w_out

def ffn_half(s, shift, scale, gate, g_pre, g_post, w_in, w_out):
    h = swiglu(modulate(rmsnorm(s, g_pre), shift, scale), w_in, w_out)
    return s + 0.5 * gate * rmsnorm(h, g_post)

def short_conv(x, w, b):
    L = x.shape[1]
    pad = SHORT_CONV // 2
    xp = jnp.pad(x, ((0, 0), (pad, pad), (0, 0)))
    return sum(xp[:, j:j + L] * w[j] for j in range(SHORT_CONV)) + b

def hyena_kernel(L, w1, b1, w2, b2, w3, b3, w4, freq):
    f32 = jnp.float32
    bands = (FILTER_EMB - 1) // 2
    t = jnp.linspace(0.0, 1.0, L, dtype=f32)[:, None]
    w = 2.0 * math.pi * jnp.arange(L, dtype=f32)[:, None] / L
    f = jnp.linspace(1e-4, bands - 1, bands, dtype=f32)[None, :]
    z = jnp.concatenate([t, jnp.cos(f * w), -jnp.sin(f * w)], axis=-1)
    h = jnp.sin(freq * (z @ w1 + b1))
    h = jnp.sin(freq * (h @ w2 + b2))
    h = jnp.sin(freq * (h @ w3 + b3))
    h = (h @ w4).astype(f32)
    deltas = jnp.linspace(math.log(DECAY_TARGET) / SLOW_DECAY_PCT,
                          math.log(DECAY_TARGET) / FAST_DECAY_PCT, D_HYENA, dtype=f32)
    decay = jnp.exp(-t * jnp.abs(deltas))
    h_fwd, h_bwd = jnp.split(h, 2, axis=-1)
    h_fwd = h_fwd * decay
    h_bwd = h_bwd * decay
    k = jnp.concatenate([h_fwd, jnp.zeros_like(h_fwd[:1]), h_bwd[:0:-1]], axis=0)
    return k / (jnp.sum(jnp.abs(k), axis=0, keepdims=True) + EPS)

def bidir_long_conv(u, k):
    L = u.shape[1]
    uf = jnp.fft.rfft(u.astype(jnp.float32), n=2 * L, axis=1)
    kf = jnp.fft.rfft(k, n=2 * L, axis=0)
    y = jnp.fft.irfft(uf * kf[None], n=2 * L, axis=1)[:, :L]
    return y.astype(u.dtype)

def hyena_branch(z_hy, conv_w, conv_b, filt, hy_bias):
    z = short_conv(z_hy, conv_w, conv_b)
    x0, x1, v = jnp.split(z, 3, axis=-1)
    k = hyena_kernel(z.shape[1], *filt)
    u = v * x1
    y = bidir_long_conv(u, k) + u * hy_bias
    return y * x0

def axial_rope_tables(L):
    rows = L // GRID_W
    r, col = jnp.meshgrid(jnp.arange(rows), jnp.arange(GRID_W), indexing='ij')
    r = r.reshape(-1).astype(jnp.float32)
    col = col.reshape(-1).astype(jnp.float32)
    half = HEAD_DIM // 2
    inv = ROPE_THETA ** (-jnp.arange(0, half, 2, dtype=jnp.float32) / half)
    ang = jnp.stack([r[:, None] * inv, col[:, None] * inv], axis=1)
    return jnp.cos(ang), jnp.sin(ang)

def apply_axial_rope(x, cos, sin):
    B, L = x.shape[:2]
    xr = x.reshape(B, L, N_HEADS, 2, 2, 2, HEAD_DIM // 4)
    x0, x1 = xr[..., 0, :], xr[..., 1, :]
    c = cos[None, :, None, None]
    s = sin[None, :, None, None]
    out = jnp.stack([x0 * c - x1 * s, x0 * s + x1 * c], axis=-2)
    return out.reshape(x.shape).astype(x.dtype)

def diff_attention(q, k, v, lam):
    B, L = q.shape[:2]
    nb = L // Q_BLOCK
    qb = jnp.moveaxis(q.reshape(B, nb, Q_BLOCK, N_HEADS, 2, HEAD_DIM), 1, 0)

    def block(qblk):
        s = jnp.einsum('bqhmd,bkhmd->bhmqk', qblk, k).astype(jnp.float32) * (HEAD_DIM ** -0.5)
        p = jax.nn.softmax(s, axis=-1)
        p = p[:, :, 0] - lam * p[:, :, 1]
        return jnp.einsum('bhqk,bkhe->bqhe', p.astype(v.dtype), v)

    o = lax.map(block, qb)
    return jnp.moveaxis(o, 0, 1).reshape(B, L, N_HEADS, 2 * HEAD_DIM)

def context_kv(h, w_in):
    B, L = h.shape[:2]
    k, v = jnp.split(h @ w_in[:, SPLITS[1]:SPLITS[3]], 2, axis=-1)
    return k.reshape(B, L, N_HEADS, 2, HEAD_DIM), v.reshape(B, L, N_HEADS, 2 * HEAD_DIM)

def token_mixer(h, w_in, conv_w, conv_b, filt, hy_bias, lam, lam_init, subln_g,
                w_hy_out, w_da_out, w_o, rope, ctx_kv):
    B, L = h.shape[:2]
    z_hy, q, k, v, gates = jnp.split(h @ w_in, SPLITS, axis=-1)
    y_hy = hyena_branch(z_hy, conv_w, conv_b, filt, hy_bias) @ w_hy_out
    q = q.reshape(B, L, N_HEADS, 2, HEAD_DIM)
    k = k.reshape(B, L, N_HEADS, 2, HEAD_DIM)
    v = v.reshape(B, L, N_HEADS, 2 * HEAD_DIM)
    if rope is not None:
        q = apply_axial_rope(q, *rope)
        k = apply_axial_rope(k, *rope)
    if ctx_kv is not None:
        k = jnp.concatenate([k, ctx_kv[0]], axis=1)
        v = jnp.concatenate([v, ctx_kv[1]], axis=1)
    o = diff_attention(q, k, v, lam)
    o = rmsnorm(o, subln_g) * (1.0 - lam_init)
    y_da = o.reshape(B, L, D_ATTN) @ w_da_out
    g_hy, g_da = jnp.split(jax.nn.sigmoid(gates), 2, axis=-1)
    return (g_hy * y_hy + g_da * y_da) @ w_o

def first_inputs(seed: int = 0) -> dict:
    key = jax.random.key(seed)
    ks = jax.random.split(key, 32)
    f32 = jnp.float32

    def nrm(k, shape, scale):
        return jax.random.normal(k, shape, f32) * scale

    return {
        'x': nrm(ks[0], (BATCH, SEQ, D_MODEL), 1.0),
        'c': nrm(ks[1], (BATCH, D_MODEL), 1.0),
        'ctx': nrm(ks[2], (BATCH, CTX_LEN, D_MODEL), 1.0),
        'c_ctx': nrm(ks[3], (D_MODEL,), 1.0),
        'w_ada': nrm(ks[4], (DEPTH, D_MODEL, N_MOD * D_MODEL), 0.5 * D_MODEL ** -0.5),
        'b_ada': nrm(ks[5], (DEPTH, N_MOD * D_MODEL), 0.01),
        'norm_g': 1.0 + nrm(ks[6], (DEPTH, 6, D_MODEL), 0.02),
        'w_ff_in': nrm(ks[7], (DEPTH, 2, D_MODEL, 2 * D_FF), D_MODEL ** -0.5),
        'w_ff_out': nrm(ks[8], (DEPTH, 2, D_FF, D_MODEL), D_FF ** -0.5),
        'w_in': nrm(ks[9], (DEPTH, D_MODEL, N_PROJ), D_MODEL ** -0.5),
        'hy_conv_w': nrm(ks[10], (DEPTH, SHORT_CONV, 3 * D_HYENA), SHORT_CONV ** -0.5),
        'hy_conv_b': nrm(ks[11], (DEPTH, 3 * D_HYENA), 0.01),
        'filt_w1': nrm(ks[12], (DEPTH, FILTER_EMB, FILTER_ORDER), FILTER_EMB ** -0.5),
        'filt_b1': nrm(ks[13], (DEPTH, FILTER_ORDER), 0.1),
        'filt_w2': nrm(ks[14], (DEPTH, FILTER_ORDER, FILTER_ORDER), FILTER_ORDER ** -0.5),
        'filt_b2': nrm(ks[15], (DEPTH, FILTER_ORDER), 0.1),
        'filt_w3': nrm(ks[16], (DEPTH, FILTER_ORDER, FILTER_ORDER), FILTER_ORDER ** -0.5),
        'filt_b3': nrm(ks[17], (DEPTH, FILTER_ORDER), 0.1),
        'filt_w4': nrm(ks[18], (DEPTH, FILTER_ORDER, 2 * D_HYENA), FILTER_ORDER ** -0.5),
        'filt_freq': 1.0 + nrm(ks[19], (DEPTH, FILTER_ORDER), 0.01),
        'hy_bias': nrm(ks[20], (DEPTH, D_HYENA), 0.1),
        'lambda_q1': nrm(ks[21], (DEPTH, HEAD_DIM), 0.1),
        'lambda_k1': nrm(ks[22], (DEPTH, HEAD_DIM), 0.1),
        'lambda_q2': nrm(ks[23], (DEPTH, HEAD_DIM), 0.1),
        'lambda_k2': nrm(ks[24], (DEPTH, HEAD_DIM), 0.1),
        'subln_g': 1.0 + nrm(ks[25], (DEPTH, 2 * HEAD_DIM), 0.02),
        'w_hy_out': nrm(ks[26], (DEPTH, D_HYENA, D_MODEL), D_HYENA ** -0.5),
        'w_da_out': nrm(ks[27], (DEPTH, D_ATTN, D_MODEL), D_ATTN ** -0.5),
        'w_o': nrm(ks[28], (DEPTH, D_MODEL, D_MODEL), D_MODEL ** -0.5),
    }

def first_block(x, c, ctx, c_ctx, w_ada, b_ada, norm_g, w_ff_in, w_ff_out, w_in,
              hy_conv_w, hy_conv_b, filt_w1, filt_b1, filt_w2, filt_b2, filt_w3, filt_b3,
              filt_w4, filt_freq, hy_bias, lambda_q1, lambda_k1, lambda_q2, lambda_k2,
              subln_g, w_hy_out, w_da_out, w_o):
    rope = axial_rope_tables(x.shape[1])
    xs, cs = x, ctx
    for l in range(DEPTH):
        lam_init = 0.8 - 0.6 * math.exp(-0.3 * l)
        lam = (jnp.exp(jnp.sum(lambda_q1[l] * lambda_k1[l]).astype(jnp.float32))
               - jnp.exp(jnp.sum(lambda_q2[l] * lambda_k2[l]).astype(jnp.float32)) + lam_init)
        mod_x = jnp.split((jax.nn.silu(c) @ w_ada[l] + b_ada[l])[:, None, :], N_MOD, axis=-1)
        mod_c = jnp.split((jax.nn.silu(c_ctx) @ w_ada[l] + b_ada[l])[None, None, :], N_MOD, axis=-1)
        g = norm_g[l]
        filt = (filt_w1[l], filt_b1[l], filt_w2[l], filt_b2[l], filt_w3[l], filt_b3[l],
                filt_w4[l], filt_freq[l])
        mixer_params = (w_in[l], hy_conv_w[l], hy_conv_b[l], filt, hy_bias[l], lam, lam_init,
                        subln_g[l], w_hy_out[l], w_da_out[l], w_o[l])
        xs = ffn_half(xs, mod_x[0], mod_x[1], mod_x[2], g[0], g[1], w_ff_in[l, 0], w_ff_out[l, 0])
        cs = ffn_half(cs, mod_c[0], mod_c[1], mod_c[2], g[0], g[1], w_ff_in[l, 0], w_ff_out[l, 0])
        hx = modulate(rmsnorm(xs, g[2]), mod_x[3], mod_x[4])
        hc = modulate(rmsnorm(cs, g[2]), mod_c[3], mod_c[4])
        y = token_mixer(hx, *mixer_params, rope, context_kv(hc, w_in[l]))
        xs = xs + mod_x[5] * rmsnorm(y, g[3])
        if l < DEPTH - 1:
            yc = token_mixer(hc, *mixer_params, None, None)
            cs = cs + mod_c[5] * rmsnorm(yc, g[3])
            cs = ffn_half(cs, mod_c[6], mod_c[7], mod_c[8], g[4], g[5], w_ff_in[l, 1], w_ff_out[l, 1])
        xs = ffn_half(xs, mod_x[6], mod_x[7], mod_x[8], g[4], g[5], w_ff_in[l, 1], w_ff_out[l, 1])
    return xs


RWKV_HEAD = 64
RWKV_HEADS = 8
RWKV_DIM = RWKV_HEADS * RWKV_HEAD
W_LORA = 64
A_LORA = 64
G_LORA = 128
DECAY_SCALE = math.exp(-0.5)
LNX_EPS = 64e-5
ATT_HEADS = 8
ATT_KV_HEADS = 2
ATT_HEAD = 64
ATT_DIM = ATT_HEADS * ATT_HEAD
KV_DIM = ATT_KV_HEADS * ATT_HEAD
WINDOW = 128
BLOCK = 128
NEG_INF = -1e30
N_EXPERTS = 16
CAPACITY_FACTOR = 2
EXPERT_FF = 1024
NORM_EPS = 1e-6

RWKV_SPLITS = (RWKV_DIM, 2 * RWKV_DIM, 3 * RWKV_DIM, 3 * RWKV_DIM + G_LORA,
               3 * RWKV_DIM + G_LORA + W_LORA, 3 * RWKV_DIM + G_LORA + 2 * W_LORA,
               3 * RWKV_DIM + G_LORA + 2 * W_LORA + A_LORA)
RWKV_COLS = 3 * RWKV_DIM + G_LORA + 2 * W_LORA + 2 * A_LORA
ATT_SPLITS = (ATT_DIM, ATT_DIM + KV_DIM, ATT_DIM + 2 * KV_DIM, ATT_DIM + 2 * KV_DIM + D_MODEL)
IN_COLS = RWKV_COLS + ATT_DIM + 2 * KV_DIM + 2 * D_MODEL


def rms_norm(x, g):
    xf = x.astype(jnp.float32)
    y = xf * lax.rsqrt(jnp.mean(xf * xf, axis=-1, keepdims=True) + NORM_EPS)
    return (y * g.astype(jnp.float32)).astype(x.dtype)

def centred_token_shift(u, mu_prev, mu_next):
    prev = jnp.pad(u, ((0, 0), (1, 0), (0, 0)))[:, :-1]
    nxt = jnp.pad(u, ((0, 0), (0, 1), (0, 0)))[:, 1:]
    return u + mu_prev * (prev - u) + mu_next * (nxt - u)

def wkv7_scan(r, decay, k, v, kk, a, reverse):
    B, T, H, N = r.shape
    xs = tuple(jnp.moveaxis(t.astype(jnp.float32), 1, 0) for t in (r, decay, k, v, kk, a))

    def step(S, inp):
        r_t, w_t, k_t, v_t, kk_t, a_t = inp
        s_kk = jnp.einsum('bhij,bhj->bhi', S, kk_t)
        S = (S * w_t[:, :, None, :]
             - s_kk[..., None] * (a_t * kk_t)[:, :, None, :]
             + v_t[..., None] * k_t[:, :, None, :])
        return S, jnp.einsum('bhij,bhj->bhi', S, r_t)

    S0 = jnp.zeros((B, H, N, N), jnp.float32)
    _, y = lax.scan(step, S0, xs, reverse=reverse)
    return jnp.moveaxis(y, 0, 1)

def rwkv7_bidir(u, w0_f, w_up_f, w0_b, w_up_b, a0_f, a_up_f, a0_b, a_up_b, g_up, k_k, k_a, r_k, ln_w, ln_b):
    f32 = jnp.float32
    B, T, _ = u.shape
    r, k, v, g_lo, wf_lo, wb_lo, af_lo, ab_lo = jnp.split(u, RWKV_SPLITS, axis=-1)

    def heads(t):
        return t.reshape(B, T, RWKV_HEADS, RWKV_HEAD)

    def decay(w0, lo, up):
        return jnp.exp(-DECAY_SCALE * jax.nn.sigmoid((w0 + jnp.tanh(lo) @ up).astype(f32)))

    def icl_rate(a0, lo, up):
        return jax.nn.sigmoid((a0 + lo @ up).astype(f32))

    kf = k.astype(f32)
    kk = heads(kf * k_k.astype(f32))
    kk = kk / jnp.maximum(jnp.sqrt(jnp.sum(kk * kk, axis=-1, keepdims=True)), 1e-12)
    a_f = icl_rate(a0_f, af_lo, a_up_f)
    a_b = icl_rate(a0_b, ab_lo, a_up_b)
    k_f = heads(kf * (1.0 + (a_f - 1.0) * k_a.astype(f32)))
    k_b = heads(kf * (1.0 + (a_b - 1.0) * k_a.astype(f32)))
    r4 = heads(r.astype(f32))
    v4 = heads(v.astype(f32))

    wkv = (wkv7_scan(r4, heads(decay(w0_f, wf_lo, w_up_f)), k_f, v4, kk, heads(a_f), False)
           + wkv7_scan(r4, heads(decay(w0_b, wb_lo, w_up_b)), k_b, v4, kk, heads(a_b), True))

    mean = jnp.mean(wkv, axis=-1, keepdims=True)
    var = jnp.mean(jnp.square(wkv - mean), axis=-1, keepdims=True)
    normed = ((wkv - mean) * lax.rsqrt(var + LNX_EPS)).reshape(B, T, RWKV_DIM)
    normed = normed * ln_w.astype(f32) + ln_b.astype(f32)

    rk = r_k.astype(f32)
    bonus = ((jnp.sum(r4 * k_f * rk, axis=-1, keepdims=True)
              + jnp.sum(r4 * k_b * rk, axis=-1, keepdims=True)) * v4).reshape(B, T, RWKV_DIM)
    g = (jax.nn.sigmoid(g_lo) @ g_up).astype(f32)
    return ((normed + bonus) * g).astype(u.dtype)

def alibi_slopes(n_heads):
    return 2.0 ** (-8.0 * np.arange(1, n_heads + 1) / n_heads)

def banded_gqa_attention(q, k, v, sink):
    f32 = jnp.float32
    B, T, HQ, DH = q.shape
    G = HQ // ATT_KV_HEADS
    nb = T // BLOCK
    span = BLOCK + 2 * WINDOW
    q = q.reshape(B, T, ATT_KV_HEADS, G, DH) * (DH ** -0.5)
    kp = jnp.pad(k, ((0, 0), (WINDOW, WINDOW), (0, 0), (0, 0)))
    vp = jnp.pad(v, ((0, 0), (WINDOW, WINDOW), (0, 0), (0, 0)))
    slopes = jnp.asarray(alibi_slopes(HQ), f32).reshape(ATT_KV_HEADS, G)
    sink_l = sink.astype(f32).reshape(1, ATT_KV_HEADS, G, 1, 1)
    l_idx = jnp.arange(BLOCK)
    j_idx = jnp.arange(span)
    rel = j_idx[None, :] - WINDOW - l_idx[:, None]
    in_window = jnp.abs(rel) <= WINDOW
    alibi = -slopes[:, :, None, None] * jnp.abs(rel).astype(f32)

    def one_block(i):
        start = i * BLOCK
        qb = lax.dynamic_slice_in_dim(q, start, BLOCK, axis=1)
        kb = lax.dynamic_slice_in_dim(kp, start, span, axis=1)
        vb = lax.dynamic_slice_in_dim(vp, start, span, axis=1)
        key_pos = start - WINDOW + j_idx
        valid = in_window & ((key_pos >= 0) & (key_pos < T))[None, :]
        s = jnp.einsum('blkgd,bjkd->bkglj', qb, kb).astype(f32) + alibi
        s = jnp.where(valid, s, NEG_INF)
        m = jnp.maximum(jnp.max(s, axis=-1, keepdims=True), sink_l)
        p = jnp.exp(s - m)
        denom = jnp.sum(p, axis=-1, keepdims=True) + jnp.exp(sink_l - m)
        return jnp.einsum('bkglj,bjkd->blkgd', (p / denom).astype(vb.dtype), vb)

    out = lax.map(one_block, jnp.arange(nb))
    return jnp.moveaxis(out, 0, 1).reshape(B, T, HQ * DH)

def expert_choice_moe(h, w_router, w_gate, w_up, w_down):
    B, T, D = h.shape
    cap = CAPACITY_FACTOR * T // N_EXPERTS
    affinity = jax.nn.softmax((h @ w_router).astype(jnp.float32), axis=-1)
    top_vals, top_idx = lax.top_k(jnp.swapaxes(affinity, 1, 2), cap)
    b_idx = jnp.arange(B)[:, None, None]
    xs = h[b_idx, top_idx]
    hid = jax.nn.silu(jnp.einsum('becd,edf->becf', xs, w_gate)) * jnp.einsum('becd,edf->becf', xs, w_up)
    ys = jnp.einsum('becf,efd->becd', hid, w_down) * top_vals[..., None].astype(h.dtype)
    return jnp.zeros_like(h).at[b_idx, top_idx].add(ys)

def second_inputs(seed: int = 0) -> dict:
    key = jax.random.key(seed)
    ks = jax.random.split(key, 32)
    L, D, f32 = DEPTH, D_MODEL, jnp.float32
    nrm = lambda k, shape, s: (jax.random.normal(k, shape, f32) * s)
    return {
        'x': nrm(ks[0], (BATCH, SEQ, D), 1.0),
        'norm_mix_g': 1.0 + nrm(ks[1], (L, D), 0.1),
        'w_in': nrm(ks[2], (L, D, IN_COLS), D ** -0.5),
        'mu_prev': jax.random.uniform(ks[3], (L, RWKV_COLS), f32, 0.05, 0.45),
        'mu_next': jax.random.uniform(ks[4], (L, RWKV_COLS), f32, 0.05, 0.45),
        'w0_f': nrm(ks[5], (L, RWKV_DIM), 1.0),
        'w_up_f': nrm(ks[6], (L, W_LORA, RWKV_DIM), 0.5 * W_LORA ** -0.5),
        'w0_b': nrm(ks[7], (L, RWKV_DIM), 1.0),
        'w_up_b': nrm(ks[8], (L, W_LORA, RWKV_DIM), 0.5 * W_LORA ** -0.5),
        'a0_f': nrm(ks[9], (L, RWKV_DIM), 0.5),
        'a_up_f': nrm(ks[10], (L, A_LORA, RWKV_DIM), 0.5 * A_LORA ** -0.5),
        'a0_b': nrm(ks[11], (L, RWKV_DIM), 0.5),
        'a_up_b': nrm(ks[12], (L, A_LORA, RWKV_DIM), 0.5 * A_LORA ** -0.5),
        'g_up': nrm(ks[13], (L, G_LORA, RWKV_DIM), G_LORA ** -0.5),
        'k_k': 0.85 + nrm(ks[14], (L, RWKV_DIM), 0.05),
        'k_a': 1.0 + nrm(ks[15], (L, RWKV_DIM), 0.05),
        'r_k': nrm(ks[16], (L, RWKV_HEADS, RWKV_HEAD), 0.1),
        'ln_x_w': 1.0 + nrm(ks[17], (L, RWKV_DIM), 0.1),
        'ln_x_b': nrm(ks[18], (L, RWKV_DIM), 0.02),
        'attn_sink': nrm(ks[19], (L, ATT_HEADS), 0.5),
        'w_proj_rwkv': nrm(ks[20], (L, RWKV_DIM, D), RWKV_DIM ** -0.5),
        'w_proj_attn': nrm(ks[21], (L, ATT_DIM, D), ATT_DIM ** -0.5),
        'w_out': nrm(ks[22], (L, D, D), D ** -0.5),
        'norm_ffn_g': 1.0 + nrm(ks[23], (L, D), 0.1),
        'w_router': nrm(ks[24], (L, D, N_EXPERTS), D ** -0.5),
        'exp_w_gate': nrm(ks[25], (L, N_EXPERTS, D, EXPERT_FF), D ** -0.5),
        'exp_w_up': nrm(ks[26], (L, N_EXPERTS, D, EXPERT_FF), D ** -0.5),
        'exp_w_down': nrm(ks[27], (L, N_EXPERTS, EXPERT_FF, D), EXPERT_FF ** -0.5),
        'norm_final_g': 1.0 + nrm(ks[28], (D,), 0.1),
    }

def second_block(x, norm_mix_g, w_in, mu_prev, mu_next, w0_f, w_up_f, w0_b, w_up_b, a0_f, a_up_f, a0_b, a_up_b,
              g_up, k_k, k_a, r_k, ln_x_w, ln_x_b, attn_sink, w_proj_rwkv, w_proj_attn, w_out, norm_ffn_g,
              w_router, exp_w_gate, exp_w_up, exp_w_down, norm_final_g):
    B, T, _ = x.shape
    for layer in range(DEPTH):
        h = rms_norm(x, norm_mix_g[layer])
        u = h @ w_in[layer]
        u_rwkv = centred_token_shift(u[..., :RWKV_COLS], mu_prev[layer], mu_next[layer])
        q, k_att, v_att, gl_rwkv, gl_attn = jnp.split(u[..., RWKV_COLS:], ATT_SPLITS, axis=-1)
        y_rwkv = rwkv7_bidir(u_rwkv, w0_f[layer], w_up_f[layer], w0_b[layer], w_up_b[layer],
                             a0_f[layer], a_up_f[layer], a0_b[layer], a_up_b[layer], g_up[layer],
                             k_k[layer], k_a[layer], r_k[layer], ln_x_w[layer], ln_x_b[layer])
        y_attn = banded_gqa_attention(q.reshape(B, T, ATT_HEADS, ATT_HEAD),
                                      k_att.reshape(B, T, ATT_KV_HEADS, ATT_HEAD),
                                      v_att.reshape(B, T, ATT_KV_HEADS, ATT_HEAD), attn_sink[layer])
        merged = (jax.nn.sigmoid(gl_rwkv) * (y_rwkv @ w_proj_rwkv[layer])
                  + jax.nn.sigmoid(gl_attn) * (y_attn @ w_proj_attn[layer]))
        x = x + merged @ w_out[layer]
        x = x + expert_choice_moe(rms_norm(x, norm_ffn_g[layer]), w_router[layer],
                                  exp_w_gate[layer], exp_w_up[layer], exp_w_down[layer])
    return rms_norm(x, norm_final_g)


def setup_inputs(seed=0):
    out = dict(first_inputs(seed))
    for name, value in second_inputs(seed + 1).items():
        if name != "x":
            out[name + "_2"] = value
    return out


def reference(
    x, c, ctx, c_ctx, w_ada, b_ada, norm_g, w_ff_in, w_ff_out, w_in, hy_conv_w, hy_conv_b,
    filt_w1, filt_b1, filt_w2, filt_b2, filt_w3, filt_b3, filt_w4, filt_freq, hy_bias,
    lambda_q1, lambda_k1, lambda_q2, lambda_k2, subln_g, w_hy_out, w_da_out, w_o, norm_mix_g_2,
    w_in_2, mu_prev_2, mu_next_2, w0_f_2, w_up_f_2, w0_b_2, w_up_b_2, a0_f_2, a_up_f_2, a0_b_2,
    a_up_b_2, g_up_2, k_k_2, k_a_2, r_k_2, ln_x_w_2, ln_x_b_2, attn_sink_2, w_proj_rwkv_2,
    w_proj_attn_2, w_out_2, norm_ffn_g_2, w_router_2, exp_w_gate_2, exp_w_up_2, exp_w_down_2,
    norm_final_g_2,
):
    x = first_block(
        x, c, ctx, c_ctx, w_ada, b_ada, norm_g, w_ff_in, w_ff_out, w_in, hy_conv_w, hy_conv_b,
        filt_w1, filt_b1, filt_w2, filt_b2, filt_w3, filt_b3, filt_w4, filt_freq, hy_bias,
        lambda_q1, lambda_k1, lambda_q2, lambda_k2, subln_g, w_hy_out, w_da_out, w_o,
    )
    return second_block(
        x, norm_mix_g_2, w_in_2, mu_prev_2, mu_next_2, w0_f_2, w_up_f_2, w0_b_2, w_up_b_2,
        a0_f_2, a_up_f_2, a0_b_2, a_up_b_2, g_up_2, k_k_2, k_a_2, r_k_2, ln_x_w_2, ln_x_b_2,
        attn_sink_2, w_proj_rwkv_2, w_proj_attn_2, w_out_2, norm_ffn_g_2, w_router_2,
        exp_w_gate_2, exp_w_up_2, exp_w_down_2, norm_final_g_2,
    )


_drawn_inputs = setup_inputs


def setup_inputs(seed=0):
    import zlib

    import numpy as np

    out = dict(_drawn_inputs(seed))
    spreads = {}
    factors = {'norm_g': 3.218,
     'hy_conv_b': 47.46,
     'filt_b1': 5.152,
     'filt_b2': 4.894,
     'filt_b3': 3.166,
     'filt_freq': 8.0,
     'lambda_q1': 5.025,
     'lambda_k1': 7.134,
     'subln_g': 92.349,
     'w_up_f_2': 3.54,
     'w_up_b_2': 3.886,
     'k_k_2': 200.0,
     'ln_x_b_2': 7.825,
     'attn_sink_2': 14.864,
     'a_up_f_2': 2.703,
     'a_up_b_2': 2.935,
     'k_a_2': 3.783,
     'ln_x_w_2': 2.955}
    for name, (base, spread) in spreads.items():
        noise = np.random.default_rng([zlib.crc32(name.encode()), seed]).standard_normal(out[name].shape)
        drawn = base * np.exp(spread * noise) if base else spread * noise
        out[name] = jnp.asarray(drawn.astype(out[name].dtype))
    for name, factor in factors.items():
        out[name] = (out[name] * factor).astype(out[name].dtype)
    return out
```

```python
import math

import numpy as np
import concourse.bass as bass
from concourse import mybir
from contextlib import ExitStack

P = 128
D = 1024
T = 256
KD = D // P
D_FF = 2816
FT = D_FF // P
N_MOD = 9
HEADS = 8
N_EXP = 16
CAP = 2 * T // N_EXP
FFT = 2 * T
SLAB = 16 * P
RING = 4
EX_RING = 12
LAM_INIT = 0.8 - 0.6 * math.exp(-0.3 * 0)
DECAY_SCALE = math.exp(-0.5)
EPS = 1e-6
LNX_EPS = 64e-5
RW_TILES = [13, 14, 4, 5, 6, 7, 0, 1, 2, 3, 8, 9, 10, 11, 12]
US_K, US_R, US_V, US_G = 2, 6, 10, 14

COLS = [("b_ada", 72), ("g", 48), ("cw0", 24), ("cw1", 24), ("cw2", 24), ("cb", 24), ("hyb", 8), ("subg", 1),
        ("fb", 3), ("ffreq", 1), ("lam", 4), ("nmix", 8), ("mup", 15), ("mun", 15), ("w0", 8), ("a0", 8),
        ("kk", 4), ("ka", 4), ("rk", 4), ("lnw", 4), ("lnb", 4), ("nffn", 8), ("nfin", 8), ("sink", 8)]
COL0 = {}
_at = 0
for _n, _c in COLS:
    COL0[_n] = _at
    _at += _c
N_COLS = _at

DENSE = [("ada_head", 8), ("ffn1_in", FT + 28), ("ffn1_out", 11), ("z", 12), ("qk", 8), ("v", 4), ("gates", 8),
         ("hyout", 4), ("daout", 4), ("wo", 4), ("ffn2_in", FT), ("ffn2_out", 11), ("rwkv", 18.5 + 8)]
N_DENSE = int(math.ceil(sum(n for _, n in DENSE)))


def _rot(n, banks=(0, 1, 2, 3)):
    return {b: len(range(i, n, len(banks))) for i, b in enumerate(banks)}


STAGES = [("mlp", {5: 3}), ("lam", {7: 1}), ("w4", _rot(8)), ("knorm", {5: 1}), ("kdft", _rot(10)),
          ("ada_head", {6: 1, 7: 1}), ("ffn1_in", {0: 11, 1: 11, 2: 11, 3: 11, 7: 6, 6: 1}), ("ffn1_out", _rot(8)),
          ("z", _rot(24)), ("qk", {**_rot(16), 5: 8, 6: 8}), ("ut", {5: 2, 6: 2}), ("v", _rot(16)),
          ("uspec", {0: 2, 1: 2, 2: 2, 3: 2}), ("yinv", _rot(8)), ("gates", _rot(16)),
          ("att", {0: 8, 1: 8, 2: 8, 3: 8, 5: 8, 6: 8, 7: 8}), ("onorm", {5: 1, 0: 1, 1: 1, 2: 1, 3: 1}),
          ("hyout", _rot(8)), ("daout", _rot(8)), ("wo", _rot(8)),
          ("ffn2_in", {0: 11, 1: 11, 2: 11, 3: 11}), ("ffn2_out", _rot(8)),
          ("shift", _rot(15)), ("lora", {0: 2, 1: 2, 2: 2, 3: 2}), ("kkn", {5: 1, 6: 1}), ("toks", {5: 3, 6: 3})]
for _s in range(2):
    STAGES += [(f"am{_s}", {0: 4, 1: 4, 2: 4, 3: 4}), (f"inv{_s}", {b: 14 for b in (0, 1, 2, 3, 5, 6)}),
               (f"tail{_s}", {0: 2, 1: 2, 2: 2, 3: 2, **({5: 2} if _s == 0 else {})})]
STAGES += [("gn", {0: 2, 1: 2, 2: 1, 3: 1, 5: 1, 6: 1}), ("aq", _rot(6)), ("batt", {0: 2, 1: 2, 2: 2, 3: 2, 5: 4, 6: 4, 7: 4}),
           ("gates2", _rot(16)), ("projr", _rot(8)), ("proja", _rot(8)), ("wout", _rot(8)),
           ("route", {0: 1, 1: 1, 2: 1}), ("htok", {5: 2, 6: 2}), ("gather", _rot(8)), ("oht", {5: 1, 6: 1}),
           ("moe", {0: 12, 1: 12, 2: 12, 3: 12, 5: 8, 6: 8, 7: 8})]
FILLS = {}
_n = [0] * 8
for _name, _uses in STAGES:
    FILLS[_name] = list(_n)
    for _b, _c in _uses.items():
        _n[_b] += _c


def constants():
    f32 = np.float32
    out = {}
    t = np.linspace(0.0, 1.0, T, dtype=f32)[:, None]
    w = (f32(2.0 * math.pi) * np.arange(T, dtype=f32)[:, None] / f32(T)).astype(f32)
    f = np.linspace(1e-4, 15, 16, dtype=f32)[None, :]
    z = np.concatenate([t, np.cos(f * w), -np.sin(f * w)], axis=-1).astype(f32)
    out["zT"] = np.ascontiguousarray(z.T)
    deltas = np.linspace(math.log(1e-2) / 1.5, math.log(1e-2) / 0.3, D, dtype=f32)
    decay = np.exp(-t * np.abs(deltas)).astype(f32)
    out["decay"] = decay.reshape(2, P, D).transpose(1, 0, 2).reshape(P, 2 * D).copy()
    tt = np.arange(T)[:, None].astype(np.float64)
    ff = np.arange(T)[None, :].astype(np.float64)
    re = np.cos(2 * np.pi * tt * ff / FFT)
    im = -np.sin(2 * np.pi * tt * ff / FFT)
    last = (-1.0) ** np.arange(T)
    fu = np.concatenate([re, im], axis=1)
    fu[:, T] = last
    out["Fu"] = fu.reshape(2, P, 2 * T).transpose(1, 0, 2).reshape(P, 4 * T).astype(f32)
    alt = re[:, :P].copy()
    alt[:, 0] = last
    fwd = np.concatenate([re, im, alt], axis=1)
    bwd = np.concatenate([re, -im, alt], axis=1)
    bwd[0] = 0.0
    fk = np.concatenate([fwd, bwd], axis=0)
    out["FK"] = fk.reshape(4, P, 5 * P).transpose(1, 0, 2).reshape(P, 20 * P).astype(f32)
    inv = np.concatenate([2 * re.T, 2 * im.T], axis=0) / FFT
    inv[0] = 1.0 / FFT
    inv[T] = last / FFT
    out["Finv"] = inv.reshape(4, P, T).transpose(1, 0, 2).reshape(P, 4 * T).astype(f32)
    p = np.arange(P)
    pos = np.arange(T)
    invf = (f32(10000.0) ** (-np.arange(0, 32, 2, dtype=f32) / f32(32))).astype(f32)
    rc = np.where(((p % 64) // 32 == 0)[:, None], (pos // 64)[None, :], (pos % 64)[None, :]).astype(f32)
    ang = (rc * invf[p % 16][:, None]).astype(f32)
    out["rope"] = np.concatenate([np.cos(ang), np.sin(ang)], axis=1).astype(f32)
    eye = np.eye(P, dtype=f32)
    blk = (p[:, None] // 64 == p[None, :] // 64).astype(f32)
    perm = np.zeros((P, P), f32)
    for m in range(P):
        if m % 32 < 16:
            perm[m + 16, m] = -1.0
        else:
            perm[m - 16, m] = 1.0
    nobwd0 = np.ones((P, 1), f32)
    nobwd0[0] = 0.0
    headsel = np.zeros((P, HEADS, HEADS), f32)
    headbc = np.zeros((HEADS, HEADS, P), f32)
    for j in range(HEADS):
        headsel[:, j, j] = 1.0
        headbc[j, j, :] = 1.0
    iota = np.broadcast_to(np.arange(1, CAP + 1, dtype=f32), (P, CAP))
    out["small"] = np.concatenate([eye, np.ones((P, P), f32), blk, perm, nobwd0, headsel.reshape(P, 64), iota], axis=1)
    out["headbc"] = headbc.reshape(HEADS, HEADS * P)
    s, u = p[:, None], p[None, :]
    keep = [np.concatenate([a, b, a, b], axis=1) for a, b in (((s < u), (s <= u)), ((s > u), (s >= u)))]
    lev = []
    for flip in (False, True):
        for lv in range(7):
            m = 1 << lv
            a, b = (u, s) if flip else (s, u)
            lev.append((a // (2 * m) == b // (2 * m)) & (a // m % 2 == 0) & (b // m % 2 == 1))
    q = np.arange(2)[None, :, None] * P + p[:, None, None]
    rel = np.abs(np.arange(T)[None, None, :] - q).astype(np.float64)
    dist = np.where(rel <= 128, -rel, -1e33)
    out["masks"] = np.concatenate([*keep, *lev, dist.reshape(P, 2 * T)], axis=1).astype(f32)
    return out


N_SMALL = 4 * P + 1 + 64 + CAP
N_MASKS = 2 * 4 * P + 14 * P + 2 * T


def blocks(w):
    k, n = w.shape
    return w.reshape(k // P, P, n // P, P).transpose(2, 0, 1, 3)


def slabs(b):
    b = b.reshape(-1, P, P)
    pad = -len(b) % 16
    if pad:
        b = np.concatenate([b, np.zeros((pad, P, P), b.dtype)])
    return b.reshape(-1, 16, P, P).transpose(0, 2, 1, 3).reshape(-1, P, SLAB)


def wide(w, n=256):
    return w.reshape(KD, P, -1, n).transpose(2, 1, 0, 3).reshape(-1, P, KD * n)


def cols(v):
    return v.reshape(-1, P).T


def pad_rows(v):
    return np.concatenate([v, np.zeros((P - v.shape[0], v.shape[1]), v.dtype)], axis=0)


def lay_out(inp):
    g = {k: np.asarray(v) for k, v in inp.items()}
    ada = blocks(g["w_ada"][0]).reshape(N_MOD, KD, KD, P, P)

    def ffn_in(w):
        b = blocks(w)
        return np.stack([b[:FT], b[FT:]], axis=1)

    f1 = ffn_in(g["w_ff_in"][0, 0])
    mixed = []
    for i in range(5):
        mixed += [slabs(ada[2 + i]), slabs(f1[4 * i:4 * i + 4])]
    mixed += [slabs(ada[7:9]), slabs(f1[20:22])]
    w_in = g["w_in"][0]
    w2 = g["w_in_2"][0]
    b2 = blocks(w2)
    order = [h for j in range(4) for h in (j, 4 + j)]
    qcols = np.concatenate([np.arange(1920 + 64 * h, 1920 + 64 * h + 64) for h in order])
    arows = np.concatenate([np.arange(64 * h, 64 * h + 64) for h in order])
    bq = blocks(w2[:, qcols])
    second = np.concatenate([
        *(b2[i:i + 1].reshape(-1, P, P) for i in RW_TILES), bq.reshape(-1, P, P), b2[19:37].reshape(-1, P, P),
        blocks(g["w_proj_rwkv_2"][0]).reshape(-1, P, P), blocks(g["w_proj_attn_2"][0][arows]).reshape(-1, P, P),
        blocks(g["w_out_2"][0]).reshape(-1, P, P)])
    dense = np.concatenate([
        slabs(ada[0:2]), *mixed, slabs(blocks(g["w_ff_out"][0, 0])), slabs(blocks(w_in[:, :5 * D])),
        wide(w_in[:, 5 * D:6 * D]), slabs(blocks(w_in[:, 6 * D:])), slabs(blocks(g["w_hy_out"][0])),
        slabs(blocks(g["w_da_out"][0])), slabs(blocks(g["w_o"][0])), slabs(ffn_in(g["w_ff_in"][0, 1])),
        slabs(blocks(g["w_ff_out"][0, 1])), slabs(second)])
    assert dense.shape == (N_DENSE, P, SLAB), dense.shape
    ex = []
    for e in range(N_EXP):
        gu = np.stack([blocks(g["exp_w_gate_2"][0, e]), blocks(g["exp_w_up_2"][0, e])], axis=1)
        ex += [slabs(gu), slabs(blocks(g["exp_w_down_2"][0, e]))]
    experts = np.concatenate(ex)
    xT = g["x"][0].T.reshape(KD, P, T)
    cT = g["ctx"][0].T.reshape(KD, P, T)
    tokens = np.concatenate([xT, cT], axis=2).transpose(1, 0, 2).reshape(P, KD * 2 * T)
    cond = np.stack([cols(g["c"][0]), cols(g["c_ctx"])], axis=2).reshape(P, KD * 2)

    def mu(v):
        return v.reshape(15, P)[RW_TILES].T

    cw = g["hy_conv_w"][0]
    parts = {
        "b_ada": cols(g["b_ada"][0]), "g": cols(g["norm_g"][0]), "cw0": cols(cw[0]), "cw1": cols(cw[1]),
        "cw2": cols(cw[2]), "cb": cols(g["hy_conv_b"][0]), "hyb": cols(g["hy_bias"][0]), "subg": cols(g["subln_g"][0]),
        "fb": pad_rows(np.stack([g["filt_b1"][0], g["filt_b2"][0], g["filt_b3"][0]], axis=1)),
        "ffreq": pad_rows(g["filt_freq"][0][:, None]),
        "lam": pad_rows(np.stack([g["lambda_q1"][0], g["lambda_q2"][0], g["lambda_k1"][0], g["lambda_k2"][0]], axis=1)),
        "nmix": cols(g["norm_mix_g_2"][0]), "mup": mu(g["mu_prev_2"][0]), "mun": mu(g["mu_next_2"][0]),
        "w0": np.concatenate([cols(g["w0_f_2"][0]), cols(g["w0_b_2"][0])], axis=1),
        "a0": np.concatenate([cols(g["a0_f_2"][0]), cols(g["a0_b_2"][0])], axis=1),
        "kk": cols(g["k_k_2"][0]), "ka": cols(g["k_a_2"][0]), "rk": cols(g["r_k_2"][0].reshape(-1)),
        "lnw": cols(g["ln_x_w_2"][0]), "lnb": cols(g["ln_x_b_2"][0]), "nffn": cols(g["norm_ffn_g_2"][0]),
        "nfin": cols(g["norm_final_g_2"]), "sink": np.broadcast_to(g["attn_sink_2"][0][None, :], (P, HEADS))}
    cc = np.concatenate([parts[n] for n, _ in COLS], axis=1)
    assert cc.shape == (P, N_COLS)
    w1 = np.concatenate([g["filt_w1"][0], np.zeros((64 - 33, 64), np.float32)], axis=0)
    filt = np.concatenate([w1, g["filt_w2"][0], g["filt_w3"][0]], axis=1)
    lora = np.concatenate([
        np.concatenate([g["w_up_f_2"][0], g["w_up_b_2"][0]], axis=0),
        np.concatenate([g["a_up_f_2"][0], g["a_up_b_2"][0]], axis=0), g["g_up_2"][0]], axis=1)
    router = g["w_router_2"][0].reshape(KD, P, N_EXP).transpose(1, 0, 2).reshape(P, KD * N_EXP)
    out = {"dense": dense, "experts": experts, "tokens": tokens, "cond": cond, "cols": cc, "filt": filt,
           "w4": g["filt_w4"][0], "lora": lora, "router": router}
    out.update(constants())
    return {k: np.ascontiguousarray(v) for k, v in out.items()}


_ARRAYS = ["dense", "experts", "tokens", "cond", "cols", "filt", "w4", "lora", "router", "zT", "decay", "Fu", "FK",
           "Finv", "rope", "small", "headbc", "masks"]


def build(nc, dram, out_dram):
    fp32 = mybir.dt.float32
    ALU = mybir.AluOpType
    ACT = mybir.ActivationFunctionType
    AXX = mybir.AxisListType.X
    mult, add, sub, mx_op, mn_op = ALU.mult, ALU.add, ALU.subtract, ALU.max, ALU.min
    ds = bass.ds

    ctx = ExitStack()
    with ctx:
        def sb(name, shape):
            return ctx.enter_context(nc.sbuf_tensor(name, shape, fp32))

        def sem(name):
            return ctx.enter_context(nc.semaphore(name))

        PAGE = 2048
        N_PAGES = 23
        arena = sb("arena", [P, N_PAGES * PAGE])

        def page(at, words, a=None):
            lo = int(at * PAGE)
            v = arena[:, lo:lo + words]
            return v if a is None else v.rearrange("p (n a) -> p n a", a=a)

        ring = [page(i, SLAB, P) for i in range(RING)]
        ring_wide = [page(i, SLAB, 256) for i in range(RING)]
        ring_flat = [page(i, SLAB) for i in range(RING)]
        ex_ring = [page(11 + i, SLAB, P) for i in range(EX_RING)]
        ex_flat = [page(11 + i, SLAB) for i in range(EX_RING)]

        col_sb = sb("col_sb", [P, N_COLS])
        small = sb("small", [P, N_SMALL])
        router = sb("router", [P, KD * N_EXP])
        mods = sb("mods", [P, N_MOD * KD * 2])
        cond = sb("cond", [P, KD * 2])
        cond_s = sb("cond_s", [P, KD * 2])
        sil = sb("sil", [P, 2 * 512])
        sq = sb("sq", [P, 2 * 512])
        sd = sb("sd", [P, 512])
        rstd = sb("rstd", [P, 512])
        eps = sb("eps", [P, 2])
        gain = sb("gain", [P, 4 * KD])
        filt = page(20, 3 * 64)[0:64]
        zT = page(20.25, T)[0:33]
        fh = sb("fh", [64, 4 * T])
        tiny = sb("tiny", [P, 64])

        def c(name, j=0, n=1):
            return col_sb[:, COL0[name] + j:COL0[name] + j + n]

        ident = small[:, 0:P]
        ones = small[:, P:2 * P]
        ones2 = fh[0:N_EXP, T:2 * T]
        blk = small[:, 2 * P:3 * P]
        perm = small[:, 3 * P:4 * P]
        nobwd0 = small[:, 4 * P:4 * P + 1]
        headsel = small[:, 4 * P + 1:4 * P + 65].rearrange("p (h m) -> p h m", m=HEADS)
        headbc = page(18.5, HEADS * P, P)[0:HEADS]
        iota = small[:, 4 * P + 65:N_SMALL]
        mods_v = mods[:, :].rearrange("p (m j r) -> p m j r", m=N_MOD, r=2)
        cond_v = cond_s[:, :].rearrange("p (k r) -> p k r", r=2)
        b_ada = c("b_ada", 0, 72).rearrange("p (m j) -> p m j", j=KD)
        sil_v = sil[:, :].rearrange("p (s n) -> p s n", n=512)
        sq_v = sq[:, :].rearrange("p (s n) -> p s n", n=512)
        gain_v = gain[:, :].rearrange("p (s j) -> p s j", j=KD)
        router_v = router[:, :].rearrange("p (k e) -> p k e", e=N_EXP)

        def mod(m, r):
            return mods_v[:, m, :, r]

        def g(i):
            return c("g", 8 * i, 8)

        X = page(4, 4096, 512)
        h1 = page(6, 4096, 512)
        hid1 = page(8, FT * 512, 512)
        y1 = page(14, 4096, 512)
        hfil = page(8, 4096, 1024)
        habs = page(10, 4096, 1024)
        FK = page(12, 20 * P, 5 * P)
        decay = page(13.5, 2048, 1024)
        w4 = page(14.5, 2048)
        Kspec = page(16, 5 * 1024, 1024)
        Fu = page(18.5, 1024, 512)
        Finv = page(19, 1024, 256)
        rope = page(19.5, 512, 256)
        x0 = page(8, 2048, 256)
        u = page(9, 2048, 256)
        zv = page(10, 2048, 256)
        hy = page(10, 2048, 256)
        utok = page(11, 2048, 1024)
        yc = page(11, 2048, 256)
        Y = page(12, 4096, 1024)
        q_sb = page(22, 2048, 256)
        kT = page(20, 4096, 512)
        vtok = page(14, 4096, 1024)
        gates = page(12, 4096, 256)
        prob = page(8, 4096, 512)
        pT = page(16, 2048, 256)
        osq = page(17, 2048, 256)
        oT = page(11, 2048, 256)
        mix = page(18, 2048, 256)
        y2 = page(19, 2048, 256)
        x = page(7, 2048, 256)
        h = page(6, 2048, 256)
        hid2 = page(8, FT * 256, 256)
        y3 = page(15, 2048, 256)
        masks = page(13, N_MASKS)
        lora = page(17, 1024)
        g_up = page(13 + N_MASKS / PAGE, 512)
        keep = masks[:, 0:1024].rearrange("p (d n) -> p d n", n=512)
        level = masks[:, 1024:1024 + 14 * P].rearrange("p (l n) -> p l n", n=P)
        dist = masks[:, 1024 + 14 * P:N_MASKS].rearrange("p (q n) -> p q n", n=T)
        US = page(8, 15 * 256, 256)
        sig = page(10, 2048, 128)
        iclr = page(11, 2048, 256)
        cum = page(12, 2048, 128)
        D1 = page(15, 2048, 128)
        D2 = page(16, 2048, 128)
        Eneg = page(19, 2048, 128)
        Einc = page(20, 2048, 128)
        Eexc = page(21, 2048, 128)
        kkn = page(22, 1024, 128)
        kkr = page(22.5, 1024, 256)
        kdir = page(4, 2048, 128)
        nrm = page(5, 1024)
        gsq_kk = page(5.5, 1024)
        kkr_flat = page(22.5, 1024)
        kkn256 = page(22, 1024, 256)
        sig256 = page(10, 2048, 256)
        iclr128 = page(11, 2048, 128)
        QQw = page(15, 4096, 256)
        QQ = page(15, 4096, 128)
        KT = page(17, 2048, 128)
        BT = page(18, 2048, 128)
        AM = page(19, 8192, 512)
        XT = page(4, 2048, 128)
        Vtok = page(5, 1024, 512)
        wkv = page(5.5, 1024, 256)
        Xw = page(10, 1024, 128)
        NL = page(10.5, 1024, 128)
        Pw = page(11, 1024, 128)
        Wsb = page(11.5, 512, 64)
        nU = page(11.75, 512, 64)
        toks = page(12, 2048, 512)
        rkk = US[:, US_K:US_K + 4, :]
        gsq = page(19, 1024)
        dev = page(19.5, 1024)
        gsd = page(20, 1024)
        grs = page(20.5, 1024)
        yr = page(4, 1024, 256)
        qa = page(15, 1280, 256)
        va = page(15.75, 256, 128)
        oa = page(16, 1024, 256)
        gates2 = page(17, 4096, 256)
        bs = page(20, 1024, 256)
        bp = page(20.5, 1024, 256)
        bpT = page(21, 1024, 256)
        mix2 = page(8, 2048, 256)
        htok = page(9, 2048, 1024)
        OH = page(10, 1024, 512)
        OHW = page(0, 1024, 512)
        OHT = page(10.5, 1024, 256)
        xsT = page(4, 4096, 512)
        hidT = page(1, 512, 256)
        msil = page(1.5, 512, 128)
        ysT = page(2, 1024, 128)
        ys4 = page(2.5, 1024)
        outb = page(8, 2048, 256)
        state_v = sq[:, 0:512].rearrange("p (d j n) -> p d j n", d=2, n=64)
        scl = sb("scl", [P, 8])
        raw = sil[:, 0:512]
        rt = sil[:, 512:1024]
        raw_v = raw[:, :].rearrange("p (s n) -> p s n", n=256)

        ps = [ctx.enter_context(nc.psum_tensor(f"bank{i}", [P, 512], fp32)) for i in range(8)]

        slab_loaded = [sem(f"slab_loaded{i}") for i in range(RING)]
        slab_started = sem("slab_started")
        ex_loaded = [sem(f"ex_loaded{i}") for i in range(EX_RING)]
        ex_started = sem("ex_started")
        full = [sem(f"full{i}") for i in range(8)]
        evac = [sem(f"evac{i}") for i in range(8)]
        consts_in = sem("consts_in")
        filters_in = sem("filters_in")
        tokens_in = sem("tokens_in")
        spectra_in = sem("spectra_in")
        masks_in = sem("masks_in")
        eps_set = sem("eps_set")
        cond_ready = sem("cond_ready")
        sq_ready = sem("sq_ready")
        sq_used = sem("sq_used")
        h_ready = sem("h_ready")
        x_ready = sem("x_ready")
        dve_step = sem("dve_step")
        act_step = sem("act_step")
        router_in = sem("router_in")
        headbc_in = sem("headbc_in")
        kn_ready = sem("kn_ready")
        mu_ready = sem("mu_ready")
        es_ready = sem("es_ready")
        arg_ready = sem("arg_ready")
        sin_ready = sem("sin_ready")
        prod_ready = sem("prod_ready")
        habs_ready = sem("habs_ready")
        z_scaled = sem("z_scaled")
        u_ready = sem("u_ready")
        y_ready = sem("y_ready")
        hy_ready = sem("hy_ready")
        nm_ready = sem("nm_ready")
        p_ready = sem("p_ready")
        osq_ready = sem("osq_ready")
        hr_ready = sem("hr_ready")
        mix_ready = sem("mix_ready")
        us_scaled = sem("us_scaled")
        act_us = sem("act_us")
        kkr_ready = sem("kkr_ready")
        kksq_ready = sem("kksq_ready")
        ss_ready = sem("ss_ready")
        nrm_ready = sem("nrm_ready")
        logs_ready = sem("logs_ready")
        exps_ready = sem("exps_ready")
        qq_ready = sem("qq_ready")
        am_zero = sem("am_zero")
        x_init = sem("x_init")
        nl_ready = sem("nl_ready")
        gsq_ready = sem("gsq_ready")
        g_ready = sem("g_ready")
        aexp = sem("aexp")
        slot_ready = sem("slot_ready")
        oh_ready = sem("oh_ready")
        hid_silu = sem("hid_silu")
        out_ready = sem("out_ready")
        out_stored = sem("out_stored")

        block = ctx.enter_context(nc.Block())

        def take(pe, stage, b, k):
            v = FILLS[stage][b] + k
            if not (isinstance(v, int) and v == 0):
                pe.wait_ge(evac[b], v)

        def got(eng, stage, b, k):
            eng.wait_ge(full[b], FILLS[stage][b] + k + 1)

        def evacuated(eng, stage, b, k):
            eng.wait_ge(evac[b], FILLS[stage][b] + k + 1)

        class Steps:

            def __init__(self, eng, s):
                self.eng, self.s, self.n = eng, s, 0

            def do(self, ins):
                self.n += 1
                ins.then_inc(self.s, 1)

            def settle(self):
                self.eng.wait_ge(self.s, self.n)

        class Stream:

            def __init__(self, eng, loaded, started, slots, n):
                self.eng, self.loaded, self.started, self.slots, self.n = eng, loaded, started, slots, n
                self.slab, self.at, self.turn = 0, 0, 0

            def block(self):
                first = self.at == 0
                if first:
                    s = self.slab % self.n
                    self.eng.wait_ge(self.loaded[s], 16 * (self.slab // self.n + 1) + self.turn)
                blk_ap = self.slots[self.slab % self.n][:, self.at, :]
                self.at = (self.at + 1) % 16
                if self.at == 0:
                    self.slab += 1
                return blk_ap, first

            def loop(self, i, per):
                assert self.at == 0 and per % self.n == 0
                self.turn = i * (16 * per // self.n)

            def end_loop(self, per, turns):
                self.turn = 0
                self.slab += per * (turns - 1)

        @block.sync
        def _(sp):
            sp.dma_start(col_sb[:, :], dram["cols"]).then_inc(consts_in, 16)
            sp.dma_start(small[:, :], dram["small"]).then_inc(consts_in, 16)
            sp.dma_start(cond[:, :], dram["cond"]).then_inc(consts_in, 16)
            sp.dma_start(arena[:, 4 * PAGE:6 * PAGE], dram["tokens"]).then_inc(tokens_in, 16)
            for j in range(RING):
                sp.dma_start(ring_flat[j], dram["dense"][j]).then_inc(slab_loaded[j], 16)
            with sp.Fori(1, N_DENSE // RING) as i:
                for j in range(RING):
                    sp.wait_ge(slab_started, i * RING + (j - RING + 2))
                    sp.dma_start(ring_flat[j], dram["dense"][ds(i * RING + j, 1), :, :].rearrange("s p n -> (s p) n"))\
                        .then_inc(slab_loaded[j], 16)
            for m in range(N_DENSE - N_DENSE % RING, N_DENSE):
                sp.wait_ge(slab_started, m - RING + 2)
                sp.dma_start(ring_flat[m % RING], dram["dense"][m]).then_inc(slab_loaded[m % RING], 16)
            sp.wait_ge(mix_ready, 2)
            for j in range(EX_RING):
                sp.dma_start(ex_flat[j], dram["experts"][j]).then_inc(ex_loaded[j], 16)
            with sp.Fori(1, N_EXP) as i:
                for j in range(EX_RING):
                    sp.wait_ge(ex_started, i * EX_RING + (j - EX_RING + 2))
                    sp.dma_start(ex_flat[j],
                                 dram["experts"][ds(i * EX_RING + j, 1), :, :].rearrange("s p n -> (s p) n"))\
                        .then_inc(ex_loaded[j], 16)
            sp.wait_ge(out_ready, 1)
            sp.dma_start(out_dram, arena[:, 8 * PAGE:9 * PAGE]).then_inc(out_stored, 16)
            sp.wait_ge(out_stored, 16)

        @block.gpsimd
        def _(pool):
            nc.gpsimd.memset(eps[:, 0:1], EPS).then_inc(eps_set, 1)
            nc.gpsimd.memset(eps[:, 1:2], LNX_EPS).then_inc(eps_set, 1)
            pool.wait_ge(qq_ready, 1)
            nc.gpsimd.memset(page(19, 8192), 0.0).then_inc(am_zero, 1)
            for s in range(2):
                for pair in range(2):
                    for lv in range(7):
                        for d in range(2):
                            n = (s * 2 + pair) * 14 + lv * 2 + d
                            if lv == 0:
                                for b in range(4):
                                    evacuated(pool, f"am{s}", b, 2 * d + 1)
                            if n >= 2:
                                pb = 3 * d
                                got(pool, f"inv{s}" if (pair or lv) else f"inv{s - 1}", pb,
                                    pair * 7 + lv - 1 if (pair or lv) else 13)
                            u0 = 8 * d + 4 * pair
                            nc.gpsimd.tensor_tensor(NL[:, 4 * d:4 * d + 4, :], AM[:, u0:u0 + 4, 0:P],
                                                    level[:, 7 * d + lv:7 * d + lv + 1, :].to_broadcast([P, 4, P]), mult)\
                                .then_inc(nl_ready, 1)

        @block.tensor
        def _(pe):
            mm = nc.tensor.matmul
            st = Stream(pe, slab_loaded, slab_started, ring, RING)

            def product(out, k_tiles, rhs, last_sem=None):
                for k in range(k_tiles):
                    w, first = st.block()
                    ins = mm(out, lhsT=w, rhs=rhs(k), start=k == 0, stop=k == k_tiles - 1)
                    if first:
                        ins.then_inc(slab_started, 1)
                if last_sem is not None:
                    ins.then_inc(last_sem, 1)

            def stat(r, j, n):
                pe.wait_ge(sq_ready, 8 * r + j + 1)
                if j == 0 and r > 0:
                    pe.wait_ge(evac[4], r)
                mm(ps[4][:, 0:n], lhsT=ones, rhs=sq_v[:, j % 2, 0:n], start=j == 0, stop=j == 7)\
                    .then_inc(sq_used if j < 7 else full[4], 1)

            def tiles(stage, count, k_tiles, rhs, n=T, after=None):
                for t in range(count):
                    b = t % 4
                    take(pe, stage, b, t // 4)
                    product(ps[b][:, 0:n], k_tiles, rhs, full[b])
                    if after:
                        after(t)

            def ada(stage, b, k):
                take(pe, stage, b, k)
                for j in range(KD):
                    product(ps[b][:, 2 * j:2 * j + 2], KD, lambda kk_: cond_v[:, kk_, :],
                            full[b] if j == KD - 1 else None)

            pe.wait_ge(filters_in, 32)
            for n in range(3):
                take(pe, "mlp", 5, n)
                if n == 0:
                    mm(ps[5][0:64, 0:T], lhsT=filt[0:33, 0:64], rhs=zT[0:33, :], start=True, stop=True)\
                        .then_inc(full[5], 1)
                else:
                    pe.wait_ge(sin_ready, n)
                    mm(ps[5][0:64, 0:T], lhsT=filt[:, 64 * n:64 * n + 64], rhs=fh[:, 0:T], start=True, stop=True)\
                        .then_inc(full[5], 1)
            pe.wait_ge(consts_in, 48)
            pe.wait_ge(prod_ready, 1)
            mm(ps[7][:, 0:2], lhsT=ones[0:64, :], rhs=tiny[0:64, 0:2], start=True, stop=True).then_inc(full[7], 1)
            for j in range(KD):
                stat(0, j, 512)
            pe.wait_ge(sin_ready, 3)
            pe.wait_ge(spectra_in, 16 * 6)
            for n in range(8):
                tt, qq = n % 2, n // 2
                take(pe, "w4", n % 4, n // 4)
                mm(ps[n % 4][:, :], lhsT=fh[:, tt * P:tt * P + P], rhs=w4[0:64, qq * 512:qq * 512 + 512],
                   start=True, stop=True).then_inc(full[n % 4], 1)
            pe.wait_ge(cond_ready, 1)
            ada("ada_head", 6, 0)
            ada("ada_head", 7, 0)
            pe.wait_ge(habs_ready, 8)
            take(pe, "knorm", 5, 0)
            for ct in range(KD):
                for kt in range(4):
                    ins = mm(ps[5][:, ct:ct + 1], lhsT=habs[:, kt, ct * P:ct * P + P],
                             rhs=nobwd0 if kt == 2 else ones[:, 0:1], start=kt == 0, stop=kt == 3)
            ins.then_inc(full[5], 1)
            for n in range(10):
                take(pe, "kdft", n % 4, n // 4)
                for kt in range(4):
                    ins = mm(ps[n % 4][:, :], lhsT=FK[:, kt, (n // 2) * P:(n // 2) * P + P],
                             rhs=hfil[:, kt, (n % 2) * 512:(n % 2) * 512 + 512], start=kt == 0, stop=kt == 3)
                ins.then_inc(full[n % 4], 1)

            def ffn(stage, r, src, hid, n, with_ada):
                def pair(q_, use):
                    for b in (2 * (q_ % 2), 2 * (q_ % 2) + 1):
                        take(pe, stage + "_in", b, use)
                        product(ps[b][:, 0:n], KD, lambda k: src[:, k, 0:n], full[b])
                per = 8 if with_ada else 4
                with pe.Fori(0, 5) as i:
                    st.loop(i, per)
                    if with_ada:
                        ada(stage + "_in", 7, i)
                    for q_ in range(4):
                        pair(q_, i * 2 + q_ // 2)
                st.end_loop(per, 5)
                if with_ada:
                    ada(stage + "_in", 7, 5)
                    ada(stage + "_in", 6, 0)
                pair(0, 10)
                pair(1, 10)
                evacuated(pe, stage + "_in", 1, 10)
                evacuated(pe, stage + "_in", 3, 10)
                tiles(stage + "_out", KD, FT, lambda k: hid[:, k, 0:n], n,
                      lambda t: stat(r, t - 1, n) if t else None)
                stat(r, KD - 1, n)

            pe.wait_ge(h_ready, 1)
            ffn("ffn1", 1, h1, hid1, 512, True)
            for j in range(KD):
                stat(2, j, 512)
            pe.wait_ge(h_ready, 2)
            tiles("z", 24, KD, lambda k: h1[:, k, 0:T])

            def rotate(n):
                evacuated(pe, "qk", n % 4, n // 4)
                take(pe, "qk", 5 + n % 2, n // 2)
                mm(ps[5 + n % 2][:, 0:T], lhsT=perm, rhs=raw_v[:, n % 2, :], start=True, stop=True)\
                    .then_inc(full[5 + n % 2], 1)
            for n in range(16):
                w_n = T if n < 8 else 512
                take(pe, "qk", n % 4, n // 4)
                product(ps[n % 4][:, 0:w_n], KD, lambda k: h1[:, k, 0:w_n], full[n % 4])
                if n:
                    rotate(n - 1)
            rotate(15)
            pe.wait_ge(u_ready, 8)
            for n in range(4):
                kt, half = n // 2, n % 2
                take(pe, "ut", 5 + half, n // 2)
                for q_ in range(4):
                    ins = nc.tensor.transpose(ps[5 + half][:, q_ * P:q_ * P + P],
                                              u[:, half * 4 + q_, kt * P:kt * P + P], ident)
                ins.then_inc(full[5 + half], 1)
            for s in range(4):
                slot = st.slab % RING
                pe.wait_ge(slab_loaded[slot], 16 * (st.slab // RING + 1))
                for tt in range(4):
                    n = 4 * s + tt
                    take(pe, "v", tt, s)
                    for k in range(KD):
                        ins = mm(ps[tt][:, 0:256], lhsT=h1[:, k, tt * P:tt * P + P], rhs=ring_wide[slot][:, k, :],
                                 start=k == 0, stop=k == KD - 1)
                        if tt == 0 and k == 0:
                            ins.then_inc(slab_started, 1)
                    ins.then_inc(full[tt], 1)
                st.slab += 1
            evacuated(pe, "ut", 5, 1)
            evacuated(pe, "ut", 6, 1)
            for i in range(4):
                j, half = i // 2, i % 2
                for im in range(2):
                    b = 2 * half + im
                    take(pe, "uspec", b, j)
                    for kt in range(2):
                        ins = mm(ps[b][:, :], lhsT=Fu[:, kt, im * T + j * P:im * T + j * P + P],
                                 rhs=utok[:, kt, half * 512:half * 512 + 512], start=kt == 0, stop=kt == 1)
                    ins.then_inc(full[b], 1)
            pe.wait_ge(y_ready, 4)
            for ct in range(KD):
                take(pe, "yinv", ct % 4, ct // 4)
                for f in range(4):
                    ins = mm(ps[ct % 4][:, 0:T], lhsT=Y[:, f, ct * P:ct * P + P], rhs=Finv[:, f, :],
                             start=f == 0, stop=f == 3)
                ins.then_inc(full[ct % 4], 1)
            tiles("gates", 16, KD, lambda k: h1[:, k, 0:T])

            def scores(hd):
                for qb in range(2):
                    for m in range(2):
                        b = 2 * m + qb
                        take(pe, "att", b, hd)
                        mm(ps[b][:, :], lhsT=q_sb[64 * m:64 * m + 64, hd, qb * P:qb * P + P],
                           rhs=kT[64 * m:64 * m + 64, hd, :], start=True, stop=True).then_inc(full[b], 1)
            evacuated(pe, "qk", 5, 7)
            evacuated(pe, "qk", 6, 7)
            for b in range(4):
                evacuated(pe, "v", b, 3)
            scores(0)
            for hd in range(HEADS):
                if hd + 1 < HEADS:
                    scores(hd + 1)
                pe.wait_ge(p_ready, hd + 1)
                for qb in range(2):
                    take(pe, "att", 5 + qb, hd)
                    for kt in range(4):
                        ins = nc.tensor.transpose(ps[5 + qb][:, kt * P:kt * P + P],
                                                  prob[:, 4 * (hd % 2) + qb, kt * P:kt * P + P], ident)
                    ins.then_inc(full[5 + qb], 1)
                evacuated(pe, "att", 5, hd)
                evacuated(pe, "att", 6, hd)
                take(pe, "att", 7, hd)
                for kt in range(4):
                    ins = mm(ps[7][:, 0:T], lhsT=vtok[:, kt, hd * P:hd * P + P], rhs=pT[:, 4 * (hd % 2) + kt, :],
                             start=kt == 0, stop=kt == 3)
                ins.then_inc(full[7], 1)
            pe.wait_ge(osq_ready, 8)
            take(pe, "onorm", 5, 0)
            for j in range(HEADS):
                ins = mm(ps[5][0:HEADS, 0:T], lhsT=headsel[:, j, :], rhs=osq[:, j, :], start=j == 0, stop=j == 7)
            ins.then_inc(full[5], 1)
            pe.wait_ge(hr_ready, 1)
            pe.wait_ge(headbc_in, 16)
            for j in range(HEADS):
                b = j // 2
                if j % 2 == 0:
                    take(pe, "onorm", b, 0)
                ins = mm(ps[b][:, (j % 2) * T:(j % 2) * T + T], lhsT=headbc[:, j, :], rhs=fh[0:HEADS, 0:T],
                         start=True, stop=True)
                if j % 2:
                    ins.then_inc(full[b], 1)
            pe.wait_ge(hy_ready, 1)
            tiles("hyout", KD, KD, lambda k: hy[:, k, :])
            for b in range(4):
                evacuated(pe, "onorm", b, 0)
            tiles("daout", KD, KD, lambda k: oT[:, k, :])
            pe.wait_ge(mix_ready, 1)
            tiles("wo", KD, KD, lambda k: mix[:, k, :], T, lambda t: stat(3, t - 1, T) if t else None)
            stat(3, KD - 1, T)
            for j in range(KD):
                stat(4, j, T)
            pe.wait_ge(h_ready, 3)
            ffn("ffn2", 5, h, hid2, T, False)
            for j in range(KD):
                stat(6, j, T)
            pe.wait_ge(h_ready, 4)

            tiles("shift", 15, KD, lambda k: h[:, k, :])
            pe.wait_ge(masks_in, 48)
            evacuated(pe, "shift", 1, 0)
            for which in range(2):
                if which == 0:
                    pe.wait_ge(act_us, 1)
                for half in range(2):
                    for d in range(2):
                        b = 2 * d + half
                        take(pe, "lora", b, which)
                        for q_ in range(2):
                            j = 2 * half + q_
                            ins = mm(ps[b][:, q_ * T:q_ * T + T],
                                     lhsT=lora[64 * d:64 * d + 64, which * 512 + j * P:which * 512 + j * P + P],
                                     rhs=US[64 * d:64 * d + 64, which, :], start=True, stop=True)
                        ins.then_inc(full[b], 1)
            pe.wait_ge(kksq_ready, 1)
            for i in range(2):
                take(pe, "kkn", 5 + i, 0)
                mm(ps[5 + i][:, :], lhsT=blk, rhs=gsq_kk[:, i * 512:i * 512 + 512], start=True, stop=True)\
                    .then_inc(full[5 + i], 1)
            pe.wait_ge(qq_ready, 1)

            def to_tokens(b, k, src):
                take(pe, "toks", b, k)
                for j in range(4):
                    ins = nc.tensor.transpose(ps[b][:, j * P:j * P + P], src(j), ident)
                ins.then_inc(full[b], 1)
            for ch in range(2):
                to_tokens(5 + ch, 0, lambda j: US[:, US_V + j, ch * P:ch * P + P])
            for d in range(2):
                to_tokens(5, 1 + d, lambda j: KT[:, 8 * d + 2 * j + d, :])
                to_tokens(6, 1 + d, lambda j: BT[:, 8 * d + 2 * j + d, :])

            for s in range(2):
                for d in range(2):
                    ch = d if s == 0 else 1 - d
                    for hd in range(HEADS):
                        j, par = hd // 2, hd % 2
                        b = 2 * (j % 2) + par
                        r0 = 64 * par
                        row = 8 * d + 2 * j + ch
                        qq = QQw[r0:r0 + 64, row, :]
                        take(pe, f"am{s}", b, 2 * d + j // 2)
                        mm(ps[b][:, 0:256], lhsT=BT[r0:r0 + 64, row, :], rhs=qq, start=True, stop=True)
                        mm(ps[b][:, 256:512], lhsT=KT[r0:r0 + 64, row, :], rhs=qq, start=True, stop=True)\
                            .then_inc(full[b], 1)
                for pair in range(2):
                    for lv in range(7):
                        use = pair * 7 + lv
                        for d in range(2):
                            b = 3 * d
                            n = (s * 2 + pair) * 14 + lv * 2 + d
                            pe.wait_ge(nl_ready, n + 1)
                            if lv == 0:
                                pe.wait_ge(x_init, (s * 2 + pair) * 2 + d + 1)
                            else:
                                evacuated(pe, f"inv{s}", (1, 5)[d], use - 1)
                            take(pe, f"inv{s}", b, use)
                            for i in range(4):
                                ins = mm(ps[b][:, i * P:i * P + P], lhsT=NL[:, 4 * d + i, :], rhs=Xw[:, 4 * d + i, :],
                                         start=True, stop=True)
                            ins.then_inc(full[b], 1)
                        for d in range(2):
                            b, bx, bt = 3 * d, (1, 5)[d], (2, 6)[d]
                            u0 = 8 * d + 4 * pair
                            evacuated(pe, f"inv{s}", b, use)
                            if lv:
                                evacuated(pe, f"inv{s}", bt, use - 1)
                            take(pe, f"inv{s}", bx, use)
                            for i in range(4):
                                ins = mm(ps[bx][:, i * P:i * P + P], lhsT=XT[:, u0 + i, :], rhs=Pw[:, 4 * d + i, :],
                                         start=True, stop=True)
                            ins.then_inc(full[bx], 1)
                            take(pe, f"inv{s}", bt, use)
                            for i in range(4):
                                ins = mm(ps[bt][:, i * P:i * P + P], lhsT=Pw[:, 4 * d + i, :], rhs=XT[:, u0 + i, :],
                                         start=True, stop=True)
                            ins.then_inc(full[bt], 1)
                for d in range(2):
                    ch = d if s == 0 else 1 - d
                    if s == 0:
                        evacuated(pe, "toks", 5, 2)
                        evacuated(pe, "toks", 6, 2)
                    else:
                        evacuated(pe, "tail0", 5, d)
                    for par in range(2):
                        take(pe, f"tail{s}", par, d)
                        for j in range(4):
                            hd = 2 * j + par
                            row = 8 * d + 2 * j + ch
                            o = ps[par][:, 64 * j:64 * j + 64]
                            ins = mm(o, lhsT=AM[:, 8 * d + hd, 256:384], rhs=Vtok[:, ch, 64 * hd:64 * hd + 64],
                                     start=True, stop=s == 0)
                            if s:
                                ins = mm(o, lhsT=QQ[64 * par:64 * par + 64, 2 * row, :],
                                         rhs=state_v[64 * par:64 * par + 64, d, j, :], start=False, stop=True)
                        ins.then_inc(full[par], 1)
                    evacuated(pe, f"tail{s}", 0, d)
                    evacuated(pe, f"tail{s}", 1, d)
                    for b in (2, 6):
                        evacuated(pe, f"inv{s}", b, 13)
                    take(pe, f"tail{s}", 2, d)
                    for hd in range(HEADS):
                        ins = mm(ps[2][:, 64 * hd:64 * hd + 64], lhsT=XT[:, 8 * d + hd, :], rhs=Wsb[:, hd, :],
                                 start=True, stop=True)
                    ins.then_inc(full[2], 1)
                    evacuated(pe, f"tail{s}", 2, d)
                    take(pe, f"tail{s}", 3, d)
                    for j in range(4):
                        for par in range(2):
                            hd = 2 * j + par
                            row = 8 * d + 2 * j + ch
                            o = ps[3][64 * par:64 * par + 64, j * P:j * P + P]
                            mm(o, lhsT=Vtok[:, ch, 64 * hd:64 * hd + 64], rhs=AM[:, 8 * d + hd, 384:512],
                               start=True, stop=False)
                            ins = mm(o, lhsT=nU[:, hd, :], rhs=AM[:, 8 * d + hd, 128:256], start=False, stop=s == 0)
                            if s:
                                ins = mm(o, lhsT=state_v[64 * par:64 * par + 64, d, j, :],
                                         rhs=QQ[64 * par:64 * par + 64, 2 * row + 1, :], start=False, stop=True)
                    ins.then_inc(full[3], 1)
                    if s == 0:
                        take(pe, "tail0", 5, d)
                        for j in range(4):
                            for par in range(2):
                                hd = 2 * j + par
                                o = ps[5][64 * par:64 * par + 64, 64 * j:64 * j + 64]
                                mm(o, lhsT=toks[:, 2 * d, 64 * hd:64 * hd + 64],
                                   rhs=Vtok[:, ch, 64 * hd:64 * hd + 64], start=True, stop=False)
                                ins = mm(o, lhsT=toks[:, 2 * d + 1, 64 * hd:64 * hd + 64], rhs=nU[:, hd, :],
                                         start=False, stop=True)
                        ins.then_inc(full[5], 1)
            evacuated(pe, "tail1", 3, 1)
            for i in range(2):
                take(pe, "gn", i, 0)
                mm(ps[i][:, :], lhsT=blk, rhs=page(5.5 + 0.25 * i, 512), start=True, stop=True).then_inc(full[i], 1)
            for i in range(2):
                take(pe, "gn", 5 + i, 0)
                mm(ps[5 + i][:, :], lhsT=blk, rhs=page(8, 15 * 256)[:, (US_K + 2 * i) * T:(US_K + 2 * i + 2) * T], start=True, stop=True)\
                    .then_inc(full[5 + i], 1)
            pe.wait_ge(gsq_ready, 1)
            for i in range(2):
                take(pe, "gn", 2 + i, 0)
                mm(ps[2 + i][:, :], lhsT=blk, rhs=gsq[:, i * 512:i * 512 + 512], start=True, stop=True)\
                    .then_inc(full[2 + i], 1)
            pe.wait_ge(g_ready, 1)
            for i in range(2):
                take(pe, "gn", i, 1)
                for q_ in range(2):
                    j = 2 * i + q_
                    ins = mm(ps[i][:, q_ * T:q_ * T + T], lhsT=g_up[:, j * P:j * P + P],
                             rhs=US[:, US_G, :], start=True, stop=True)
                ins.then_inc(full[i], 1)
            tiles("aq", 5, KD, lambda k: h[:, k, :])
            bl = [st.block() for _ in range(KD)]
            take(pe, "aq", 1, 1)
            for tt in range(2):
                for k in range(KD):
                    ins = mm(ps[1][:, tt * P:tt * P + P], lhsT=h[:, k, tt * P:tt * P + P], rhs=bl[k][0],
                             start=k == 0, stop=k == KD - 1)
                    if tt == 0 and bl[k][1]:
                        ins.then_inc(slab_started, 1)
            ins.then_inc(full[1], 1)

            def band_scores(n):
                j, par = n // 2, n % 2
                b = n % 4
                take(pe, "batt", b, n // 4)
                for qb in range(2):
                    ins = mm(ps[b][:, qb * T:qb * T + T], lhsT=qa[64 * par:64 * par + 64, j, qb * P:qb * P + P],
                             rhs=qa[64 * par:64 * par + 64, 4, :], start=True, stop=True)
                ins.then_inc(full[b], 1)
            for b, k in ((0, 1), (1, 0), (2, 0), (3, 0), (1, 1)):
                evacuated(pe, "aq", b, k)
            band_scores(0)
            for n in range(HEADS):
                j, par = n // 2, n % 2
                if n + 1 < HEADS:
                    band_scores(n + 1)
                pe.wait_ge(p_ready, HEADS + n + 1)
                b = 5 + n % 2
                take(pe, "batt", b, n // 2)
                for qb in range(2):
                    for kt in range(2):
                        ins = nc.tensor.transpose(ps[b][:, kt * T + qb * P:kt * T + qb * P + P],
                                                  bp[:, 2 * (n % 2) + qb, kt * P:kt * P + P], ident)
                ins.then_inc(full[b], 1)
                evacuated(pe, "batt", b, n // 2)
                if par == 0:
                    take(pe, "batt", 7, j)
                for kt in range(2):
                    ins = mm(ps[7][64 * par:64 * par + 64, 0:T], lhsT=va[:, kt, 64 * par:64 * par + 64],
                             rhs=bpT[:, 2 * (n % 2) + kt, :], start=kt == 0, stop=kt == 1)
                if par:
                    ins.then_inc(full[7], 1)
            tiles("gates2", 16, KD, lambda k: h[:, k, :])
            evacuated(pe, "gn", 0, 1)
            evacuated(pe, "gn", 1, 1)
            tiles("projr", KD, 4, lambda k: yr[:, k, :])
            evacuated(pe, "batt", 7, 3)
            tiles("proja", KD, 4, lambda k: oa[:, k, :])
            pe.wait_ge(mix_ready, 2)
            tiles("wout", KD, KD, lambda k: mix2[:, k, :])
            for j in range(KD):
                stat(7, j, T)
            pe.wait_ge(router_in, 16)
            pe.wait_ge(h_ready, 5)
            take(pe, "route", 0, 0)
            for tt in range(2):
                for k in range(KD):
                    ins = mm(ps[0][:, tt * N_EXP:tt * N_EXP + N_EXP], lhsT=h[:, k, tt * P:tt * P + P],
                             rhs=router_v[:, k, :], start=k == 0, stop=k == KD - 1)
            ins.then_inc(full[0], 1)
            for n in range(4):
                tt, half = n // 2, n % 2
                take(pe, "htok", 5 + half, tt)
                for q_ in range(4):
                    ins = nc.tensor.transpose(ps[5 + half][:, q_ * P:q_ * P + P],
                                              h[:, half * 4 + q_, tt * P:tt * P + P], ident)
                ins.then_inc(full[5 + half], 1)
            pe.wait_ge(aexp, 2)
            take(pe, "route", 1, 0)
            for tt in range(2):
                ins = nc.tensor.transpose(ps[1][0:N_EXP, tt * P:tt * P + P], tiny[:, 32 + 16 * tt:48 + 16 * tt], ident)
            ins.then_inc(full[1], 1)
            pe.wait_ge(slot_ready, 1)
            take(pe, "route", 2, 0)
            for tt in range(2):
                ins = nc.tensor.transpose(ps[2][:, tt * N_EXP:tt * N_EXP + N_EXP], fh[0:N_EXP, tt * P:tt * P + P],
                                          ident[0:N_EXP, 0:N_EXP])
            ins.then_inc(full[2], 1)
            pe.wait_ge(oh_ready, 2)
            evacuated(pe, "htok", 5, 1)
            evacuated(pe, "htok", 6, 1)
            for dt in range(KD):
                take(pe, "gather", dt % 4, dt // 4)
                for tt in range(2):
                    ins = mm(ps[dt % 4][:, :], lhsT=htok[:, tt, dt * P:dt * P + P], rhs=OH[:, tt, :],
                             start=tt == 0, stop=tt == 1)
                ins.then_inc(full[dt % 4], 1)
            for tt in range(2):
                take(pe, "oht", 5 + tt, 0)
                for g4 in range(4):
                    ins = nc.tensor.transpose(ps[5 + tt][:, g4 * P:g4 * P + P], OHW[:, tt, g4 * P:g4 * P + P], ident)
                ins.then_inc(full[5 + tt], 1)
            for b in range(4):
                evacuated(pe, "gather", b, 1)
            evacuated(pe, "oht", 5, 0)
            evacuated(pe, "oht", 6, 0)
            ex = Stream(pe, ex_loaded, ex_started, ex_ring, EX_RING)

            def ex_product(out, k_tiles, rhs):
                for k in range(k_tiles):
                    w, first = ex.block()
                    ins = mm(out, lhsT=w, rhs=rhs(k), start=k == 0, stop=k == k_tiles - 1)
                    if first:
                        ins.then_inc(ex_started, 1)
                return ins

            with pe.Fori(0, 4) as i:
                ex.loop(i, 4 * EX_RING)
                for q_ in range(4):
                    xs = [xsT[:, k:k + 1, ds(i * P + q_ * CAP, CAP)] for k in range(KD)]
                    for half in range(2):
                        b = 2 * (q_ % 2) + half
                        take(pe, "moe", b, i * 3 + q_ // 2)
                        for f in range(4):
                            for up in range(2):
                                ins = ex_product(ps[b][:, up * P + f * CAP:up * P + f * CAP + CAP], KD, lambda k: xs[k])
                        ins.then_inc(full[b], 1)
                    evacuated(pe, "moe", 2 * (q_ % 2), i * 3 + q_ // 2)
                    evacuated(pe, "moe", 2 * (q_ % 2) + 1, i * 3 + q_ // 2)
                    b = 5 + q_ % 2
                    take(pe, "moe", b, i * 2 + q_ // 2)
                    for dt in range(KD):
                        ins = ex_product(ps[b][:, dt * CAP:dt * CAP + CAP], KD,
                                         lambda k: hidT[:, q_ % 2, k * CAP:k * CAP + CAP])
                    ins.then_inc(full[b], 1)
                evacuated(pe, "moe", 5, i * 2 + 1)
                evacuated(pe, "moe", 6, i * 2 + 1)
                for half in range(2):
                    take(pe, "moe", 7, i * 2 + half)
                    for d4 in range(4):
                        ins = nc.tensor.transpose(ps[7][:, d4 * P:d4 * P + P], ysT[:, half * 4 + d4, :], ident)
                    ins.then_inc(full[7], 1)
                evacuated(pe, "moe", 7, i * 2 + 1)
                for b in range(4):
                    take(pe, "moe", b, i * 3 + 2)
                    for q_ in range(2):
                        dt = 2 * b + q_
                        ins = mm(ps[b][:, q_ * T:q_ * T + T], lhsT=ys4[:, dt * P:dt * P + P],
                                 rhs=OHT[:, ds(i, 1), :], start=True, stop=True)
                    ins.then_inc(full[b], 1)
            for j in range(KD):
                stat(8, j, T)

        @block.scalar
        def _(act):
            A = nc.scalar.activation
            act.dma_start(filt, dram["filt"]).then_inc(filters_in, 16)
            act.dma_start(zT, dram["zT"]).then_inc(filters_in, 16)
            act.dma_start(w4[0:64, :], dram["w4"]).then_inc(spectra_in, 16)
            act.dma_start(page(13.5, 2048), dram["decay"]).then_inc(spectra_in, 16)
            act.dma_start(page(12, 20 * P), dram["FK"]).then_inc(spectra_in, 16)
            act.dma_start(page(18.5, 1024), dram["Fu"]).then_inc(spectra_in, 16)
            act.dma_start(page(19, 1024), dram["Finv"]).then_inc(spectra_in, 16)
            act.dma_start(page(19.5, 512), dram["rope"]).then_inc(spectra_in, 16)
            act.dma_start(router[:, :], dram["router"]).then_inc(router_in, 16)

            def square(r, j, src, n):
                if j >= 2:
                    act.wait_ge(sq_used, 7 * r + j - 1)
                elif r:
                    act.wait_ge(full[4], r)
                A(sq_v[:, j % 2, 0:n], src, ACT.Square).then_inc(sq_ready, 1)

            def root(r, n):
                act.wait_ge(full[4], r + 1)
                A(sd[:, 0:n], ps[4][:, 0:n], ACT.Sqrt, bias=eps[:, 0:1], scale=1.0 / D).then_inc(evac[4], 1)

            act.wait_ge(consts_in, 48)
            A(cond_s[:, :], cond[:, :], ACT.Silu).then_inc(cond_ready, 1)
            for n in range(3):
                act.wait_ge(arg_ready, n + 1)
                A(fh[:, 0:T], fh[:, T:2 * T], ACT.Sin).then_inc(sin_ready, 1)
            got(act, "lam", 7, 0)
            A(tiny[:, 2:4], ps[7][:, 0:2], ACT.Exp).then_inc(evac[7], 1)
            act.wait_ge(tokens_in, 16)
            for j in range(KD):
                square(0, j, X[:, j, :], 512)
            act.wait_ge(eps_set, 2)
            root(0, 512)
            for n in range(8):
                tt, qq = n % 2, n // 2
                kt, lo = (qq // 2) * 2 + tt, (qq % 2) * 512
                evacuated(act, "w4", n % 4, n // 4)
                A(habs[:, kt, lo:lo + 512], hfil[:, kt, lo:lo + 512], ACT.Abs).then_inc(habs_ready, 1)
            for n in range(10):
                got(act, "kdft", n % 4, n // 4)
                A(Kspec[:, n // 2, (n % 2) * 512:(n % 2) * 512 + 512], ps[n % 4][:, :], ACT.Copy)\
                    .then_inc(evac[n % 4], 1)

            def ffn(stage, r, y, n):
                def gate(q_, use):
                    b = 2 * (q_ % 2)
                    got(act, stage + "_in", b, use)
                    act.wait_ge(evac[b + 1], FILLS[stage + "_in"][b + 1] + use)
                    A(sil_v[:, q_ % 2, 0:n], ps[b][:, 0:n], ACT.Silu).then_inc(evac[b], 1)
                with act.Fori(0, 5) as i:
                    for q_ in range(4):
                        gate(q_, i * 2 + q_ // 2)
                gate(0, 10)
                gate(1, 10)
                leave(stage + "_out", r, y, n)

            def leave(stage, r, y, n):
                for t in range(KD):
                    got(act, stage, t % 4, t // 4)
                    A(y[:, t, 0:n], ps[t % 4][:, 0:n], ACT.Copy).then_inc(evac[t % 4], 1)
                    evacuated(act, stage, t % 4, t // 4)
                    square(r, t, y[:, t, 0:n], n)
                root(r, n)

            ffn("ffn1", 1, y1, 512)
            for j in range(KD):
                act.wait_ge(x_ready, 1 + j // 4)
                square(2, j, X[:, j, :], 512)
            root(2, 512)
            for n in range(24):
                got(act, "z", n % 4, n // 4)
                A((x0, u, zv)[n // 8][:, n % 8, :], ps[n % 4][:, 0:T], ACT.Identity, bias=c("cb", n),
                  scale=c("cw1", n)).then_inc(z_scaled, 1)
            for n in range(16):
                got(act, "qk", n % 4, n // 4)
                if n >= 2:
                    evacuated(act, "qk", 5 + n % 2, n // 2 - 1)
                if n >= 8:
                    A(kT[:, n - 8, T:2 * T], ps[n % 4][:, T:2 * T], ACT.Copy)
                A(raw_v[:, n % 2, :], ps[n % 4][:, 0:T], ACT.Copy).then_inc(evac[n % 4], 1)
            for n in range(16):
                s, tt = n // 4, n % 4
                got(act, "v", tt, s)
                A(vtok[:, tt, s * 256:s * 256 + 256], ps[tt][:, 0:256], ACT.Copy).then_inc(evac[tt], 1)
            act.wait_ge(y_ready, 4)
            act.dma_start(page(18.5, HEADS * P)[0:HEADS], dram["headbc"]).then_inc(headbc_in, 16)
            act.wait_ge(kn_ready, 1)
            for ct in range(KD):
                got(act, "yinv", ct % 4, ct // 4)
                A(yc[:, ct, :], ps[ct % 4][:, 0:T], ACT.Copy, scale=tiny[:, 8 + ct:9 + ct]).then_inc(evac[ct % 4], 1)
            for n in range(16):
                got(act, "gates", n % 4, n // 4)
                A(gates[:, n, :], ps[n % 4][:, 0:T], ACT.Sigmoid).then_inc(evac[n % 4], 1)

            def exps(hd):
                act.wait_ge(nm_ready, hd + 1)
                o = 4 * (hd % 2)
                for b in range(4):
                    A(prob[:, o + b, :], ps[b][:, :], ACT.Exp, bias=tiny[:, 16 + o + b:17 + o + b],
                      scale=0.125, accum_out=tiny[:, 24 + o + b:25 + o + b]).then_inc(evac[b], 1)
            exps(0)
            for hd in range(HEADS):
                if hd + 1 < HEADS:
                    exps(hd + 1)
                got(act, "att", 5, hd)
                A(pT[:, 4 * (hd % 2):4 * (hd % 2) + 4, 0:P], ps[5][:, :].rearrange("p (k n) -> p k n", n=P), ACT.Copy)\
                    .then_inc(evac[5], 1)
                got(act, "att", 7, hd)
                A(oT[:, hd, :], ps[7][:, 0:T], ACT.Copy).then_inc(evac[7], 1)
                evacuated(act, "att", 7, hd)
                A(osq[:, hd, :], oT[:, hd, :], ACT.Square).then_inc(osq_ready, 1)
            got(act, "onorm", 5, 0)
            A(fh[0:HEADS, T:2 * T], ps[5][0:HEADS, 0:T], ACT.Sqrt, bias=eps[0:HEADS, 0:1], scale=1.0 / P)\
                .then_inc(evac[5], 1)
            leave("wo", 3, y2, T)
            act.wait_ge(mix_ready, 1)
            act.dma_start(masks, dram["masks"]).then_inc(masks_in, 16)
            act.dma_start(lora, dram["lora"][:, 0:1024]).then_inc(masks_in, 16)
            act.dma_start(g_up, dram["lora"][:, 1024:1536]).then_inc(masks_in, 16)
            for j in range(KD):
                act.wait_ge(x_ready, 3 + j // 4)
                square(4, j, x[:, j, :], T)
            root(4, T)
            ffn("ffn2", 5, y3, T)
            for j in range(KD):
                act.wait_ge(x_ready, 5 + j // 4)
                square(6, j, x[:, j, :], T)
            root(6, T)

            act.wait_ge(mu_ready, 1)
            for t in range(15):
                got(act, "shift", t % 4, t // 4)
                A(US[:, t, :], ps[t % 4][:, 0:T], ACT.Copy, scale=rt[:, 256 + t:257 + t]).then_inc(us_scaled, 1)
            evacuated(act, "shift", 0, 0)
            A(US[:, 0, :], US[:, 0, :], ACT.Tanh).then_inc(act_us, 1)
            evacuated(act, "shift", 14 % 4, 14 // 4)
            A(US[:, US_G, :], US[:, US_G, :], ACT.Sigmoid).then_inc(g_ready, 1)
            for which in range(2):
                dst = (sig256, iclr)[which]
                for half in range(2):
                    for d in range(2):
                        b = 2 * d + half
                        got(act, "lora", b, which)
                        for q_ in range(2):
                            j = 4 * d + 2 * half + q_
                            ins = A(dst[:, j, :], ps[b][:, q_ * T:q_ * T + T], ACT.Sigmoid,
                                    bias=c(("w0", "a0")[which], j))
                        ins.then_inc(evac[b], 1)
            act.wait_ge(kkr_ready, 1)
            A(gsq_kk, kkr_flat, ACT.Square).then_inc(kksq_ready, 1)
            act.wait_ge(ss_ready, 1)
            A(nrm, nrm, ACT.Sqrt).then_inc(nrm_ready, 1)
            for d in range(2):
                act.wait_ge(logs_ready, d + 1)
                o = slice(8 * d, 8 * d + 8)
                inc = (D1, D2)[d]
                A(Einc[:, o, :], inc[:, o, :], ACT.Exp, scale=-DECAY_SCALE)
                A(Eneg[:, o, :], inc[:, o, :], ACT.Exp, scale=DECAY_SCALE)
                A(Eexc[:, o, :], (D2, D1)[d][:, o, :], ACT.Exp, scale=(-DECAY_SCALE, DECAY_SCALE)[d])
                A(scl[:, 4 * d:4 * d + 4], scl[:, 4 * d:4 * d + 4], ACT.Exp, scale=-DECAY_SCALE).then_inc(exps_ready, 1)
            for k in range(3):
                for b in (5, 6):
                    got(act, "toks", b, k)
                    dst = Vtok[:, b - 5, :] if k == 0 else toks[:, 2 * (k - 1) + b - 5, :]
                    A(dst, ps[b][:, :], ACT.Copy).then_inc(evac[b], 1)
            for s in range(2):
                for use in range(14):
                    for d in range(2):
                        got(act, f"inv{s}", 3 * d, use)
                        A(Pw[:, 4 * d:4 * d + 4, :], ps[3 * d][:, :].rearrange("p (i n) -> p i n", n=P), ACT.Copy)\
                            .then_inc(evac[3 * d], 1)
                for d in range(2):
                    for par in range(2):
                        got(act, f"tail{s}", par, d)
                        A(Wsb.rearrange("p (j r) n -> p j r n", r=2)[:, :, par, :],
                          ps[par][:, 0:256].rearrange("p (j n) -> p j n", n=64), ACT.Copy).then_inc(evac[par], 1)
                    got(act, f"tail{s}", 2, d)
                    A(nU, ps[2][:, :].rearrange("p (h n) -> p h n", n=64), ACT.Copy, scale=-1.0).then_inc(evac[2], 1)
            for i in range(2):
                evacuated(act, "gn", i, 0)
            A(gsq, dev, ACT.Square).then_inc(gsq_ready, 1)
            for i in range(2):
                got(act, "gn", 2 + i, 0)
                A(gsd[:, i * 512:i * 512 + 512], ps[2 + i][:, :], ACT.Sqrt, bias=eps[:, 1:2], scale=1.0 / 64)\
                    .then_inc(evac[2 + i], 1)
            for t in range(5):
                got(act, "aq", t % 4, t // 4)
                A(qa[:, t, :], ps[t % 4][:, 0:T], ACT.Copy, scale=0.125 if t < 4 else 1.0).then_inc(evac[t % 4], 1)
            got(act, "aq", 1, 1)
            A(va, ps[1][:, 0:T].rearrange("p (k n) -> p k n", n=P), ACT.Copy).then_inc(evac[1], 1)

            def band_exps(n):
                act.wait_ge(nm_ready, HEADS + n + 1)
                o, head = 2 * (n % 2), n // 2 + 4 * (n % 2)
                for qb in range(2):
                    A(bp[:, o + qb, :], bs[:, o + qb, :], ACT.Exp, bias=tiny[:, 16 + o + qb:17 + o + qb],
                      accum_out=tiny[:, 20 + o + qb:21 + o + qb])
                A(tiny[:, 24 + o:26 + o], tiny[:, 16 + o:18 + o], ACT.Exp, bias=c("sink", head)).then_inc(es_ready, 1)
            band_exps(0)
            for n in range(HEADS):
                if n + 1 < HEADS:
                    band_exps(n + 1)
                b = 5 + n % 2
                got(act, "batt", b, n // 2)
                A(bpT[:, 2 * (n % 2):2 * (n % 2) + 2, :], ps[b][:, :].rearrange("p (k n) -> p k n", n=T), ACT.Copy)\
                    .then_inc(evac[b], 1)
                if n % 2:
                    got(act, "batt", 7, n // 2)
                    A(oa[:, n // 2, :], ps[7][:, 0:T], ACT.Copy).then_inc(evac[7], 1)
            for n in range(16):
                got(act, "gates2", n % 4, n // 4)
                A(gates2[:, n, :], ps[n % 4][:, 0:T], ACT.Sigmoid).then_inc(evac[n % 4], 1)
            for j in range(KD):
                evacuated(act, "wout", j % 4, j // 4)
                square(7, j, x[:, j, :], T)
            root(7, T)
            act.wait_ge(nm_ready, 2 * HEADS + 1)
            for tt in range(2):
                ins = A(tiny[:, 32 + 16 * tt:48 + 16 * tt], ps[0][:, 16 * tt:16 * tt + 16], ACT.Exp,
                        bias=tiny[:, 16 + tt:17 + tt], accum_out=tiny[:, 20 + tt:21 + tt])
            ins.then_inc(evac[0], 1)
            for n in range(4):
                tt, half = n // 2, n % 2
                got(act, "htok", 5 + half, tt)
                A(htok[:, tt, half * 512:half * 512 + 512], ps[5 + half][:, :], ACT.Copy).then_inc(evac[5 + half], 1)
            for dt in range(KD):
                got(act, "gather", dt % 4, dt // 4)
                A(xsT[:, dt, :], ps[dt % 4][:, :], ACT.Copy).then_inc(evac[dt % 4], 1)
            with act.Fori(0, 4) as i:
                for q_ in range(4):
                    for half in range(2):
                        b = 2 * (q_ % 2) + half
                        got(act, "moe", b, i * 3 + q_ // 2)
                        A(msil[:, b, :], ps[b][:, 0:P], ACT.Silu).then_inc(hid_silu, 1)
                    b = 5 + q_ % 2
                    got(act, "moe", b, i * 2 + q_ // 2)
                    A(ysT[:, :, q_ * CAP:q_ * CAP + CAP], ps[b][:, 0:256].rearrange("p (j n) -> p j n", n=CAP), ACT.Copy)\
                        .then_inc(evac[b], 1)
                for half in range(2):
                    got(act, "moe", 7, i * 2 + half)
                    A(ys4[:, half * 512:half * 512 + 512], ps[7][:, :], ACT.Copy).then_inc(evac[7], 1)
            for j in range(KD):
                evacuated(act, "moe", j // 2, 11)
                square(8, j, x[:, j, :], T)
            root(8, T)

        @block.vector
        def _(dve):
            V = nc.vector
            tt_, ts_, stt = V.tensor_tensor, V.tensor_scalar, V.scalar_tensor_tensor
            steps = Steps(dve, dve_step)
            do, settle = steps.do, steps.settle

            def inverse_root(r, n):
                dve.wait_ge(evac[4], r + 1)
                do(V.reciprocal(rstd[:, 0:n], sd[:, 0:n]))

            def normalise(src, dst, parts):
                settle()
                for j in range(KD):
                    for lo, hi, gn_, shift in parts:
                        ins = stt(dst[:, j, lo:hi], src[:, j, lo:hi], gn_[:, j:j + 1], rstd[:, lo:hi], mult, mult)
                        if shift is not None or j < KD - 1:
                            do(ins)
                if parts[0][3] is not None:
                    settle()
                    for j in range(KD):
                        for lo, hi, gn_, shift in parts:
                            ins = ts_(dst[:, j, lo:hi], dst[:, j, lo:hi], shift[:, j:j + 1], None, add)
                ins.then_inc(h_ready, 1)

            def residual(y, parts, src, dst, n):
                settle()
                for half in range(2):
                    js = slice(4 * half, 4 * half + 4)
                    for j in range(4 * half, 4 * half + 4):
                        for lo, hi, gn_ in parts:
                            do(stt(y[:, j, lo:hi], y[:, j, lo:hi], gn_[:, j:j + 1], rstd[:, lo:hi], mult, mult))
                    settle()
                    tt_(dst[:, js, 0:n], src[:, js, 0:n], y[:, js, 0:n], add).then_inc(x_ready, 1)

            TWO_PI_HI, TWO_PI_LO = 6.28125, 2 * math.pi - 6.28125
            ROUND = 1.5 * 2.0 ** 23
            PI = 3.1415925
            dve.wait_ge(consts_in, 48)
            for n in range(3):
                got(dve, "mlp", 5, n)
                a, k1, k2 = fh[:, T:2 * T], fh[:, 2 * T:3 * T], fh[:, 3 * T:4 * T]
                ts_(a, ps[5][0:64, 0:T], c("fb", n)[0:64], c("ffreq")[0:64], add, mult).then_inc(evac[5], 1)
                evacuated(dve, "mlp", 5, n)
                do(ts_(k1, a, 1.0 / (2 * math.pi), ROUND, mult, add))
                settle()
                do(ts_(k1, k1, ROUND, None, sub))
                settle()
                do(stt(a, k1, -TWO_PI_HI, a, mult, add))
                settle()
                do(stt(a, k1, -TWO_PI_LO, a, mult, add))
                settle()
                ts_(a, a, PI, -PI, mn_op, mx_op).then_inc(arg_ready, 1)
            tt_(tiny[0:64, 0:2], c("lam", 0, 2)[0:64], c("lam", 2, 2)[0:64], mult).then_inc(prod_ready, 1)
            evacuated(dve, "lam", 7, 0)
            do(stt(tiny[:, 4:5], tiny[:, 3:4], LAM_INIT, tiny[:, 2:3], sub, sub))
            inverse_root(0, 512)
            dve.wait_ge(spectra_in, 96)
            for n in range(8):
                tt, qq = n % 2, n // 2
                kt, lo = (qq // 2) * 2 + tt, (qq % 2) * 512
                got(dve, "w4", n % 4, n // 4)
                tt_(hfil[:, kt, lo:lo + 512], ps[n % 4][:, :], decay[:, tt, lo:lo + 512], mult).then_inc(evac[n % 4], 1)

            def ada(stage, b, k, m):
                got(dve, stage, b, k)
                tt_(mods_v[:, m, :, :], ps[b][:, 0:2 * KD].rearrange("p (m j r) -> p m j r", m=1, r=2),
                    b_ada[:, m, :].unsqueeze(3).to_broadcast([P, 1, KD, 2]), add).then_inc(evac[b], 1)
            ada("ada_head", 6, 0, slice(0, 1))
            ada("ada_head", 7, 0, slice(1, 2))
            evacuated(dve, "ada_head", 7, 0)
            for r in range(2):
                do(stt(gain_v[:, r, :], mod(1, r), 1.0, g(0), add, mult))
            normalise(X, h1, [(0, T, gain_v[:, 0, :], mod(0, 0)), (T, 2 * T, gain_v[:, 1, :], mod(0, 1))])
            got(dve, "knorm", 5, 0)
            ts_(tiny[:, 8:16], ps[5][:, 0:KD], EPS, None, add).then_inc(evac[5], 1)
            evacuated(dve, "knorm", 5, 0)
            V.reciprocal(tiny[:, 8:16], tiny[:, 8:16]).then_inc(kn_ready, 1)

            def ffn_in(stage, hid, n, with_ada):
                def up(q_, use, at):
                    b = 2 * (q_ % 2)
                    dve.wait_ge(evac[b], FILLS[stage + "_in"][b] + use + 1)
                    got(dve, stage + "_in", b + 1, use)
                    tt_(hid[:, at, 0:n], sil_v[:, q_ % 2:q_ % 2 + 1, 0:n], ps[b + 1][:, 0:n].unsqueeze(1), mult)\
                        .then_inc(evac[b + 1], 1)
                with dve.Fori(0, 5) as i:
                    if with_ada:
                        ada(stage + "_in", 7, i, ds(i + 2, 1))
                    for q_ in range(4):
                        up(q_, i * 2 + q_ // 2, ds(i * 4 + q_, 1))
                if with_ada:
                    ada(stage + "_in", 7, 5, slice(7, 8))
                    ada(stage + "_in", 6, 0, slice(8, 9))
                up(0, 10, slice(20, 21))
                up(1, 10, slice(21, 22))

            ffn_in("ffn1", hid1, 512, True)
            evacuated(dve, "ffn1_in", 7, 5)
            evacuated(dve, "ffn1_in", 6, 0)
            for r in range(2):
                do(stt(gain_v[:, 2 + r, :], mod(2, r), 0.5, g(1), mult, mult))
                do(stt(gain_v[:, r, :], mod(4, r), 1.0, g(2), add, mult))
            inverse_root(1, 512)
            residual(y1, [(0, T, gain_v[:, 2, :]), (T, 2 * T, gain_v[:, 3, :])], X, X, 512)
            inverse_root(2, 512)
            normalise(X, h1, [(0, T, gain_v[:, 0, :], mod(3, 0)), (T, 2 * T, gain_v[:, 1, :], mod(3, 1))])
            for n in range(24):
                b, dst = n % 4, (x0, u, zv)[n // 8][:, n % 8, :]
                dve.wait_ge(z_scaled, n + 1)
                do(stt(dst[:, 1:T], ps[b][:, 0:T - 1], c("cw0", n), dst[:, 1:T], mult, add))
                settle()
                stt(dst[:, 0:T - 1], ps[b][:, 1:T], c("cw2", n), dst[:, 0:T - 1], mult, add).then_inc(evac[b], 1)
                if n >= 16:
                    evacuated(dve, "z", b, n // 4)
                    tt_(u[:, n - 16, :], u[:, n - 16, :], dst, mult).then_inc(u_ready, 1)
            for n in range(16):
                b = 5 + n % 2
                dst = q_sb[:, n, :] if n < 8 else kT[:, n - 8, 0:T]
                got(dve, "qk", b, n // 2)
                if n >= 2:
                    evacuated(dve, "qk", b, n // 2 - 1)
                r = rt[:, (n % 2) * T:(n % 2) * T + T]
                do(tt_(r, ps[b][:, 0:T], rope[:, 1, :], mult))
                do(tt_(dst, raw_v[:, n % 2, :], rope[:, 0, :], mult))
                settle()
                tt_(dst, dst, r, add).then_inc(evac[b], 1)
            for n in range(4):
                kt, half = n // 2, n % 2
                got(dve, "ut", 5 + half, kt)
                V.tensor_copy(utok[:, kt, half * 512:half * 512 + 512], ps[5 + half][:, :]).then_inc(evac[5 + half], 1)
            for i in range(4):
                j, half = i // 2, i % 2
                o = slice(half * 512, half * 512 + 512)
                br, bi = 2 * half, 2 * half + 1
                k_alt = Kspec[:, 4, o] if j == 0 else Kspec[:, 1, o]
                if i:
                    settle()
                    dve.wait_ge(y_ready, i)
                got(dve, "uspec", br, j)
                do(tt_(Y[:, j, o], ps[br][:, :], Kspec[:, j, o], mult))
                tt_(Y[:, 2 + j, o], ps[br][:, :], Kspec[:, 2 + j, o], mult).then_inc(evac[br], 1)
                got(dve, "uspec", bi, j)
                do(tt_(rt, ps[bi][:, :], Kspec[:, 2 + j, o], mult))
                tt_(raw, ps[bi][:, :], k_alt, mult).then_inc(evac[bi], 1)
                settle()
                do(tt_(Y[:, j, o], Y[:, j, o], rt, sub))
                evacuated(dve, "uspec", bi, j)
                evacuated(dve, "uspec", br, j)
                tt_(Y[:, 2 + j, o], Y[:, 2 + j, o], raw, add).then_inc(y_ready, 1)
            for ct in range(KD):
                evacuated(dve, "yinv", ct % 4, ct // 4)
                do(stt(yc[:, ct, :], u[:, ct, :], c("hyb", ct), yc[:, ct, :], mult, add))
            settle()
            tt_(hy, yc, x0, mult).then_inc(hy_ready, 1)

            def maxima(hd):
                o = 4 * (hd % 2)
                for b in range(4):
                    got(dve, "att", b, hd)
                    do(V.tensor_reduce(tiny[:, 16 + o + b:17 + o + b], ps[b][:, :], AXX, mx_op))
                settle()
                ts_(tiny[:, 16 + o:20 + o], tiny[:, 16 + o:20 + o], -0.125, None, mult).then_inc(nm_ready, 1)
            maxima(0)
            for hd in range(HEADS):
                o = 4 * (hd % 2)
                for b in range(4):
                    evacuated(dve, "att", b, hd)
                do(V.reciprocal(tiny[:, 24 + o:28 + o], tiny[:, 24 + o:28 + o]))
                settle()
                do(ts_(tiny[:, 26 + o:28 + o], tiny[:, 26 + o:28 + o], tiny[:, 4:5], None, mult))
                for qb in range(2):
                    do(ts_(prob[:, o + qb, :], prob[:, o + qb, :], tiny[:, 24 + o + qb:25 + o + qb], None, mult))
                settle()
                for qb in range(2):
                    ins = stt(prob[:, o + qb, :], prob[:, o + 2 + qb, :], tiny[:, 26 + o + qb:27 + o + qb],
                              prob[:, o + qb, :], mult, add)
                ins.then_inc(p_ready, 1)
                if hd + 1 < HEADS:
                    maxima(hd + 1)
                got(dve, "att", 6, hd)
                V.tensor_copy(pT[:, o:o + 4, P:2 * P], ps[6][:, :].rearrange("p (k n) -> p k n", n=P))\
                    .then_inc(evac[6], 1)
            do(ts_(tiny[:, 5:6], c("subg"), 1.0 - LAM_INIT, None, mult))
            evacuated(dve, "onorm", 5, 0)
            V.reciprocal(fh[0:HEADS, 0:T], fh[0:HEADS, T:2 * T]).then_inc(hr_ready, 1)
            settle()
            for j in range(HEADS):
                got(dve, "onorm", j // 2, 0)
                ins = stt(oT[:, j, :], oT[:, j, :], tiny[:, 5:6], ps[j // 2][:, (j % 2) * T:(j % 2) * T + T], mult, mult)
                if j % 2:
                    ins.then_inc(evac[j // 2], 1)
            for t in range(KD):
                got(dve, "hyout", t % 4, t // 4)
                tt_(mix[:, t, :], ps[t % 4][:, 0:T], gates[:, t, :], mult).then_inc(evac[t % 4], 1)

            def gated_add(stage, dst, gts):
                for t in range(KD):
                    got(dve, stage, t % 4, t // 4)
                    settle()
                    tt_(rt[:, 0:T], ps[t % 4][:, 0:T], gts[:, KD + t, :], mult).then_inc(evac[t % 4], 1)
                    evacuated(dve, stage, t % 4, t // 4)
                    ins = tt_(dst[:, t, :], dst[:, t, :], rt[:, 0:T], add)
                    if t < KD - 1:
                        do(ins)
                ins.then_inc(mix_ready, 1)
            for b in range(4):
                evacuated(dve, "hyout", b, 1)
            gated_add("daout", mix, gates)
            do(tt_(gain_v[:, 2, :], mod(5, 0), g(3), mult))
            do(stt(gain_v[:, 0, :], mod(7, 0), 1.0, g(4), add, mult))
            inverse_root(3, T)
            residual(y2, [(0, T, gain_v[:, 2, :])], X, x, T)
            inverse_root(4, T)
            normalise(x, h, [(0, T, gain_v[:, 0, :], mod(6, 0))])
            ffn_in("ffn2", hid2, T, False)
            do(stt(gain_v[:, 2, :], mod(8, 0), 0.5, g(5), mult, mult))
            inverse_root(5, T)
            residual(y3, [(0, T, gain_v[:, 2, :])], x, x, T)
            do(tt_(rt[:, 256:271], c("mup", 0, 15), c("mun", 0, 15), add))
            settle()
            ts_(rt[:, 256:271], rt[:, 256:271], -1.0, 1.0, mult, add).then_inc(mu_ready, 1)
            inverse_root(6, T)
            normalise(x, h, [(0, T, c("nmix", 0, 8), None)])

            for t in range(15):
                b, dst = t % 4, US[:, t, :]
                dve.wait_ge(us_scaled, t + 1)
                do(stt(dst[:, 1:T], ps[b][:, 0:T - 1], c("mup", t), dst[:, 1:T], mult, add))
                settle()
                stt(dst[:, 0:T - 1], ps[b][:, 1:T], c("mun", t), dst[:, 0:T - 1], mult, add).then_inc(evac[b], 1)
            for b in range(4):
                dve.wait_ge(evac[b], FILLS["lora"][b])
            for j in range(3):
                do(ts_(kkr[:, j, :], US[:, US_K + j, :], c("kk", j), None, mult))
            ts_(kkr[:, 3, :], US[:, US_K + 3, :], c("kk", 3), None, mult).then_inc(kkr_ready, 1)
            for d in range(2):
                for half in range(2):
                    evacuated(dve, "lora", 2 * d + half, 0)
                for row in range(8 * d, 8 * d + 8):
                    do(V.tensor_tensor_scan(cum[:, row, :], ones, sig[:, row, :], 0.0, mult, add))
                settle()
                o = slice(8 * d, 8 * d + 8)
                do(tt_(D1[:, o, :], cum[:, o, :], cum[:, o, 63:64].to_broadcast([P, 8, P]), sub))
                cv = cum[:, o, :].rearrange("p (j c) n -> p j c n", c=2)
                sv = scl[:, 4 * d:4 * d + 4]
                do(tt_(sv, cv[:, :, 0, 127], cv[:, :, 0, 63], sub))
                settle()
                do(tt_(sv, sv, cv[:, :, 1, 63], add))
                if d == 0:
                    ins = tt_(D2[:, o, :], D1[:, o, :], sig[:, o, :], sub)
                else:
                    ins = tt_(D2[:, o, :], sig[:, o, :], D1[:, o, :], sub)
                ins.then_inc(logs_ready, 1)
            for i in range(2):
                got(dve, "kkn", 5 + i, 0)
                ts_(nrm[:, i * 512:i * 512 + 512], ps[5 + i][:, :], 1e-24, None, mx_op).then_inc(evac[5 + i], 1)
            evacuated(dve, "kkn", 5, 0)
            evacuated(dve, "kkn", 6, 0)
            V.tensor_copy(tiny[:, 0:1], nrm[:, 0:1]).then_inc(ss_ready, 1)
            do(ts_(tiny[:, 28:32], c("ka", 0, 4), -1.0, 1.0, mult, add))
            for b in range(4):
                evacuated(dve, "lora", b, 1)
            settle()
            kd256 = page(4, 2048, 256)
            for d in range(2):
                for j in range(4):
                    do(ts_(kd256[:, 4 * d + j, :], iclr[:, 4 * d + j, :], c("ka", j), tiny[:, 28 + j:29 + j], mult, add))
            settle()
            for d in range(2):
                do(tt_(kd256[:, 4 * d:4 * d + 4, :], kd256[:, 4 * d:4 * d + 4, :], US[:, US_K:US_K + 4, :], mult))
            settle()
            do(tt_(rkk, kd256[:, 0:4, :], kd256[:, 4:8, :], add))
            settle()
            for j in range(4):
                do(stt(US[:, US_K + j, :], US[:, US_K + j, :], c("rk", j), US[:, US_R + j, :], mult, mult))
            dve.wait_ge(nrm_ready, 1)
            do(V.reciprocal(nrm, nrm))
            settle()
            do(tt_(kkn256, kkr, nrm.rearrange("p (j n) -> p j n", n=T), mult))
            settle()
            r_rows = page(8, 15 * 256, P)[:, 2 * US_R:2 * US_R + 8, :]
            QQv = QQ.rearrange("p (a w) n -> p a w n", w=2)
            for d in range(2):
                dve.wait_ge(exps_ready, d + 1)
            for d in range(2):
                o = slice(8 * d, 8 * d + 8)
                do(tt_(BT[:, o, :], kkn, iclr128[:, o, :], mult))
                do(tt_(KT[:, o, :], kdir[:, o, :], Eneg[:, o, :], mult))
                do(tt_(QQv[:, o, 0, :], kkn, Eexc[:, o, :], mult))
                do(tt_(QQv[:, o, 1, :], r_rows, Einc[:, o, :], mult))
            settle()
            tt_(BT, BT, Eneg, mult).then_inc(qq_ready, 1)
            dve.wait_ge(am_zero, 1)
            dve.wait_ge(masks_in, 48)
            keep_bits = keep.bitcast(mybir.dt.uint32)
            for s in range(2):
                for d in range(2):
                    for hd in range(HEADS):
                        j, par = hd // 2, hd % 2
                        b = 2 * (j % 2) + par
                        got(dve, f"am{s}", b, 2 * d + j // 2)
                        V.copy_predicated(AM[:, 8 * d + hd, :], keep_bits[:, d, :], ps[b][:, :]).then_inc(evac[b], 1)
                for pair in range(2):
                    for d in range(2):
                        u0 = 8 * d + 4 * pair
                        eye4 = ident.unsqueeze(1).to_broadcast([P, 4, P])
                        if s:
                            got(dve, "tail0", 2, d)
                        if s or pair:
                            for b in ((1, 2), (5, 6))[d]:
                                evacuated(dve, f"inv{s if pair else 0}", b, 6 if pair else 13)
                        do(V.tensor_copy(Xw[:, 4 * d:4 * d + 4, :], eye4))
                        V.tensor_copy(XT[:, u0:u0 + 4, :], eye4).then_inc(x_init, 1)
                    for lv in range(7):
                        use = pair * 7 + lv
                        for d in range(2):
                            bx, bt = (1, 5)[d], (2, 6)[d]
                            u0 = 8 * d + 4 * pair
                            if lv == 0:
                                dve.wait_ge(x_init, (s * 2 + pair) * 2 + d + 1)
                            else:
                                evacuated(dve, f"inv{s}", bx, use - 1)
                                evacuated(dve, f"inv{s}", bt, use - 1)
                            for dst, b in ((Xw[:, 4 * d:4 * d + 4, :], bx), (XT[:, u0:u0 + 4, :], bt)):
                                got(dve, f"inv{s}", b, use)
                                tt_(dst, dst, ps[b][:, :].rearrange("p (i n) -> p i n", n=P), sub).then_inc(evac[b], 1)
                for d in range(2):
                    ch = d if s == 0 else 1 - d
                    w_c = wkv[:, :, ch * P:ch * P + P]
                    y_ps = ps[3][:, :].rearrange("p (j n) -> p j n", n=P)
                    got(dve, f"tail{s}", 3, d)
                    if s == 0:
                        V.tensor_copy(w_c, y_ps).then_inc(evac[3], 1)
                        got(dve, "tail0", 5, d)
                        tt_(state_v[:, d, :, :], ps[5][:, 0:256].rearrange("p (j n) -> p j n", n=64),
                            scl[:, 4 * d:4 * d + 4].unsqueeze(2).to_broadcast([P, 4, 64]), mult).then_inc(evac[5], 1)
                    else:
                        evacuated(dve, "tail0", 3, 1)
                        tt_(w_c, w_c, y_ps, add).then_inc(evac[3], 1)
            wkv_flat = page(5.5, 1024)
            evacuated(dve, "tail1", 3, 1)
            for i in range(2):
                o = slice(i * 512, i * 512 + 512)
                got(dve, "gn", i, 0)
                stt(dev[:, o], ps[i][:, :], -1.0 / 64, wkv_flat[:, o], mult, add).then_inc(evac[i], 1)
            US_flat = page(8, 15 * 256)
            bonus = page(21, 1024)
            for i in range(2):
                got(dve, "gn", 5 + i, 0)
                tt_(bonus[:, i * 512:i * 512 + 512], ps[5 + i][:, :],
                    US_flat[:, US_V * T + i * 512:US_V * T + i * 512 + 512], mult).then_inc(evac[5 + i], 1)
            for i in range(2):
                evacuated(dve, "gn", 2 + i, 0)
            do(V.reciprocal(grs, gsd))
            settle()
            do(tt_(dev, dev, grs, mult))
            settle()
            for j in range(4):
                do(ts_(dev[:, j * T:j * T + T], dev[:, j * T:j * T + T], c("lnw", j), c("lnb", j), mult, add))
            evacuated(dve, "gn", 5, 0)
            evacuated(dve, "gn", 6, 0)
            settle()
            do(tt_(dev, dev, bonus, add))
            settle()
            for i in range(2):
                o = slice(i * 512, i * 512 + 512)
                got(dve, "gn", i, 1)
                tt_(page(4, 1024)[:, o], dev[:, o], ps[i][:, :], mult).then_inc(evac[i], 1)

            def band_maxima(n):
                b, o, head = n % 4, 2 * (n % 2), n // 2 + 4 * (n % 2)
                got(dve, "batt", b, n // 4)
                stt(bs[:, o:o + 2, :], dist, 2.0 ** -(head + 1), ps[b][:, :].rearrange("p (q n) -> p q n", n=T), mult, add)\
                    .then_inc(evac[b], 1)
                evacuated(dve, "batt", b, n // 4)
                do(V.tensor_reduce(tiny[:, 16 + o:18 + o], bs[:, o:o + 2, :], AXX, mx_op))
                settle()
                ts_(tiny[:, 16 + o:18 + o], tiny[:, 16 + o:18 + o], c("sink", head), -1.0, mx_op, mult)\
                    .then_inc(nm_ready, 1)
            band_maxima(0)
            for n in range(HEADS):
                o = 2 * (n % 2)
                dve.wait_ge(es_ready, n + 1)
                do(tt_(tiny[:, 20 + o:22 + o], tiny[:, 20 + o:22 + o], tiny[:, 24 + o:26 + o], add))
                settle()
                do(V.reciprocal(tiny[:, 20 + o:22 + o], tiny[:, 20 + o:22 + o]))
                settle()
                for qb in range(2):
                    ins = ts_(bp[:, o + qb, :], bp[:, o + qb, :], tiny[:, 20 + o + qb:21 + o + qb], None, mult)
                ins.then_inc(p_ready, 1)
                if n + 1 < HEADS:
                    band_maxima(n + 1)
            for t in range(KD):
                got(dve, "projr", t % 4, t // 4)
                for hh in range(2):
                    evacuated(dve, "gates2", t % 4, t // 4 + 2 * hh)
                tt_(mix2[:, t, :], ps[t % 4][:, 0:T], gates2[:, t, :], mult).then_inc(evac[t % 4], 1)
            for b in range(4):
                evacuated(dve, "projr", b, 1)
            gated_add("proja", mix2, gates2)
            for t in range(KD):
                got(dve, "wout", t % 4, t // 4)
                tt_(x[:, t, :], x[:, t, :], ps[t % 4][:, 0:T], add).then_inc(evac[t % 4], 1)
            for b in range(4):
                evacuated(dve, "wout", b, 1)
            inverse_root(7, T)
            normalise(x, h, [(0, T, c("nffn", 0, 8), None)])

            aff = tiny[:, 32:64].rearrange("p (t e) -> p t e", e=N_EXP)
            got(dve, "route", 0, 0)
            do(V.tensor_reduce(tiny[:, 16:18], ps[0][:, 0:2 * N_EXP].rearrange("p (t e) -> p t e", e=N_EXP), AXX, mx_op))
            settle()
            ts_(tiny[:, 16:18], tiny[:, 16:18], -1.0, None, mult).then_inc(nm_ready, 1)
            evacuated(dve, "route", 0, 0)
            do(V.reciprocal(tiny[:, 20:22], tiny[:, 20:22]))
            settle()
            for tt in range(2):
                ts_(aff[:, tt, :], aff[:, tt, :], tiny[:, 20 + tt:21 + tt], None, mult).then_inc(aexp, 1)
            E16 = slice(0, N_EXP)
            affT, work, slot = fh[E16, 2 * T:3 * T], fh[E16, 3 * T:4 * T], fh[E16, 0:T]
            gt, eq, run, sel = (sq[E16, i * T:i * T + T] for i in range(4))
            top, n_gt, room = rt[E16, 480:488], rt[E16, 488:489], rt[E16, 489:490]
            got(dve, "route", 1, 0)
            do(V.tensor_copy(affT, ps[1][E16, 0:T]))
            V.tensor_copy(work, ps[1][E16, 0:T]).then_inc(evac[1], 1)
            evacuated(dve, "route", 1, 0)
            settle()
            for i in range(CAP // 8):
                do(V.max(top, work))
                settle()
                if i + 1 < CAP // 8:
                    do(V.match_replace(work, top, work, -1.0))
                    settle()
            do(V.memset(ones2, 1.0))
            do(ts_(gt, affT, top[:, 7:8], 0.0, ALU.is_gt, add, accum_out=n_gt))
            do(ts_(eq, affT, top[:, 7:8], None, ALU.is_equal))
            settle()
            do(ts_(room, n_gt, -1.0, float(CAP), mult, add))
            do(V.tensor_tensor_scan(run, ones2, eq, 0.0, mult, add))
            settle()
            do(stt(eq, run, room, eq, ALU.is_le, mult))
            settle()
            do(tt_(sel, gt, eq, add))
            settle()
            do(V.tensor_tensor_scan(run, ones2, sel, 0.0, mult, add))
            settle()
            tt_(slot, run, sel, mult).then_inc(slot_ready, 1)
            got(dve, "route", 2, 0)
            V.tensor_copy(rt[:, 0:2 * N_EXP], ps[2][:, 0:2 * N_EXP]).then_inc(evac[2], 1)
            evacuated(dve, "route", 2, 0)
            for tt in range(2):
                do(tt_(OH[:, tt, :].rearrange("p (e r) -> p e r", r=CAP),
                       iota.unsqueeze(1).to_broadcast([P, N_EXP, CAP]),
                       rt[:, tt * N_EXP:tt * N_EXP + N_EXP].unsqueeze(2).to_broadcast([P, N_EXP, CAP]), ALU.is_equal))
            settle()
            for tt in range(2):
                tt_(OHW[:, tt, :].rearrange("p (e r) -> p e r", r=CAP), OH[:, tt, :].rearrange("p (e r) -> p e r", r=CAP),
                    aff[:, tt, :].unsqueeze(2).to_broadcast([P, N_EXP, CAP]), mult).then_inc(oh_ready, 1)
            for tt in range(2):
                got(dve, "oht", 5 + tt, 0)
                V.tensor_copy(OHT[:, :, tt * P:tt * P + P], ps[5 + tt][:, :].rearrange("p (g n) -> p g n", n=P))\
                    .then_inc(evac[5 + tt], 1)
            with dve.Fori(0, 4) as i:
                for q_ in range(4):
                    for half in range(2):
                        b = 2 * (q_ % 2) + half
                        dve.wait_ge(hid_silu, i * 8 + (q_ * 2 + half + 1))
                        tt_(hidT[:, q_ % 2, half * P:half * P + P], msil[:, b, :], ps[b][:, P:2 * P], mult)\
                            .then_inc(evac[b], 1)
                for b in range(4):
                    got(dve, "moe", b, i * 3 + 2)
                    tt_(x[:, 2 * b:2 * b + 2, :], x[:, 2 * b:2 * b + 2, :], ps[b][:, :].rearrange("p (j n) -> p j n", n=T),
                        add).then_inc(evac[b], 1)
            inverse_root(8, T)
            settle()
            for j in range(KD):
                ins = stt(outb[:, j, :], x[:, j, :], c("nfin", j), rstd[:, 0:T], mult, mult)
            ins.then_inc(out_ready, 1)


def kernel(**inputs):
    import concourse.bacc as bacc
    from concourse.bass_utils import run_bass_kernel_spmd

    nc = bacc.Bacc("TRN2", target_bir_lowering=False, num_devices=1)
    laid = lay_out(inputs)
    dram = {n: nc.dram_tensor(f"{n}_dram", laid[n].shape, mybir.dt.from_np(laid[n].dtype), kind="ExternalInput").ap()
            for n in _ARRAYS}
    out = nc.dram_tensor("out_dram", (P, KD * T), mybir.dt.float32, kind="ExternalOutput").ap()
    build(nc, dram, out)
    r = run_bass_kernel_spmd(nc, [{f"{n}_dram": laid[n] for n in _ARRAYS}], core_ids=[0])
    y = r.results[0]["out_dram"].reshape(P, KD, T)
    return np.ascontiguousarray(y.transpose(2, 1, 0).reshape(1, T, D))
```

```python
import math

import numpy as np
import concourse.bass as bass
from concourse import mybir
from contextlib import ExitStack

P = 128
D = 1024
T = 256
KD = D // P
D_FF = 2816
FT = D_FF // P
N_MOD = 9
HEADS = 8
N_EXP = 16
CAP = 2 * T // N_EXP
FFT = 2 * T
SLAB = 16 * P
RING = 4
EX_RING = 16
GROUP = 4
N_GROUPS = N_EXP // GROUP
LAM_INIT = 0.8 - 0.6 * math.exp(-0.3 * 0)
DECAY_SCALE = math.exp(-0.5)
EPS = 1e-6
LNX_EPS = 64e-5
RW_TILES = [13, 14, 4, 5, 6, 7, 0, 1, 2, 3, 8, 9, 10, 11, 12]
US_K, US_R, US_V, US_G = 2, 6, 10, 14

COLS = [("b_ada", 72), ("g", 48), ("cw0", 24), ("cw1", 24), ("cw2", 24), ("cb", 24), ("hyb", 8), ("subg", 1),
        ("fb", 3), ("ffreq", 1), ("lam", 4), ("nmix", 8), ("mup", 15), ("mun", 15), ("w0", 8), ("a0", 8),
        ("kk", 4), ("ka", 4), ("rk", 4), ("lnw", 4), ("lnb", 4), ("nffn", 8), ("nfin", 8), ("sink", 8)]
COL0 = {}
_at = 0
for _n, _c in COLS:
    COL0[_n] = _at
    _at += _c
N_COLS = _at

DENSE = [("ada_head", 8), ("ffn1_in", FT + 20), ("ffn1_out", 11), ("z", 12 + 8), ("qk", 8), ("v", 4), ("gates", 8),
         ("hyout", 4), ("daout", 4), ("wo", 4), ("ffn2_in", FT), ("ffn2_out", 11), ("rwkv", 18.5 + 8)]
N_DENSE = int(math.ceil(sum(n for _, n in DENSE)))


def _rot(n, banks=(0, 1, 2, 3)):
    return {b: len(range(i, n, len(banks))) for i, b in enumerate(banks)}


STAGES = [("mlp", {5: 3}), ("lam", {7: 1}), ("w4", _rot(8)), ("knorm", {5: 1}),
          ("ada_head", {7: 2, 6: 2}), ("ffn1_in", {0: 11, 1: 11, 2: 11, 3: 11, 7: 5, 6: 5}), ("ffn1_out", _rot(8)),
          ("kdft", _rot(10)), ("z", {**_rot(24), 7: 2, 6: 2}), ("qk", {**_rot(16), 5: 8, 6: 8}), ("ut", {5: 2, 6: 2}), ("v", _rot(16)),
          ("uspec", {0: 2, 1: 2, 2: 2, 3: 2}), ("yinv", _rot(8)), ("gates", _rot(16)),
          ("att", {0: 8, 1: 8, 2: 8, 3: 8, 5: 8, 6: 8, 7: 8}), ("onorm", {5: 1, 0: 1, 1: 1, 2: 1, 3: 1}),
          ("daout", _rot(8)), ("wo", _rot(8)),
          ("ffn2_in", {0: 11, 1: 11, 2: 11, 3: 11}), ("ffn2_out", _rot(8)),
          ("shift", _rot(15)), ("lora", {0: 2, 1: 2, 2: 2, 3: 2}), ("kkn", {5: 1, 6: 1}),
          ("aq", _rot(6)), ("toks", {5: 3, 6: 3})]
for _s in range(2):
    STAGES += [(f"am{_s}", {0: 4, 1: 4, 2: 4, 3: 4}), (f"inv{_s}", {b: 14 for b in (0, 1, 2, 3, 5, 6)}),
               (f"tail{_s}", {0: 2, 1: 2, 2: 2, 3: 2, **({5: 2} if _s == 0 else {})})]
STAGES += [("gn", {0: 2, 1: 2, 2: 1, 3: 1, 5: 1, 6: 1}), ("batt", {0: 4, 1: 4, 5: 4, 6: 4, 7: 4}),
           ("gates2", _rot(16, (2, 3))), ("projr", _rot(8)), ("proja", _rot(8)), ("wout", _rot(8)),
           ("route", {0: 1, 1: 1, 2: 1}), ("htok", {5: 2, 6: 2}), ("oht", {5: 1, 6: 1}),
           ("moe", {b: n * N_GROUPS for b, n in {0: 2, 1: 2, 2: 2, 3: 2, 5: 3, 6: 3}.items()})]
FILLS = {}
_n = [0] * 8
for _name, _uses in STAGES:
    FILLS[_name] = list(_n)
    for _b, _c in _uses.items():
        _n[_b] += _c


def constants():
    f32 = np.float32
    out = {}
    t = np.linspace(0.0, 1.0, T, dtype=f32)[:, None]
    w = (f32(2.0 * math.pi) * np.arange(T, dtype=f32)[:, None] / f32(T)).astype(f32)
    f = np.linspace(1e-4, 15, 16, dtype=f32)[None, :]
    z = np.concatenate([t, np.cos(f * w), -np.sin(f * w)], axis=-1).astype(f32)
    out["zT"] = np.ascontiguousarray(z.T)
    deltas = np.linspace(math.log(1e-2) / 1.5, math.log(1e-2) / 0.3, D, dtype=f32)
    decay = np.exp(-t * np.abs(deltas)).astype(f32)
    out["decay"] = decay.reshape(2, P, D).transpose(1, 0, 2).reshape(P, 2 * D).copy()
    tt = np.arange(T)[:, None].astype(np.float64)
    ff = np.arange(T)[None, :].astype(np.float64)
    re = np.cos(2 * np.pi * tt * ff / FFT)
    im = -np.sin(2 * np.pi * tt * ff / FFT)
    last = (-1.0) ** np.arange(T)
    fu = np.concatenate([re, im], axis=1)
    fu[:, T] = last
    out["Fu"] = fu.reshape(2, P, 2 * T).transpose(1, 0, 2).reshape(P, 4 * T).astype(f32)
    alt = re[:, :P].copy()
    alt[:, 0] = last
    fwd = np.concatenate([re, im, alt], axis=1)
    bwd = np.concatenate([re, -im, alt], axis=1)
    bwd[0] = 0.0
    fk = np.concatenate([fwd, bwd], axis=0).reshape(4, P, 5 * P).transpose(1, 0, 2).astype(f32)
    out["FK"] = fk[:, :, :4 * P].reshape(P, 16 * P)
    out["FKalt"] = fk[:, :, 4 * P:].reshape(P, 4 * P)
    inv = np.concatenate([2 * re.T, 2 * im.T], axis=0) / FFT
    inv[0] = 1.0 / FFT
    inv[T] = last / FFT
    out["Finv"] = inv.reshape(4, P, T).transpose(1, 0, 2).reshape(P, 4 * T).astype(f32)
    p = np.arange(P)
    pos = np.arange(T)
    invf = (f32(10000.0) ** (-np.arange(0, 32, 2, dtype=f32) / f32(32))).astype(f32)
    rc = np.where(((p % 64) // 32 == 0)[:, None], (pos // 64)[None, :], (pos % 64)[None, :]).astype(f32)
    ang = (rc * invf[p % 16][:, None]).astype(f32)
    out["rope"] = np.concatenate([np.cos(ang), np.sin(ang)], axis=1).astype(f32)
    eye = np.eye(P, dtype=f32)
    blk = (p[:, None] // 64 == p[None, :] // 64).astype(f32)
    perm = np.zeros((P, P), f32)
    for m in range(P):
        if m % 32 < 16:
            perm[m + 16, m] = -1.0
        else:
            perm[m - 16, m] = 1.0
    nobwd0 = np.ones((P, 1), f32)
    nobwd0[0] = 0.0
    headsel = np.zeros((P, HEADS, HEADS), f32)
    headbc = np.zeros((HEADS, HEADS, P), f32)
    for j in range(HEADS):
        headsel[:, j, j] = 1.0
        headbc[j, j, :] = 1.0
    adasel = np.zeros((P, 4), f32)
    for half in range(2):
        for par in range(2):
            for r in range(2):
                adasel[32 * (2 * half + par) + r, 2 * half + r] = 1.0
    iota = np.broadcast_to(np.arange(1, CAP + 1, dtype=f32), (P, CAP))
    out["small"] = np.concatenate([eye, np.ones((P, P), f32), blk, perm, nobwd0, headsel.reshape(P, 64), iota, adasel], axis=1)
    out["headbc"] = headbc.reshape(HEADS, HEADS * P)
    s, u = p[:, None], p[None, :]
    keep = [np.concatenate([a, b, a, b], axis=1) for a, b in (((s < u), (s <= u)), ((s > u), (s >= u)))]
    lev = []
    for flip in (False, True):
        for lv in range(7):
            m = 1 << lv
            a, b = (u, s) if flip else (s, u)
            lev.append((a // (2 * m) == b // (2 * m)) & (a // m % 2 == 0) & (b // m % 2 == 1))
    q = np.arange(2)[None, :, None] * P + p[:, None, None]
    rel = np.abs(np.arange(T)[None, None, :] - q).astype(np.float64)
    dist = np.where(rel <= 128, -rel, -1e33)
    out["masks"] = np.concatenate([*keep, *lev, dist.reshape(P, 2 * T)], axis=1).astype(f32)
    return out


N_SMALL = 4 * P + 1 + 64 + CAP + 4
N_MASKS = 2 * 4 * P + 14 * P + 2 * T


def blocks(w):
    k, n = w.shape
    return w.reshape(k // P, P, n // P, P).transpose(2, 0, 1, 3)


def slabs(b):
    b = b.reshape(-1, P, P)
    pad = -len(b) % 16
    if pad:
        b = np.concatenate([b, np.zeros((pad, P, P), b.dtype)])
    return b.reshape(-1, 16, P, P).transpose(0, 2, 1, 3).reshape(-1, P, SLAB)


def wide(w, n=256):
    return w.reshape(KD, P, -1, n).transpose(2, 1, 0, 3).reshape(-1, P, KD * n)


def k_pairs(w):
    return w.reshape(KD // 2, 2, P, D).transpose(0, 2, 1, 3).reshape(KD // 2, P, SLAB)


def cols(v):
    return v.reshape(-1, P).T


def pad_rows(v):
    return np.concatenate([v, np.zeros((P - v.shape[0], v.shape[1]), v.dtype)], axis=0)


def lay_out(inp):
    g = {k: np.asarray(v) for k, v in inp.items()}
    ada = np.stack([k_pairs(g["w_ada"][0][:, m * D:m * D + D]) for m in range(N_MOD)])

    def ffn_in(w):
        b = blocks(w)
        return np.stack([b[:FT], b[FT:]], axis=1)

    f1 = ffn_in(g["w_ff_in"][0, 0])
    mixed = []
    for i in range(5):
        for q in range(4):
            mixed += [ada[2 + i][q:q + 1], slabs(f1[4 * i + q:4 * i + q + 1])]
    mixed += [slabs(f1[20:22])]
    w_in = g["w_in"][0]
    zs, late = slabs(blocks(w_in[:, :3 * D])), np.concatenate([ada[7], ada[8]])
    z = [a[i:i + 1] for i in range(12) for a in (zs, late) if i < len(a)]
    w2 = g["w_in_2"][0]
    b2 = blocks(w2)
    order = [h for j in range(4) for h in (j, 4 + j)]
    qcols = np.concatenate([np.arange(1920 + 64 * h, 1920 + 64 * h + 64) for h in order])
    arows = np.concatenate([np.arange(64 * h, 64 * h + 64) for h in order])
    bq = blocks(w2[:, qcols])
    second = np.concatenate([
        *(b2[i:i + 1].reshape(-1, P, P) for i in RW_TILES), bq.reshape(-1, P, P), b2[19:37].reshape(-1, P, P),
        blocks(g["w_proj_rwkv_2"][0]).reshape(-1, P, P), blocks(g["w_proj_attn_2"][0][arows]).reshape(-1, P, P),
        blocks(g["w_out_2"][0]).reshape(-1, P, P)])
    dense = np.concatenate([
        ada[0], ada[1], *mixed, slabs(blocks(g["w_ff_out"][0, 0])), *z, slabs(blocks(w_in[:, 3 * D:5 * D])),
        wide(w_in[:, 5 * D:6 * D]), slabs(blocks(w_in[:, 6 * D:])), slabs(blocks(g["w_hy_out"][0])),
        slabs(blocks(g["w_da_out"][0])), slabs(blocks(g["w_o"][0])), slabs(ffn_in(g["w_ff_in"][0, 1])),
        slabs(blocks(g["w_ff_out"][0, 1])), slabs(second)])
    assert dense.shape == (N_DENSE, P, SLAB), dense.shape
    gate, up, down = (np.stack([k_pairs(w) for w in g[n][0]]).reshape(N_GROUPS, GROUP, KD // 2, P, SLAB).swapaxes(1, 2)
                      for n in ("exp_w_gate_2", "exp_w_up_2", "exp_w_down_2"))
    gate_up = np.stack([gate, up], axis=2).reshape(N_GROUPS, -1, P, SLAB)
    experts = np.concatenate([gate_up, down.reshape(N_GROUPS, -1, P, SLAB)], axis=1).reshape(-1, P, SLAB)
    xT = g["x"][0].T.reshape(KD, P, T)
    cT = g["ctx"][0].T.reshape(KD, P, T)
    tokens = np.concatenate([xT, cT], axis=2).transpose(1, 0, 2).reshape(P, KD * 2 * T)
    cond = np.stack([cols(g["c"][0]), cols(g["c_ctx"])], axis=2).reshape(P, KD * 2)

    def mu(v):
        return v.reshape(15, P)[RW_TILES].T

    cw = g["hy_conv_w"][0]
    parts = {
        "b_ada": cols(g["b_ada"][0]), "g": cols(g["norm_g"][0]), "cw0": cols(cw[0]), "cw1": cols(cw[1]),
        "cw2": cols(cw[2]), "cb": cols(g["hy_conv_b"][0]), "hyb": cols(g["hy_bias"][0]), "subg": cols(g["subln_g"][0]),
        "fb": pad_rows(np.stack([g["filt_b1"][0], g["filt_b2"][0], g["filt_b3"][0]], axis=1)),
        "ffreq": pad_rows(g["filt_freq"][0][:, None]),
        "lam": pad_rows(np.stack([g["lambda_q1"][0], g["lambda_q2"][0], g["lambda_k1"][0], g["lambda_k2"][0]], axis=1)),
        "nmix": cols(g["norm_mix_g_2"][0]), "mup": mu(g["mu_prev_2"][0]), "mun": mu(g["mu_next_2"][0]),
        "w0": np.concatenate([cols(g["w0_f_2"][0]), cols(g["w0_b_2"][0])], axis=1),
        "a0": np.concatenate([cols(g["a0_f_2"][0]), cols(g["a0_b_2"][0])], axis=1),
        "kk": cols(g["k_k_2"][0]), "ka": cols(g["k_a_2"][0]), "rk": cols(g["r_k_2"][0].reshape(-1)),
        "lnw": cols(g["ln_x_w_2"][0]), "lnb": cols(g["ln_x_b_2"][0]), "nffn": cols(g["norm_ffn_g_2"][0]),
        "nfin": cols(g["norm_final_g_2"]), "sink": np.broadcast_to(g["attn_sink_2"][0][None, :], (P, HEADS))}
    cc = np.concatenate([parts[n] for n, _ in COLS], axis=1)
    assert cc.shape == (P, N_COLS)
    w1 = np.concatenate([g["filt_w1"][0], np.zeros((64 - 33, 64), np.float32)], axis=0)
    filt = np.concatenate([w1, g["filt_w2"][0], g["filt_w3"][0]], axis=1)
    lora = np.concatenate([
        np.concatenate([g["w_up_f_2"][0], g["w_up_b_2"][0]], axis=0),
        np.concatenate([g["a_up_f_2"][0], g["a_up_b_2"][0]], axis=0), g["g_up_2"][0]], axis=1)
    router = g["w_router_2"][0].reshape(KD, P, N_EXP).transpose(1, 0, 2).reshape(P, KD * N_EXP)
    out = {"dense": dense, "experts": experts, "tokens": tokens, "cond": cond, "cols": cc, "filt": filt,
           "w4": g["filt_w4"][0], "lora": lora, "router": router}
    out.update(constants())
    return {k: np.ascontiguousarray(v) for k, v in out.items()}


_ARRAYS = ["dense", "experts", "tokens", "cond", "cols", "filt", "w4", "lora", "router", "zT", "decay", "Fu", "FK", "FKalt",
           "Finv", "rope", "small", "headbc", "masks"]


def build(nc, dram, out_dram):
    fp32 = mybir.dt.float32
    ALU = mybir.AluOpType
    ACT = mybir.ActivationFunctionType
    AXX = mybir.AxisListType.X
    mult, add, sub, mx_op, mn_op = ALU.mult, ALU.add, ALU.subtract, ALU.max, ALU.min
    ds = bass.ds

    ctx = ExitStack()
    with ctx:
        def sb(name, shape):
            return ctx.enter_context(nc.sbuf_tensor(name, shape, fp32))

        def sem(name):
            return ctx.enter_context(nc.semaphore(name))

        PAGE = 2048
        N_PAGES = 23
        arena = sb("arena", [P, N_PAGES * PAGE])

        def page(at, words, a=None):
            lo = int(at * PAGE)
            v = arena[:, lo:lo + words]
            return v if a is None else v.rearrange("p (n a) -> p n a", a=a)

        ring = [page(i, SLAB, P) for i in range(RING)]
        ring_wide = [page(i, SLAB, 256) for i in range(RING)]
        ring_flat = [page(i, SLAB) for i in range(RING)]
        EX_PAGES = [*range(11, 23), *range(RING)]
        ex_flat = [page(i, SLAB) for i in EX_PAGES]

        col_sb = sb("col_sb", [P, N_COLS])
        small = sb("small", [P, N_SMALL])
        router = sb("router", [P, KD * N_EXP])
        mods = sb("mods", [P, N_MOD * KD * 2])
        cond = sb("cond", [P, KD * 2])
        cond_s = sb("cond_s", [P, KD * 32])
        sil = sb("sil", [P, 2 * 512])
        sq = sb("sq", [P, 2 * 512])
        sd = sb("sd", [P, 512])
        rstd = sb("rstd", [P, 512])
        eps = sb("eps", [P, 2])
        gain = sb("gain", [P, 4 * KD])
        filt = page(20, 3 * 64)[0:64]
        zT = page(20.25, T)[0:33]
        fh = sb("fh", [64, 4 * T])
        tiny = sb("tiny", [P, 64])

        def c(name, j=0, n=1):
            return col_sb[:, COL0[name] + j:COL0[name] + j + n]

        ident = small[:, 0:P]
        ones = small[:, P:2 * P]
        ones2 = fh[0:N_EXP, T:2 * T]
        blk = small[:, 2 * P:3 * P]
        perm = small[:, 3 * P:4 * P]
        nobwd0 = small[:, 4 * P:4 * P + 1]
        headsel = small[:, 4 * P + 1:4 * P + 65].rearrange("p (h m) -> p h m", m=HEADS)
        headbc = page(19, HEADS * P, P)[0:HEADS]
        iota = small[:, 4 * P + 65:N_SMALL - 4]
        adasel = small[:, N_SMALL - 4:N_SMALL]
        ada_rows = sd
        mods_v = mods[:, :].rearrange("p (m j r) -> p m j r", m=N_MOD, r=2)
        cond_v = cond_s[:, :].rearrange("p (k r) -> p k r", r=32)
        sil_v = sil[:, :].rearrange("p (s n) -> p s n", n=512)
        sq_v = sq[:, :].rearrange("p (s n) -> p s n", n=512)
        gain_v = gain[:, :].rearrange("p (s j) -> p s j", j=KD)
        router_v = router[:, :].rearrange("p (k e) -> p k e", e=N_EXP)

        def mod(m, r):
            return mods_v[:, m, :, r]

        def g(i):
            return c("g", 8 * i, 8)

        X = page(4, 4096, 512)
        h1 = page(6, 4096, 512)
        hid1 = page(8, FT * 512, 512)
        y1 = page(14, 4096, 512)
        hfil = page(20, 4096, 1024)
        habs = page(10, 4096, 1024)
        FK = page(22, 16 * P, 4 * P)
        FK_alt = page(13.5, 4 * P, P)
        decay = page(8, 2048, 1024)
        w4 = page(9, 2048)
        Kspec = page(16, 5 * 1024, 1024)
        Fu = page(18.5, 1024, 512)
        Finv = page(19, 1024, 256)
        rope = page(19.5, 512, 256)
        x0 = page(8, 2048, 256)
        u = page(9, 2048, 256)
        zv = page(10, 2048, 256)
        hy = page(10, 2048, 256)
        utok = page(11, 2048, 1024)
        yc = page(11, 2048, 256)
        Y = page(12, 4096, 1024)
        q_sb = page(22, 2048, 256)
        kT = page(20, 4096, 512)
        vtok = page(14, 4096, 1024)
        gates = page(12, 4096, 256)
        prob = page(8, 4096, 512)
        pT = page(16, 2048, 256)
        osq = page(17, 2048, 256)
        oT = page(11, 2048, 256)
        mix = page(18, 2048, 256)
        y2 = page(19, 2048, 256)
        x = page(7, 2048, 256)
        h = page(6, 2048, 256)
        hid2 = page(8, FT * 256, 256)
        y3 = page(15, 2048, 256)
        masks = page(13, N_MASKS)
        lora = page(17, 1024)
        g_up = page(13 + N_MASKS / PAGE, 512)
        keep = masks[:, 0:1024].rearrange("p (d n) -> p d n", n=512)
        level = masks[:, 1024:1024 + 14 * P].rearrange("p (l n) -> p l n", n=P)
        dist = masks[:, 1024 + 14 * P:N_MASKS].rearrange("p (q n) -> p q n", n=T)
        US = page(8, 15 * 256, 256)
        sig = page(10, 2048, 128)
        iclr = page(11, 2048, 256)
        cum = page(12, 2048, 128)
        D1 = page(15, 2048, 128)
        D2 = page(16, 2048, 128)
        Eneg = page(19, 2048, 128)
        Einc = page(20, 2048, 128)
        Eexc = page(21, 2048, 128)
        kkn = page(22, 1024, 128)
        kkr = page(22.5, 1024, 256)
        kdir = page(4, 2048, 128)
        nrm = page(5, 1024)
        gsq_kk = page(5.5, 1024)
        kkr_flat = page(22.5, 1024)
        kkn256 = page(22, 1024, 256)
        sig256 = page(10, 2048, 256)
        iclr128 = page(11, 2048, 128)
        QQw = page(15, 4096, 256)
        QQ = page(15, 4096, 128)
        KT = page(17, 2048, 128)
        BT = page(18, 2048, 128)
        AM = page(19, 8192, 512)
        XT = page(4, 2048, 128)
        Vtok = page(5, 1024, 512)
        wkv = page(5.5, 1024, 256)
        Xw = page(10, 1024, 128)
        NL = page(10.5, 1024, 128)
        Pw = page(11, 1024, 128)
        Wsb = page(11.5, 512, 64)
        nU = page(11.75, 512, 64)
        toks = page(12, 2048, 512)
        rkk = US[:, US_K:US_K + 4, :]
        gsq = page(19, 1024)
        dev = page(19.5, 1024)
        gsd = page(20, 1024)
        grs = page(20.5, 1024)
        yr = page(4, 1024, 256)
        qa = sil[:, :].rearrange("p (n a) -> p n a", a=256)
        ka = sq[:, 512:768]
        va = sq[:, 768:1024].rearrange("p (n a) -> p n a", a=128)
        oa = page(16, 1024, 256)
        gates2 = page(17, 4096, 256)
        bs = page(20, 1024, 256)
        bp = page(20.5, 1024, 256)
        bpT = page(21, 1024, 256)
        mix2 = page(8, 2048, 256)
        htok = page(9, 2048, 1024)
        OH = page(10, 1024, 512)
        OHW = page(8, 1024, 512)
        OHT = page(10.5, 1024, 256)
        xg = page(4, 1024, P)
        msil = page(4.5, 1024)
        hid = page(5, 1024)
        hidT = page(5.5, 1024, P)
        ys4 = page(8.5, 1024)
        outb = page(8, 2048, 256)
        state_v = sq[:, 0:512].rearrange("p (d j n) -> p d j n", d=2, n=64)
        scl = sb("scl", [P, 8])
        raw = sil[:, 0:512]
        rt = sil[:, 512:1024]
        raw_v = raw[:, :].rearrange("p (s n) -> p s n", n=256)

        ps = [ctx.enter_context(nc.psum_tensor(f"bank{i}", [P, 512], fp32)) for i in range(8)]

        slab_loaded = [sem(f"slab_loaded{i}") for i in range(RING)]
        slab_started = sem("slab_started")
        ex_loaded = [sem(f"ex_loaded{i}") for i in range(EX_RING)]
        ex_started = sem("ex_started")
        full = [sem(f"full{i}") for i in range(8)]
        evac = [sem(f"evac{i}") for i in range(8)]
        consts_in = sem("consts_in")
        filters_in = sem("filters_in")
        tokens_in = sem("tokens_in")
        decay_in = sem("decay_in")
        spectra_in = sem("spectra_in")
        masks_in = sem("masks_in")
        eps_set = sem("eps_set")
        cond_zero = sem("cond_zero")
        cond_ready = sem("cond_ready")
        sq_ready = sem("sq_ready")
        sq_used = sem("sq_used")
        h_ready = sem("h_ready")
        x_ready = sem("x_ready")
        dve_step = sem("dve_step")
        act_step = sem("act_step")
        router_in = sem("router_in")
        headbc_in = sem("headbc_in")
        kn_ready = sem("kn_ready")
        mu_ready = sem("mu_ready")
        es_ready = sem("es_ready")
        arg_ready = sem("arg_ready")
        sin_ready = sem("sin_ready")
        prod_ready = sem("prod_ready")
        habs_ready = sem("habs_ready")
        z_scaled = sem("z_scaled")
        u_ready = sem("u_ready")
        y_ready = sem("y_ready")
        hy_ready = sem("hy_ready")
        nm_ready = sem("nm_ready")
        p_ready = sem("p_ready")
        osq_ready = sem("osq_ready")
        hr_ready = sem("hr_ready")
        mix_ready = sem("mix_ready")
        us_scaled = sem("us_scaled")
        act_us = sem("act_us")
        kkr_ready = sem("kkr_ready")
        kksq_ready = sem("kksq_ready")
        ss_ready = sem("ss_ready")
        nrm_ready = sem("nrm_ready")
        logs_ready = sem("logs_ready")
        exps_ready = sem("exps_ready")
        qq_ready = sem("qq_ready")
        am_zero = sem("am_zero")
        x_init = sem("x_init")
        nl_ready = sem("nl_ready")
        gsq_ready = sem("gsq_ready")
        g_ready = sem("g_ready")
        gates_ready = sem("gates_ready")
        aexp = sem("aexp")
        slot_ready = sem("slot_ready")
        oh_ready = sem("oh_ready")
        out_ready = sem("out_ready")
        out_stored = sem("out_stored")

        block = ctx.enter_context(nc.Block())

        def norm_fill(r):
            return r + (KD if r >= 3 else 0)

        SCATTER = (2, 3, 5, 6)

        def take(pe, stage, b, k):
            v = FILLS[stage][b] + k
            if not (isinstance(v, int) and v == 0):
                pe.wait_ge(evac[b], v)

        def got(eng, stage, b, k):
            eng.wait_ge(full[b], FILLS[stage][b] + k + 1)

        def evacuated(eng, stage, b, k):
            eng.wait_ge(evac[b], FILLS[stage][b] + k + 1)

        class Steps:

            def __init__(self, eng, s):
                self.eng, self.s, self.n = eng, s, 0

            def do(self, ins):
                self.n += 1
                ins.then_inc(self.s, 1)

            def settle(self):
                self.eng.wait_ge(self.s, self.n)

        class Stream:

            def __init__(self, eng, loaded, started, slots, n):
                self.eng, self.loaded, self.started, self.slots, self.n = eng, loaded, started, slots, n
                self.slab, self.at, self.turn = 0, 0, 0

            def block(self):
                first = self.at == 0
                if first:
                    s = self.slab % self.n
                    self.eng.wait_ge(self.loaded[s], 16 * (self.slab // self.n + 1) + self.turn)
                blk_ap = self.slots[self.slab % self.n][:, self.at, :]
                self.at = (self.at + 1) % 16
                if self.at == 0:
                    self.slab += 1
                return blk_ap, first

            def whole(self, slots):
                assert self.at == 0
                s = self.slab % self.n
                self.eng.wait_ge(self.loaded[s], 16 * (self.slab // self.n + 1) + self.turn)
                self.slab += 1
                return slots[s]

            def loop(self, i, per):
                assert self.at == 0 and per % self.n == 0
                self.turn = i * (16 * per // self.n)

            def end_loop(self, per, turns):
                self.turn = 0
                self.slab += per * (turns - 1)

        @block.sync
        def _(sp):
            sp.dma_start(col_sb[:, :], dram["cols"]).then_inc(consts_in, 16)
            sp.dma_start(small[:, :], dram["small"]).then_inc(consts_in, 16)
            sp.dma_start(cond[:, :], dram["cond"]).then_inc(consts_in, 16)
            sp.dma_start(arena[:, 4 * PAGE:6 * PAGE], dram["tokens"]).then_inc(tokens_in, 16)
            for j in range(RING):
                sp.dma_start(ring_flat[j], dram["dense"][j]).then_inc(slab_loaded[j], 16)
            with sp.Fori(1, N_DENSE // RING) as i:
                for j in range(RING):
                    sp.wait_ge(slab_started, i * RING + (j - RING + 2))
                    sp.dma_start(ring_flat[j], dram["dense"][ds(i * RING + j, 1), :, :].rearrange("s p n -> (s p) n"))\
                        .then_inc(slab_loaded[j], 16)
            for m in range(N_DENSE - N_DENSE % RING, N_DENSE):
                sp.wait_ge(slab_started, m - RING + 2)
                sp.dma_start(ring_flat[m % RING], dram["dense"][m]).then_inc(slab_loaded[m % RING], 16)
            sp.wait_ge(mix_ready, 2)
            for j in range(EX_RING):
                if j == EX_RING - RING:
                    sp.wait_ge(h_ready, 5)
                sp.dma_start(ex_flat[j], dram["experts"][j]).then_inc(ex_loaded[j], 16)
            with sp.Fori(1, 12 * N_EXP // EX_RING) as i:
                for j in range(EX_RING):
                    sp.wait_ge(ex_started, i * EX_RING + (j // GROUP * GROUP - EX_RING + 2 * GROUP))
                    sp.dma_start(ex_flat[j],
                                 dram["experts"][ds(i * EX_RING + j, 1), :, :].rearrange("s p n -> (s p) n"))\
                        .then_inc(ex_loaded[j], 16)
            sp.wait_ge(out_ready, 1)
            sp.dma_start(out_dram, arena[:, 8 * PAGE:9 * PAGE]).then_inc(out_stored, 16)
            sp.wait_ge(out_stored, 16)

        @block.gpsimd
        def _(pool):
            nc.gpsimd.memset(cond_s[:, :], 0.0).then_inc(cond_zero, 1)
            nc.gpsimd.memset(eps[:, 0:1], EPS).then_inc(eps_set, 1)
            nc.gpsimd.memset(eps[:, 1:2], LNX_EPS).then_inc(eps_set, 1)
            pool.wait_ge(qq_ready, 1)
            nc.gpsimd.memset(page(19, 8192), 0.0).then_inc(am_zero, 1)
            for s in range(2):
                for pair in range(2):
                    for lv in range(7):
                        for d in range(2):
                            n = (s * 2 + pair) * 14 + lv * 2 + d
                            if lv == 0:
                                for b in range(4):
                                    evacuated(pool, f"am{s}", b, 2 * d + 1)
                            if n >= 2:
                                pb = 3 * d
                                got(pool, f"inv{s}" if (pair or lv) else f"inv{s - 1}", pb,
                                    pair * 7 + lv - 1 if (pair or lv) else 13)
                            u0 = 8 * d + 4 * pair
                            nc.gpsimd.tensor_tensor(NL[:, 4 * d:4 * d + 4, :], AM[:, u0:u0 + 4, 0:P],
                                                    level[:, 7 * d + lv:7 * d + lv + 1, :].to_broadcast([P, 4, P]), mult)\
                                .then_inc(nl_ready, 1)

        @block.tensor
        def _(pe):
            mm = nc.tensor.matmul
            st = Stream(pe, slab_loaded, slab_started, ring, RING)

            def product(out, k_tiles, rhs, last_sem=None):
                for k in range(k_tiles):
                    w, first = st.block()
                    ins = mm(out, lhsT=w, rhs=rhs(k), start=k == 0, stop=k == k_tiles - 1)
                    if first:
                        ins.then_inc(slab_started, 1)
                if last_sem is not None:
                    ins.then_inc(last_sem, 1)

            def stat(r, j, n):
                pe.wait_ge(sq_ready, 8 * r + j + 1)
                if j == 0 and r > 0:
                    pe.wait_ge(evac[4], norm_fill(r))
                mm(ps[4][:, 0:n], lhsT=ones, rhs=sq_v[:, j % 2, 0:n], start=j == 0, stop=j == 7)\
                    .then_inc(sq_used if j < 7 else full[4], 1)

            def tiles(stage, count, k_tiles, rhs, n=T, after=None):
                for t in range(count):
                    b = t % 4
                    take(pe, stage, b, t // 4)
                    product(ps[b][:, 0:n], k_tiles, rhs, full[b])
                    if after:
                        after(t)

            def ada_sums(stage, k, kp):
                if kp == 0:
                    take(pe, stage, 7, k)
                slab = st.whole(ring_flat)
                for q_ in range(4):
                    half, par = q_ // 2, q_ % 2
                    ins = mm(ps[7][32 * q_:32 * q_ + 32, :], lhsT=cond_v[:, 2 * kp + par, :],
                             rhs=slab[:, par * D + half * 512:par * D + half * 512 + 512],
                             start=kp == 0, stop=kp == KD // 2 - 1)
                    if q_ == 0:
                        ins.then_inc(slab_started, 1)
                if kp == KD // 2 - 1:
                    ins.then_inc(full[7], 1)

            def ada_columns(stage, k, k_rows):
                evacuated(pe, stage, 7, k_rows)
                take(pe, stage, 6, k)
                for j in range(4):
                    ins = mm(ps[6][:, 4 * j:4 * j + 4], lhsT=ada_rows[:, j * P:j * P + P], rhs=adasel,
                             start=True, stop=True)
                ins.then_inc(full[6], 1)

            pe.wait_ge(filters_in, 32)
            for n in range(3):
                take(pe, "mlp", 5, n)
                if n == 0:
                    mm(ps[5][0:64, 0:T], lhsT=filt[0:33, 0:64], rhs=zT[0:33, :], start=True, stop=True)\
                        .then_inc(full[5], 1)
                else:
                    pe.wait_ge(sin_ready, n)
                    mm(ps[5][0:64, 0:T], lhsT=filt[:, 64 * n:64 * n + 64], rhs=fh[:, 0:T], start=True, stop=True)\
                        .then_inc(full[5], 1)
            pe.wait_ge(consts_in, 48)
            pe.wait_ge(prod_ready, 1)
            mm(ps[7][:, 0:2], lhsT=ones[0:64, :], rhs=tiny[0:64, 0:2], start=True, stop=True).then_inc(full[7], 1)
            for j in range(KD):
                stat(0, j, 512)
            pe.wait_ge(sin_ready, 3)
            pe.wait_ge(decay_in, 32)
            for n in range(8):
                tt, qq = n % 2, n // 2
                take(pe, "w4", n % 4, n // 4)
                mm(ps[n % 4][:, :], lhsT=fh[:, tt * P:tt * P + P], rhs=w4[0:64, qq * 512:qq * 512 + 512],
                   start=True, stop=True).then_inc(full[n % 4], 1)
            pe.wait_ge(cond_ready, 1)
            for k in range(2):
                for kp in range(KD // 2):
                    ada_sums("ada_head", k, kp)
                ada_columns("ada_head", k, k)
            pe.wait_ge(habs_ready, 8)
            take(pe, "knorm", 5, 0)
            for ct in range(KD):
                for kt in range(4):
                    ins = mm(ps[5][:, ct:ct + 1], lhsT=habs[:, kt, ct * P:ct * P + P],
                             rhs=nobwd0 if kt == 2 else ones[:, 0:1], start=kt == 0, stop=kt == 3)
            ins.then_inc(full[5], 1)
            def filter_spectrum(tiles_):
                for n in tiles_:
                    take(pe, "kdft", n % 4, n // 4)
                    for kt in range(4):
                        part = FK_alt[:, kt, :] if n // 2 == 4 else FK[:, kt, (n // 2) * P:(n // 2) * P + P]
                        ins = mm(ps[n % 4][:, :], lhsT=part, rhs=hfil[:, kt, (n % 2) * 512:(n % 2) * 512 + 512],
                                 start=kt == 0, stop=kt == 3)
                    ins.then_inc(full[n % 4], 1)

            def ffn(stage, r, src, hid, n, with_ada):
                def pair(q_, use):
                    for b in (2 * (q_ % 2), 2 * (q_ % 2) + 1):
                        take(pe, stage + "_in", b, use)
                        product(ps[b][:, 0:n], KD, lambda k: src[:, k, 0:n], full[b])
                per = 8 if with_ada else 4
                with pe.Fori(0, 5) as i:
                    st.loop(i, per)
                    for q_ in range(4):
                        if with_ada:
                            ada_sums(stage + "_in", i, q_)
                        pair(q_, i * 2 + q_ // 2)
                    if with_ada:
                        ada_columns(stage + "_in", i, i)
                st.end_loop(per, 5)
                pair(0, 10)
                pair(1, 10)
                evacuated(pe, stage + "_in", 1, 10)
                evacuated(pe, stage + "_in", 3, 10)
                tiles(stage + "_out", KD, FT, lambda k: hid[:, k, 0:n], n,
                      lambda t: stat(r, t - 1, n) if t else None)
                stat(r, KD - 1, n)

            pe.wait_ge(h_ready, 1)
            ffn("ffn1", 1, h1, hid1, 512, True)
            pe.wait_ge(spectra_in, 16 * 5)
            filter_spectrum(range(4))
            for j in range(KD):
                stat(2, j, 512)
            filter_spectrum(range(4, 10))
            pe.wait_ge(h_ready, 2)

            def late_ada(t):
                if t % 2 and t < 16:
                    ada_sums("z", t // 8, t // 2 % 4)
                if t in (9, 17):
                    ada_columns("z", t // 16, t // 16)
            tiles("z", 24, KD, lambda k: h1[:, k, 0:T], T, late_ada)

            def rotate(n):
                evacuated(pe, "qk", n % 4, n // 4)
                take(pe, "qk", 5 + n % 2, n // 2)
                mm(ps[5 + n % 2][:, 0:T], lhsT=perm, rhs=raw_v[:, n % 2, :], start=True, stop=True)\
                    .then_inc(full[5 + n % 2], 1)
            for n in range(16):
                w_n = T if n < 8 else 512
                take(pe, "qk", n % 4, n // 4)
                product(ps[n % 4][:, 0:w_n], KD, lambda k: h1[:, k, 0:w_n], full[n % 4])
                if n:
                    rotate(n - 1)
            rotate(15)
            pe.wait_ge(u_ready, 8)
            for n in range(4):
                kt, half = n // 2, n % 2
                take(pe, "ut", 5 + half, n // 2)
                for q_ in range(4):
                    ins = nc.tensor.transpose(ps[5 + half][:, q_ * P:q_ * P + P],
                                              u[:, half * 4 + q_, kt * P:kt * P + P], ident)
                ins.then_inc(full[5 + half], 1)
            for s in range(4):
                slot = st.slab % RING
                pe.wait_ge(slab_loaded[slot], 16 * (st.slab // RING + 1))
                for tt in range(4):
                    n = 4 * s + tt
                    take(pe, "v", tt, s)
                    for k in range(KD):
                        ins = mm(ps[tt][:, 0:256], lhsT=h1[:, k, tt * P:tt * P + P], rhs=ring_wide[slot][:, k, :],
                                 start=k == 0, stop=k == KD - 1)
                        if tt == 0 and k == 0:
                            ins.then_inc(slab_started, 1)
                    ins.then_inc(full[tt], 1)
                st.slab += 1
            evacuated(pe, "ut", 5, 1)
            evacuated(pe, "ut", 6, 1)
            for i in range(4):
                j, half = i // 2, i % 2
                for im in range(2):
                    b = 2 * half + im
                    take(pe, "uspec", b, j)
                    for kt in range(2):
                        ins = mm(ps[b][:, :], lhsT=Fu[:, kt, im * T + j * P:im * T + j * P + P],
                                 rhs=utok[:, kt, half * 512:half * 512 + 512], start=kt == 0, stop=kt == 1)
                    ins.then_inc(full[b], 1)
            pe.wait_ge(y_ready, 4)
            for ct in range(KD):
                take(pe, "yinv", ct % 4, ct // 4)
                for f in range(4):
                    ins = mm(ps[ct % 4][:, 0:T], lhsT=Y[:, f, ct * P:ct * P + P], rhs=Finv[:, f, :],
                             start=f == 0, stop=f == 3)
                ins.then_inc(full[ct % 4], 1)
            tiles("gates", 16, KD, lambda k: h1[:, k, 0:T])

            def scores(hd):
                for qb in range(2):
                    for m in range(2):
                        b = 2 * m + qb
                        take(pe, "att", b, hd)
                        mm(ps[b][:, :], lhsT=q_sb[64 * m:64 * m + 64, hd, qb * P:qb * P + P],
                           rhs=kT[64 * m:64 * m + 64, hd, :], start=True, stop=True).then_inc(full[b], 1)
            evacuated(pe, "qk", 5, 7)
            evacuated(pe, "qk", 6, 7)
            for b in range(4):
                evacuated(pe, "v", b, 3)
            scores(0)
            for hd in range(HEADS):
                if hd + 1 < HEADS:
                    scores(hd + 1)
                if hd == 0:
                    pe.wait_ge(hy_ready, 1)
                pe.wait_ge(evac[4], 3 + hd)
                product(ps[4][:, 0:T], KD, lambda k: hy[:, k, :], full[4])
                pe.wait_ge(p_ready, hd + 1)
                for qb in range(2):
                    take(pe, "att", 5 + qb, hd)
                    for kt in range(4):
                        ins = nc.tensor.transpose(ps[5 + qb][:, kt * P:kt * P + P],
                                                  prob[:, 4 * (hd % 2) + qb, kt * P:kt * P + P], ident)
                    ins.then_inc(full[5 + qb], 1)
                evacuated(pe, "att", 5, hd)
                evacuated(pe, "att", 6, hd)
                take(pe, "att", 7, hd)
                for kt in range(4):
                    ins = mm(ps[7][:, 0:T], lhsT=vtok[:, kt, hd * P:hd * P + P], rhs=pT[:, 4 * (hd % 2) + kt, :],
                             start=kt == 0, stop=kt == 3)
                ins.then_inc(full[7], 1)
            pe.wait_ge(osq_ready, 8)
            take(pe, "onorm", 5, 0)
            for j in range(HEADS):
                ins = mm(ps[5][0:HEADS, 0:T], lhsT=headsel[:, j, :], rhs=osq[:, j, :], start=j == 0, stop=j == 7)
            ins.then_inc(full[5], 1)
            pe.wait_ge(hr_ready, 1)
            pe.wait_ge(headbc_in, 16)
            for j in range(HEADS):
                b = j // 2
                if j % 2 == 0:
                    take(pe, "onorm", b, 0)
                ins = mm(ps[b][:, (j % 2) * T:(j % 2) * T + T], lhsT=headbc[:, j, :], rhs=fh[0:HEADS, 0:T],
                         start=True, stop=True)
                if j % 2:
                    ins.then_inc(full[b], 1)
            for b in range(4):
                evacuated(pe, "onorm", b, 0)
            tiles("daout", KD, KD, lambda k: oT[:, k, :])
            pe.wait_ge(mix_ready, 1)
            tiles("wo", KD, KD, lambda k: mix[:, k, :], T, lambda t: stat(3, t - 1, T) if t else None)
            stat(3, KD - 1, T)
            for j in range(KD):
                stat(4, j, T)
            pe.wait_ge(h_ready, 3)
            ffn("ffn2", 5, h, hid2, T, False)
            for j in range(KD):
                stat(6, j, T)
            pe.wait_ge(h_ready, 4)

            tiles("shift", 15, KD, lambda k: h[:, k, :])
            pe.wait_ge(masks_in, 48)
            evacuated(pe, "shift", 1, 0)
            for which in range(2):
                if which == 0:
                    pe.wait_ge(act_us, 1)
                for half in range(2):
                    for d in range(2):
                        b = 2 * d + half
                        take(pe, "lora", b, which)
                        for q_ in range(2):
                            j = 2 * half + q_
                            ins = mm(ps[b][:, q_ * T:q_ * T + T],
                                     lhsT=lora[64 * d:64 * d + 64, which * 512 + j * P:which * 512 + j * P + P],
                                     rhs=US[64 * d:64 * d + 64, which, :], start=True, stop=True)
                        ins.then_inc(full[b], 1)
            pe.wait_ge(kksq_ready, 1)
            for i in range(2):
                take(pe, "kkn", 5 + i, 0)
                mm(ps[5 + i][:, :], lhsT=blk, rhs=gsq_kk[:, i * 512:i * 512 + 512], start=True, stop=True)\
                    .then_inc(full[5 + i], 1)
            tiles("aq", 5, KD, lambda k: h[:, k, :])
            bl = [st.block() for _ in range(KD)]
            take(pe, "aq", 1, 1)
            for tt in range(2):
                for k in range(KD):
                    ins = mm(ps[1][:, tt * P:tt * P + P], lhsT=h[:, k, tt * P:tt * P + P], rhs=bl[k][0],
                             start=k == 0, stop=k == KD - 1)
                    if tt == 0 and bl[k][1]:
                        ins.then_inc(slab_started, 1)
            ins.then_inc(full[1], 1)

            pe.wait_ge(qq_ready, 1)

            def to_tokens(b, k, src):
                take(pe, "toks", b, k)
                for j in range(4):
                    ins = nc.tensor.transpose(ps[b][:, j * P:j * P + P], src(j), ident)
                ins.then_inc(full[b], 1)
            for ch in range(2):
                to_tokens(5 + ch, 0, lambda j: US[:, US_V + j, ch * P:ch * P + P])
            for d in range(2):
                to_tokens(5, 1 + d, lambda j: KT[:, 8 * d + 2 * j + d, :])
                to_tokens(6, 1 + d, lambda j: BT[:, 8 * d + 2 * j + d, :])

            for s in range(2):
                for d in range(2):
                    ch = d if s == 0 else 1 - d
                    for hd in range(HEADS):
                        j, par = hd // 2, hd % 2
                        b = 2 * (j % 2) + par
                        r0 = 64 * par
                        row = 8 * d + 2 * j + ch
                        qq = QQw[r0:r0 + 64, row, :]
                        take(pe, f"am{s}", b, 2 * d + j // 2)
                        mm(ps[b][:, 0:256], lhsT=BT[r0:r0 + 64, row, :], rhs=qq, start=True, stop=True)
                        mm(ps[b][:, 256:512], lhsT=KT[r0:r0 + 64, row, :], rhs=qq, start=True, stop=True)\
                            .then_inc(full[b], 1)
                for pair in range(2):
                    for lv in range(7):
                        use = pair * 7 + lv
                        for d in range(2):
                            b = 3 * d
                            n = (s * 2 + pair) * 14 + lv * 2 + d
                            pe.wait_ge(nl_ready, n + 1)
                            if lv == 0:
                                pe.wait_ge(x_init, (s * 2 + pair) * 2 + d + 1)
                            else:
                                evacuated(pe, f"inv{s}", (1, 5)[d], use - 1)
                            take(pe, f"inv{s}", b, use)
                            for i in range(4):
                                ins = mm(ps[b][:, i * P:i * P + P], lhsT=NL[:, 4 * d + i, :], rhs=Xw[:, 4 * d + i, :],
                                         start=True, stop=True)
                            ins.then_inc(full[b], 1)
                        for d in range(2):
                            b, bx, bt = 3 * d, (1, 5)[d], (2, 6)[d]
                            u0 = 8 * d + 4 * pair
                            evacuated(pe, f"inv{s}", b, use)
                            if lv:
                                evacuated(pe, f"inv{s}", bt, use - 1)
                            take(pe, f"inv{s}", bx, use)
                            for i in range(4):
                                ins = mm(ps[bx][:, i * P:i * P + P], lhsT=XT[:, u0 + i, :], rhs=Pw[:, 4 * d + i, :],
                                         start=True, stop=True)
                            ins.then_inc(full[bx], 1)
                            take(pe, f"inv{s}", bt, use)
                            for i in range(4):
                                ins = mm(ps[bt][:, i * P:i * P + P], lhsT=Pw[:, 4 * d + i, :], rhs=XT[:, u0 + i, :],
                                         start=True, stop=True)
                            ins.then_inc(full[bt], 1)
                for d in range(2):
                    ch = d if s == 0 else 1 - d
                    if s == 0:
                        evacuated(pe, "toks", 5, 2)
                        evacuated(pe, "toks", 6, 2)
                    else:
                        evacuated(pe, "tail0", 5, d)
                    for par in range(2):
                        take(pe, f"tail{s}", par, d)
                        for j in range(4):
                            hd = 2 * j + par
                            row = 8 * d + 2 * j + ch
                            o = ps[par][:, 64 * j:64 * j + 64]
                            ins = mm(o, lhsT=AM[:, 8 * d + hd, 256:384], rhs=Vtok[:, ch, 64 * hd:64 * hd + 64],
                                     start=True, stop=s == 0)
                            if s:
                                ins = mm(o, lhsT=QQ[64 * par:64 * par + 64, 2 * row, :],
                                         rhs=state_v[64 * par:64 * par + 64, d, j, :], start=False, stop=True)
                        ins.then_inc(full[par], 1)
                    evacuated(pe, f"tail{s}", 0, d)
                    evacuated(pe, f"tail{s}", 1, d)
                    for b in (2, 6):
                        evacuated(pe, f"inv{s}", b, 13)
                    take(pe, f"tail{s}", 2, d)
                    for hd in range(HEADS):
                        ins = mm(ps[2][:, 64 * hd:64 * hd + 64], lhsT=XT[:, 8 * d + hd, :], rhs=Wsb[:, hd, :],
                                 start=True, stop=True)
                    ins.then_inc(full[2], 1)
                    evacuated(pe, f"tail{s}", 2, d)
                    take(pe, f"tail{s}", 3, d)
                    for j in range(4):
                        for par in range(2):
                            hd = 2 * j + par
                            row = 8 * d + 2 * j + ch
                            o = ps[3][64 * par:64 * par + 64, j * P:j * P + P]
                            mm(o, lhsT=Vtok[:, ch, 64 * hd:64 * hd + 64], rhs=AM[:, 8 * d + hd, 384:512],
                               start=True, stop=False)
                            ins = mm(o, lhsT=nU[:, hd, :], rhs=AM[:, 8 * d + hd, 128:256], start=False, stop=s == 0)
                            if s:
                                ins = mm(o, lhsT=state_v[64 * par:64 * par + 64, d, j, :],
                                         rhs=QQ[64 * par:64 * par + 64, 2 * row + 1, :], start=False, stop=True)
                    ins.then_inc(full[3], 1)
                    if s == 0:
                        take(pe, "tail0", 5, d)
                        for j in range(4):
                            for par in range(2):
                                hd = 2 * j + par
                                o = ps[5][64 * par:64 * par + 64, 64 * j:64 * j + 64]
                                mm(o, lhsT=toks[:, 2 * d, 64 * hd:64 * hd + 64],
                                   rhs=Vtok[:, ch, 64 * hd:64 * hd + 64], start=True, stop=False)
                                ins = mm(o, lhsT=toks[:, 2 * d + 1, 64 * hd:64 * hd + 64], rhs=nU[:, hd, :],
                                         start=False, stop=True)
                        ins.then_inc(full[5], 1)
            evacuated(pe, "tail1", 3, 1)
            for i in range(2):
                take(pe, "gn", i, 0)
                mm(ps[i][:, :], lhsT=blk, rhs=page(5.5 + 0.25 * i, 512), start=True, stop=True).then_inc(full[i], 1)
            for i in range(2):
                take(pe, "gn", 5 + i, 0)
                mm(ps[5 + i][:, :], lhsT=blk, rhs=page(8, 15 * 256)[:, (US_K + 2 * i) * T:(US_K + 2 * i + 2) * T], start=True, stop=True)\
                    .then_inc(full[5 + i], 1)
            pe.wait_ge(gsq_ready, 1)
            for i in range(2):
                take(pe, "gn", 2 + i, 0)
                mm(ps[2 + i][:, :], lhsT=blk, rhs=gsq[:, i * 512:i * 512 + 512], start=True, stop=True)\
                    .then_inc(full[2 + i], 1)
            pe.wait_ge(g_ready, 1)
            for i in range(2):
                take(pe, "gn", i, 1)
                for q_ in range(2):
                    j = 2 * i + q_
                    ins = mm(ps[i][:, q_ * T:q_ * T + T], lhsT=g_up[:, j * P:j * P + P],
                             rhs=US[:, US_G, :], start=True, stop=True)
                ins.then_inc(full[i], 1)
            def band_scores(n):
                j, par = n // 2, n % 2
                b = n % 2
                take(pe, "batt", b, n // 2)
                for qb in range(2):
                    ins = mm(ps[b][:, qb * T:qb * T + T], lhsT=qa[64 * par:64 * par + 64, j, qb * P:qb * P + P],
                             rhs=ka[64 * par:64 * par + 64, :], start=True, stop=True)
                ins.then_inc(full[b], 1)
            for b, k in ((0, 1), (1, 0), (2, 0), (3, 0), (1, 1)):
                evacuated(pe, "aq", b, k)

            def gate2(t):
                b = 2 + t % 2
                take(pe, "gates2", b, t // 2)
                product(ps[b][:, 0:T], KD, lambda k: h[:, k, :], full[b])
            band_scores(0)
            for n in range(HEADS):
                j, par = n // 2, n % 2
                if n + 1 < HEADS:
                    band_scores(n + 1)
                gate2(2 * n)
                pe.wait_ge(p_ready, HEADS + n + 1)
                b = 5 + n % 2
                take(pe, "batt", b, n // 2)
                for qb in range(2):
                    for kt in range(2):
                        ins = nc.tensor.transpose(ps[b][:, kt * T + qb * P:kt * T + qb * P + P],
                                                  bp[:, 2 * (n % 2) + qb, kt * P:kt * P + P], ident)
                ins.then_inc(full[b], 1)
                gate2(2 * n + 1)
                evacuated(pe, "batt", b, n // 2)
                if par == 0:
                    take(pe, "batt", 7, j)
                for kt in range(2):
                    ins = mm(ps[7][64 * par:64 * par + 64, 0:T], lhsT=va[:, kt, 64 * par:64 * par + 64],
                             rhs=bpT[:, 2 * (n % 2) + kt, :], start=kt == 0, stop=kt == 1)
                if par:
                    ins.then_inc(full[7], 1)
            evacuated(pe, "gn", 0, 1)
            evacuated(pe, "gn", 1, 1)
            tiles("projr", KD, 4, lambda k: yr[:, k, :])
            evacuated(pe, "batt", 7, 3)
            tiles("proja", KD, 4, lambda k: oa[:, k, :])
            pe.wait_ge(mix_ready, 2)
            tiles("wout", KD, KD, lambda k: mix2[:, k, :])
            for j in range(KD):
                stat(7, j, T)
            pe.wait_ge(router_in, 16)
            pe.wait_ge(h_ready, 5)
            take(pe, "route", 0, 0)
            for tt in range(2):
                for k in range(KD):
                    ins = mm(ps[0][:, tt * N_EXP:tt * N_EXP + N_EXP], lhsT=h[:, k, tt * P:tt * P + P],
                             rhs=router_v[:, k, :], start=k == 0, stop=k == KD - 1)
            ins.then_inc(full[0], 1)
            for n in range(4):
                tt, half = n // 2, n % 2
                take(pe, "htok", 5 + half, tt)
                for q_ in range(4):
                    ins = nc.tensor.transpose(ps[5 + half][:, q_ * P:q_ * P + P],
                                              h[:, half * 4 + q_, tt * P:tt * P + P], ident)
                ins.then_inc(full[5 + half], 1)
            pe.wait_ge(aexp, 2)
            take(pe, "route", 1, 0)
            for tt in range(2):
                ins = nc.tensor.transpose(ps[1][0:N_EXP, tt * P:tt * P + P], tiny[:, 32 + 16 * tt:48 + 16 * tt], ident)
            ins.then_inc(full[1], 1)
            pe.wait_ge(slot_ready, 1)
            take(pe, "route", 2, 0)
            for tt in range(2):
                ins = nc.tensor.transpose(ps[2][:, tt * N_EXP:tt * N_EXP + N_EXP], fh[0:N_EXP, tt * P:tt * P + P],
                                          ident[0:N_EXP, 0:N_EXP])
            ins.then_inc(full[2], 1)
            pe.wait_ge(oh_ready, 2)
            evacuated(pe, "htok", 5, 1)
            evacuated(pe, "htok", 6, 1)
            for tt in range(2):
                take(pe, "oht", 5 + tt, 0)
                for g4 in range(4):
                    ins = nc.tensor.transpose(ps[5 + tt][:, g4 * P:g4 * P + P], OHW[:, tt, g4 * P:g4 * P + P], ident)
                ins.then_inc(full[5 + tt], 1)
            evacuated(pe, "oht", 5, 0)
            evacuated(pe, "oht", 6, 0)
            ex = Stream(pe, ex_loaded, ex_started, ex_flat, EX_RING)

            def group_product(banks, kp, lhs):
                slab = [ex.whole(ex_flat) for _ in range(GROUP)]
                for par in range(2):
                    for half in range(2):
                        for e in range(GROUP):
                            ins = mm(ps[banks[half]][32 * e:32 * e + 32, :], lhsT=lhs[:, 2 * kp + par, CAP * e:CAP * e + CAP],
                                     rhs=slab[e][:, par * D + half * 512:par * D + half * 512 + 512],
                                     start=kp == 0 and par == 0, stop=kp == KD // 2 - 1 and par == 1)
                            if par == half == e == 0:
                                ins.then_inc(ex_started, GROUP)
                        if kp == KD // 2 - 1 and par == 1:
                            ins.then_inc(full[banks[half]], 1)

            with pe.Fori(0, N_GROUPS) as i:
                ex.loop(i, 12 * GROUP)
                for half in range(2):
                    take(pe, "moe", 5 + half, i * 3)
                    for q_ in range(4):
                        k = 4 * half + q_
                        for tt in range(2):
                            ins = mm(ps[5 + half][:, q_ * P:q_ * P + P], lhsT=htok[:, tt, k * P:k * P + P],
                                     rhs=OH[:, tt, ds(i * P, P)], start=tt == 0, stop=tt == 1)
                    ins.then_inc(full[5 + half], 1)
                evacuated(pe, "moe", 5, i * 3)
                evacuated(pe, "moe", 6, i * 3)
                for b in range(4):
                    take(pe, "moe", b, i * 2)
                for kp in range(KD // 2):
                    group_product((0, 1), kp, xg)
                    group_product((2, 3), kp, xg)
                for half in range(2):
                    evacuated(pe, "moe", 2 + half, i * 2)
                    take(pe, "moe", 5 + half, i * 3 + 1)
                    for q_ in range(4):
                        f = 4 * half + q_
                        ins = nc.tensor.transpose(ps[5 + half][:, q_ * P:q_ * P + P], hid[:, f * P:f * P + P], ident)
                    ins.then_inc(full[5 + half], 1)
                evacuated(pe, "moe", 5, i * 3 + 1)
                evacuated(pe, "moe", 6, i * 3 + 1)
                take(pe, "moe", 0, i * 2 + 1)
                take(pe, "moe", 1, i * 2 + 1)
                for kp in range(KD // 2):
                    group_product((0, 1), kp, hidT)
                evacuated(pe, "moe", 0, i * 2 + 1)
                evacuated(pe, "moe", 1, i * 2 + 1)
                for n, (b, k) in enumerate(((2, i * 2 + 1), (3, i * 2 + 1), (5, i * 3 + 2), (6, i * 3 + 2))):
                    take(pe, "moe", b, k)
                    for q_ in range(2):
                        dt = 2 * n + q_
                        ins = mm(ps[b][:, q_ * T:q_ * T + T], lhsT=ys4[:, dt * P:dt * P + P],
                                 rhs=OHT[:, ds(i, 1), :], start=True, stop=True)
                    ins.then_inc(full[b], 1)
            for j in range(KD):
                stat(8, j, T)

        @block.scalar
        def _(act):
            A = nc.scalar.activation
            act.dma_start(filt, dram["filt"]).then_inc(filters_in, 16)
            act.dma_start(zT, dram["zT"]).then_inc(filters_in, 16)
            act.dma_start(w4[0:64, :], dram["w4"]).then_inc(decay_in, 16)
            act.dma_start(page(8, 2048), dram["decay"]).then_inc(decay_in, 16)

            def square(r, j, src, n):
                if j >= 2:
                    act.wait_ge(sq_used, 7 * r + j - 1)
                elif r:
                    act.wait_ge(full[4], norm_fill(r))
                A(sq_v[:, j % 2, 0:n], src, ACT.Square).then_inc(sq_ready, 1)

            def root(r, n):
                act.wait_ge(full[4], norm_fill(r) + 1)
                A(sd[:, 0:n], ps[4][:, 0:n], ACT.Sqrt, bias=eps[:, 0:1], scale=1.0 / D).then_inc(evac[4], 1)

            act.wait_ge(consts_in, 48)
            act.wait_ge(cond_zero, 1)
            A(cond_v[:, :, 0:2], cond[:, :].rearrange("p (k r) -> p k r", r=2), ACT.Silu).then_inc(cond_ready, 1)
            for n in range(3):
                act.wait_ge(arg_ready, n + 1)
                A(fh[:, 0:T], fh[:, T:2 * T], ACT.Sin).then_inc(sin_ready, 1)
            got(act, "lam", 7, 0)
            A(tiny[:, 2:4], ps[7][:, 0:2], ACT.Exp).then_inc(evac[7], 1)
            act.wait_ge(tokens_in, 16)
            for j in range(KD):
                square(0, j, X[:, j, :], 512)
            act.wait_ge(eps_set, 2)
            root(0, 512)
            act.dma_start(page(22, 16 * P), dram["FK"]).then_inc(spectra_in, 16)
            act.dma_start(page(13.5, 4 * P), dram["FKalt"]).then_inc(spectra_in, 16)
            act.dma_start(page(18.5, 1024), dram["Fu"]).then_inc(spectra_in, 16)
            act.dma_start(page(19, 1024), dram["Finv"]).then_inc(spectra_in, 16)
            act.dma_start(page(19.5, 512), dram["rope"]).then_inc(spectra_in, 16)
            act.dma_start(router[:, :], dram["router"]).then_inc(router_in, 16)
            for n in range(8):
                tt, qq = n % 2, n // 2
                kt, lo = (qq // 2) * 2 + tt, (qq % 2) * 512
                evacuated(act, "w4", n % 4, n // 4)
                A(habs[:, kt, lo:lo + 512], hfil[:, kt, lo:lo + 512], ACT.Abs).then_inc(habs_ready, 1)

            def filter_spectrum(tiles_):
                for n in tiles_:
                    got(act, "kdft", n % 4, n // 4)
                    A(Kspec[:, n // 2, (n % 2) * 512:(n % 2) * 512 + 512], ps[n % 4][:, :], ACT.Copy)\
                        .then_inc(evac[n % 4], 1)

            def ffn(stage, r, y, n):
                def gate(q_, use):
                    b = 2 * (q_ % 2)
                    got(act, stage + "_in", b, use)
                    act.wait_ge(evac[b + 1], FILLS[stage + "_in"][b + 1] + use)
                    A(sil_v[:, q_ % 2, 0:n], ps[b][:, 0:n], ACT.Silu).then_inc(evac[b], 1)
                with act.Fori(0, 5) as i:
                    for q_ in range(4):
                        gate(q_, i * 2 + q_ // 2)
                gate(0, 10)
                gate(1, 10)
                leave(stage + "_out", r, y, n)

            def leave(stage, r, y, n):
                for t in range(KD):
                    got(act, stage, t % 4, t // 4)
                    A(y[:, t, 0:n], ps[t % 4][:, 0:n], ACT.Copy).then_inc(evac[t % 4], 1)
                    evacuated(act, stage, t % 4, t // 4)
                    square(r, t, y[:, t, 0:n], n)
                root(r, n)

            ffn("ffn1", 1, y1, 512)
            filter_spectrum(range(4))
            for j in range(KD):
                act.wait_ge(x_ready, 1 + j // 4)
                square(2, j, X[:, j, :], 512)
            root(2, 512)
            filter_spectrum(range(4, 10))
            for n in range(24):
                got(act, "z", n % 4, n // 4)
                A((x0, u, zv)[n // 8][:, n % 8, :], ps[n % 4][:, 0:T], ACT.Identity, bias=c("cb", n),
                  scale=c("cw1", n)).then_inc(z_scaled, 1)
            for n in range(16):
                got(act, "qk", n % 4, n // 4)
                if n >= 2:
                    evacuated(act, "qk", 5 + n % 2, n // 2 - 1)
                if n >= 8:
                    A(kT[:, n - 8, T:2 * T], ps[n % 4][:, T:2 * T], ACT.Copy)
                A(raw_v[:, n % 2, :], ps[n % 4][:, 0:T], ACT.Copy).then_inc(evac[n % 4], 1)
            for n in range(16):
                s, tt = n // 4, n % 4
                got(act, "v", tt, s)
                A(vtok[:, tt, s * 256:s * 256 + 256], ps[tt][:, 0:256], ACT.Copy).then_inc(evac[tt], 1)
            act.wait_ge(kn_ready, 1)
            for ct in range(KD):
                got(act, "yinv", ct % 4, ct // 4)
                A(yc[:, ct, :], ps[ct % 4][:, 0:T], ACT.Copy, scale=tiny[:, 8 + ct:9 + ct]).then_inc(evac[ct % 4], 1)
            act.dma_start(page(19, HEADS * P)[0:HEADS], dram["headbc"]).then_inc(headbc_in, 16)
            for n in range(16):
                got(act, "gates", n % 4, n // 4)
                A(gates[:, n, :], ps[n % 4][:, 0:T], ACT.Sigmoid).then_inc(evac[n % 4], 1)

            def exps(hd):
                act.wait_ge(nm_ready, hd + 1)
                o = 4 * (hd % 2)
                for b in range(4):
                    A(prob[:, o + b, :], ps[b][:, :], ACT.Exp, bias=tiny[:, 16 + o + b:17 + o + b],
                      scale=0.125, accum_out=tiny[:, 24 + o + b:25 + o + b]).then_inc(evac[b], 1)
            exps(0)
            for hd in range(HEADS):
                if hd + 1 < HEADS:
                    exps(hd + 1)
                got(act, "att", 5, hd)
                A(pT[:, 4 * (hd % 2):4 * (hd % 2) + 4, 0:P], ps[5][:, :].rearrange("p (k n) -> p k n", n=P), ACT.Copy)\
                    .then_inc(evac[5], 1)
                got(act, "att", 7, hd)
                A(oT[:, hd, :], ps[7][:, 0:T], ACT.Copy).then_inc(evac[7], 1)
                evacuated(act, "att", 7, hd)
                A(osq[:, hd, :], oT[:, hd, :], ACT.Square).then_inc(osq_ready, 1)
            got(act, "onorm", 5, 0)
            A(fh[0:HEADS, T:2 * T], ps[5][0:HEADS, 0:T], ACT.Sqrt, bias=eps[0:HEADS, 0:1], scale=1.0 / P)\
                .then_inc(evac[5], 1)
            leave("wo", 3, y2, T)
            act.wait_ge(mix_ready, 1)
            act.dma_start(masks, dram["masks"]).then_inc(masks_in, 16)
            act.dma_start(lora, dram["lora"][:, 0:1024]).then_inc(masks_in, 16)
            act.dma_start(g_up, dram["lora"][:, 1024:1536]).then_inc(masks_in, 16)
            for j in range(KD):
                act.wait_ge(x_ready, 3 + j // 4)
                square(4, j, x[:, j, :], T)
            root(4, T)
            ffn("ffn2", 5, y3, T)
            for j in range(KD):
                act.wait_ge(x_ready, 5 + j // 4)
                square(6, j, x[:, j, :], T)
            root(6, T)

            act.wait_ge(mu_ready, 1)
            for t in range(15):
                got(act, "shift", t % 4, t // 4)
                A(US[:, t, :], ps[t % 4][:, 0:T], ACT.Copy, scale=rt[:, 256 + t:257 + t]).then_inc(us_scaled, 1)
            evacuated(act, "shift", 0, 0)
            A(US[:, 0, :], US[:, 0, :], ACT.Tanh).then_inc(act_us, 1)
            evacuated(act, "shift", 14 % 4, 14 // 4)
            A(US[:, US_G, :], US[:, US_G, :], ACT.Sigmoid).then_inc(g_ready, 1)
            for which in range(2):
                dst = (sig256, iclr)[which]
                for half in range(2):
                    for d in range(2):
                        b = 2 * d + half
                        got(act, "lora", b, which)
                        for q_ in range(2):
                            j = 4 * d + 2 * half + q_
                            ins = A(dst[:, j, :], ps[b][:, q_ * T:q_ * T + T], ACT.Sigmoid,
                                    bias=c(("w0", "a0")[which], j))
                        ins.then_inc(evac[b], 1)
            act.wait_ge(kkr_ready, 1)
            A(gsq_kk, kkr_flat, ACT.Square).then_inc(kksq_ready, 1)
            act.wait_ge(ss_ready, 1)
            A(nrm, nrm, ACT.Sqrt).then_inc(nrm_ready, 1)
            for d in range(2):
                act.wait_ge(logs_ready, d + 1)
                o = slice(8 * d, 8 * d + 8)
                inc = (D1, D2)[d]
                A(Einc[:, o, :], inc[:, o, :], ACT.Exp, scale=-DECAY_SCALE)
                A(Eneg[:, o, :], inc[:, o, :], ACT.Exp, scale=DECAY_SCALE)
                A(Eexc[:, o, :], (D2, D1)[d][:, o, :], ACT.Exp, scale=(-DECAY_SCALE, DECAY_SCALE)[d])
                A(scl[:, 4 * d:4 * d + 4], scl[:, 4 * d:4 * d + 4], ACT.Exp, scale=-DECAY_SCALE).then_inc(exps_ready, 1)
            for t in range(5):
                got(act, "aq", t % 4, t // 4)
                A(qa[:, t, :] if t < 4 else ka, ps[t % 4][:, 0:T], ACT.Copy, scale=0.125 if t < 4 else 1.0).then_inc(evac[t % 4], 1)
            got(act, "aq", 1, 1)
            A(va, ps[1][:, 0:T].rearrange("p (k n) -> p k n", n=P), ACT.Copy).then_inc(evac[1], 1)
            for k in range(3):
                for b in (5, 6):
                    got(act, "toks", b, k)
                    dst = Vtok[:, b - 5, :] if k == 0 else toks[:, 2 * (k - 1) + b - 5, :]
                    A(dst, ps[b][:, :], ACT.Copy).then_inc(evac[b], 1)
            for s in range(2):
                for use in range(14):
                    for d in range(2):
                        got(act, f"inv{s}", 3 * d, use)
                        A(Pw[:, 4 * d:4 * d + 4, :], ps[3 * d][:, :].rearrange("p (i n) -> p i n", n=P), ACT.Copy)\
                            .then_inc(evac[3 * d], 1)
                for d in range(2):
                    for par in range(2):
                        got(act, f"tail{s}", par, d)
                        A(Wsb.rearrange("p (j r) n -> p j r n", r=2)[:, :, par, :],
                          ps[par][:, 0:256].rearrange("p (j n) -> p j n", n=64), ACT.Copy).then_inc(evac[par], 1)
                    got(act, f"tail{s}", 2, d)
                    A(nU, ps[2][:, :].rearrange("p (h n) -> p h n", n=64), ACT.Copy, scale=-1.0).then_inc(evac[2], 1)
            for i in range(2):
                evacuated(act, "gn", i, 0)
            A(gsq, dev, ACT.Square).then_inc(gsq_ready, 1)
            for i in range(2):
                got(act, "gn", 2 + i, 0)
                A(gsd[:, i * 512:i * 512 + 512], ps[2 + i][:, :], ACT.Sqrt, bias=eps[:, 1:2], scale=1.0 / 64)\
                    .then_inc(evac[2 + i], 1)
            def band_exps(n):
                act.wait_ge(nm_ready, HEADS + n + 1)
                o, head = 2 * (n % 2), n // 2 + 4 * (n % 2)
                for qb in range(2):
                    A(bp[:, o + qb, :], bs[:, o + qb, :], ACT.Exp, bias=tiny[:, 16 + o + qb:17 + o + qb],
                      accum_out=tiny[:, 20 + o + qb:21 + o + qb])
                A(tiny[:, 24 + o:26 + o], tiny[:, 16 + o:18 + o], ACT.Exp, bias=c("sink", head)).then_inc(es_ready, 1)
            def gate2(t):
                got(act, "gates2", 2 + t % 2, t // 2)
                A(gates2[:, t, :], ps[2 + t % 2][:, 0:T], ACT.Copy).then_inc(evac[2 + t % 2], 1)
            band_exps(0)
            for n in range(HEADS):
                if n + 1 < HEADS:
                    band_exps(n + 1)
                gate2(2 * n)
                b = 5 + n % 2
                got(act, "batt", b, n // 2)
                A(bpT[:, 2 * (n % 2):2 * (n % 2) + 2, :], ps[b][:, :].rearrange("p (k n) -> p k n", n=T), ACT.Copy)\
                    .then_inc(evac[b], 1)
                gate2(2 * n + 1)
                if n % 2:
                    got(act, "batt", 7, n // 2)
                    A(oa[:, n // 2, :], ps[7][:, 0:T], ACT.Copy).then_inc(evac[7], 1)
            for b in (2, 3):
                evacuated(act, "gates2", b, 7)
            for half in range(2):
                A(gates2[:, 8 * half:8 * half + 8, :], gates2[:, 8 * half:8 * half + 8, :], ACT.Sigmoid).then_inc(gates_ready, 1)
            for j in range(KD):
                evacuated(act, "wout", j % 4, j // 4)
                square(7, j, x[:, j, :], T)
            root(7, T)
            act.wait_ge(nm_ready, 2 * HEADS + 1)
            for tt in range(2):
                ins = A(tiny[:, 32 + 16 * tt:48 + 16 * tt], ps[0][:, 16 * tt:16 * tt + 16], ACT.Exp,
                        bias=tiny[:, 16 + tt:17 + tt], accum_out=tiny[:, 20 + tt:21 + tt])
            ins.then_inc(evac[0], 1)
            for n in range(4):
                tt, half = n // 2, n % 2
                got(act, "htok", 5 + half, tt)
                A(htok[:, tt, half * 512:half * 512 + 512], ps[5 + half][:, :], ACT.Copy).then_inc(evac[5 + half], 1)
            with act.Fori(0, N_GROUPS) as i:
                got(act, "moe", 5, i * 3)
                A(xg[:, 0:4, :], ps[5][:, :].rearrange("p (k n) -> p k n", n=P), ACT.Copy).then_inc(evac[5], 1)
                for half in range(2):
                    o = slice(half * 512, half * 512 + 512)
                    got(act, "moe", half, i * 2)
                    A(msil[:, o], ps[half][:, :], ACT.Silu).then_inc(evac[half], 1)
                got(act, "moe", 5, i * 3 + 1)
                A(hidT[:, 0:4, :], ps[5][:, :].rearrange("p (k n) -> p k n", n=P), ACT.Copy).then_inc(evac[5], 1)
                got(act, "moe", 0, i * 2 + 1)
                A(ys4[:, 0:512], ps[0][:, :], ACT.Copy).then_inc(evac[0], 1)
            for j in range(KD):
                b = SCATTER[j // 2]
                evacuated(act, "moe", b, (3 if b > 4 else 2) * N_GROUPS - 1)
                square(8, j, x[:, j, :], T)
            root(8, T)

        @block.vector
        def _(dve):
            V = nc.vector
            tt_, ts_, stt = V.tensor_tensor, V.tensor_scalar, V.scalar_tensor_tensor
            steps = Steps(dve, dve_step)
            do, settle = steps.do, steps.settle

            def inverse_root(r, n):
                dve.wait_ge(evac[4], norm_fill(r) + 1)
                do(V.reciprocal(rstd[:, 0:n], sd[:, 0:n]))

            def normalise(src, dst, parts):
                settle()
                for j in range(KD):
                    for lo, hi, gn_, shift in parts:
                        ins = stt(dst[:, j, lo:hi], src[:, j, lo:hi], gn_[:, j:j + 1], rstd[:, lo:hi], mult, mult)
                        if shift is not None or j < KD - 1:
                            do(ins)
                if parts[0][3] is not None:
                    settle()
                    for j in range(KD):
                        for lo, hi, gn_, shift in parts:
                            ins = ts_(dst[:, j, lo:hi], dst[:, j, lo:hi], shift[:, j:j + 1], None, add)
                ins.then_inc(h_ready, 1)

            def residual(y, parts, src, dst, n):
                settle()
                for half in range(2):
                    js = slice(4 * half, 4 * half + 4)
                    for j in range(4 * half, 4 * half + 4):
                        for lo, hi, gn_ in parts:
                            do(stt(y[:, j, lo:hi], y[:, j, lo:hi], gn_[:, j:j + 1], rstd[:, lo:hi], mult, mult))
                    settle()
                    tt_(dst[:, js, 0:n], src[:, js, 0:n], y[:, js, 0:n], add).then_inc(x_ready, 1)

            TWO_PI_HI, TWO_PI_LO = 6.28125, 2 * math.pi - 6.28125
            ROUND = 1.5 * 2.0 ** 23
            PI = 3.1415925
            dve.wait_ge(consts_in, 48)
            for n in range(3):
                got(dve, "mlp", 5, n)
                a, k1, k2 = fh[:, T:2 * T], fh[:, 2 * T:3 * T], fh[:, 3 * T:4 * T]
                ts_(a, ps[5][0:64, 0:T], c("fb", n)[0:64], c("ffreq")[0:64], add, mult).then_inc(evac[5], 1)
                evacuated(dve, "mlp", 5, n)
                do(ts_(k1, a, 1.0 / (2 * math.pi), ROUND, mult, add))
                settle()
                do(ts_(k1, k1, ROUND, None, sub))
                settle()
                do(stt(a, k1, -TWO_PI_HI, a, mult, add))
                settle()
                do(stt(a, k1, -TWO_PI_LO, a, mult, add))
                settle()
                ts_(a, a, PI, -PI, mn_op, mx_op).then_inc(arg_ready, 1)
            tt_(tiny[0:64, 0:2], c("lam", 0, 2)[0:64], c("lam", 2, 2)[0:64], mult).then_inc(prod_ready, 1)
            evacuated(dve, "lam", 7, 0)
            do(stt(tiny[:, 4:5], tiny[:, 3:4], LAM_INIT, tiny[:, 2:3], sub, sub))
            inverse_root(0, 512)
            dve.wait_ge(decay_in, 32)
            for n in range(8):
                tt, qq = n % 2, n // 2
                kt, lo = (qq // 2) * 2 + tt, (qq % 2) * 512
                got(dve, "w4", n % 4, n // 4)
                tt_(hfil[:, kt, lo:lo + 512], ps[n % 4][:, :], decay[:, tt, lo:lo + 512], mult).then_inc(evac[n % 4], 1)

            def ada_sums(stage, k):
                got(dve, stage, 7, k)
                V.tensor_copy(ada_rows[:, :], ps[7][:, :]).then_inc(evac[7], 1)

            def ada_columns(stage, k, m):
                got(dve, stage, 6, k)
                tt_(mods[:, :].rearrange("p (m h j r) -> p m j h r", m=N_MOD, h=2, r=2)[:, m, :, :, :],
                    ps[6][:, 0:16].rearrange("p (m j h r) -> p m j h r", m=1, h=2, r=2),
                    c("b_ada", 0, 72).rearrange("p (m h j) -> p m j h", m=N_MOD, h=2)[:, m, :, :].unsqueeze(4)
                    .to_broadcast([P, 1, 4, 2, 2]), add).then_inc(evac[6], 1)
            settle()
            for k in range(2):
                ada_sums("ada_head", k)
                ada_columns("ada_head", k, slice(k, k + 1))
            evacuated(dve, "ada_head", 6, 1)
            for r in range(2):
                do(stt(gain_v[:, r, :], mod(1, r), 1.0, g(0), add, mult))
            normalise(X, h1, [(0, T, gain_v[:, 0, :], mod(0, 0)), (T, 2 * T, gain_v[:, 1, :], mod(0, 1))])
            got(dve, "knorm", 5, 0)
            ts_(tiny[:, 8:16], ps[5][:, 0:KD], EPS, None, add).then_inc(evac[5], 1)
            evacuated(dve, "knorm", 5, 0)
            V.reciprocal(tiny[:, 8:16], tiny[:, 8:16]).then_inc(kn_ready, 1)

            def ffn_in(stage, hid, n, with_ada):
                def up(q_, use, at):
                    b = 2 * (q_ % 2)
                    dve.wait_ge(evac[b], FILLS[stage + "_in"][b] + use + 1)
                    got(dve, stage + "_in", b + 1, use)
                    tt_(hid[:, at, 0:n], sil_v[:, q_ % 2:q_ % 2 + 1, 0:n], ps[b + 1][:, 0:n].unsqueeze(1), mult)\
                        .then_inc(evac[b + 1], 1)
                with dve.Fori(0, 5) as i:
                    for q_ in range(4):
                        if with_ada and q_ == 3:
                            ada_sums(stage + "_in", i)
                        up(q_, i * 2 + q_ // 2, ds(i * 4 + q_, 1))
                    if with_ada:
                        ada_columns(stage + "_in", i, ds(i + 2, 1))
                up(0, 10, slice(20, 21))
                up(1, 10, slice(21, 22))

            ffn_in("ffn1", hid1, 512, True)
            evacuated(dve, "ffn1_in", 6, 4)
            for r in range(2):
                do(stt(gain_v[:, 2 + r, :], mod(2, r), 0.5, g(1), mult, mult))
                do(stt(gain_v[:, r, :], mod(4, r), 1.0, g(2), add, mult))
            inverse_root(1, 512)
            residual(y1, [(0, T, gain_v[:, 2, :]), (T, 2 * T, gain_v[:, 3, :])], X, X, 512)
            inverse_root(2, 512)
            normalise(X, h1, [(0, T, gain_v[:, 0, :], mod(3, 0)), (T, 2 * T, gain_v[:, 1, :], mod(3, 1))])
            for n in range(24):
                b, dst = n % 4, (x0, u, zv)[n // 8][:, n % 8, :]
                dve.wait_ge(z_scaled, n + 1)
                do(stt(dst[:, 1:T], ps[b][:, 0:T - 1], c("cw0", n), dst[:, 1:T], mult, add))
                settle()
                stt(dst[:, 0:T - 1], ps[b][:, 1:T], c("cw2", n), dst[:, 0:T - 1], mult, add).then_inc(evac[b], 1)
                if n >= 16:
                    evacuated(dve, "z", b, n // 4)
                    tt_(u[:, n - 16, :], u[:, n - 16, :], dst, mult).then_inc(u_ready, 1)
                if n in (7, 15):
                    ada_sums("z", n // 8)
                if n in (9, 17):
                    ada_columns("z", n // 16, slice(7 + n // 16, 8 + n // 16))
            for n in range(16):
                b = 5 + n % 2
                dst = q_sb[:, n, :] if n < 8 else kT[:, n - 8, 0:T]
                got(dve, "qk", b, n // 2)
                if n >= 2:
                    evacuated(dve, "qk", b, n // 2 - 1)
                r = rt[:, (n % 2) * T:(n % 2) * T + T]
                do(tt_(r, ps[b][:, 0:T], rope[:, 1, :], mult))
                do(tt_(dst, raw_v[:, n % 2, :], rope[:, 0, :], mult))
                settle()
                tt_(dst, dst, r, add).then_inc(evac[b], 1)
            for n in range(4):
                kt, half = n // 2, n % 2
                got(dve, "ut", 5 + half, kt)
                V.tensor_copy(utok[:, kt, half * 512:half * 512 + 512], ps[5 + half][:, :]).then_inc(evac[5 + half], 1)
            for i in range(4):
                j, half = i // 2, i % 2
                o = slice(half * 512, half * 512 + 512)
                br, bi = 2 * half, 2 * half + 1
                k_alt = Kspec[:, 4, o] if j == 0 else Kspec[:, 1, o]
                if i:
                    settle()
                    dve.wait_ge(y_ready, i)
                got(dve, "uspec", br, j)
                do(tt_(Y[:, j, o], ps[br][:, :], Kspec[:, j, o], mult))
                tt_(Y[:, 2 + j, o], ps[br][:, :], Kspec[:, 2 + j, o], mult).then_inc(evac[br], 1)
                got(dve, "uspec", bi, j)
                do(tt_(rt, ps[bi][:, :], Kspec[:, 2 + j, o], mult))
                tt_(raw, ps[bi][:, :], k_alt, mult).then_inc(evac[bi], 1)
                settle()
                do(tt_(Y[:, j, o], Y[:, j, o], rt, sub))
                evacuated(dve, "uspec", bi, j)
                evacuated(dve, "uspec", br, j)
                tt_(Y[:, 2 + j, o], Y[:, 2 + j, o], raw, add).then_inc(y_ready, 1)
            for ct in range(KD):
                evacuated(dve, "yinv", ct % 4, ct // 4)
                do(stt(yc[:, ct, :], u[:, ct, :], c("hyb", ct), yc[:, ct, :], mult, add))
            settle()
            tt_(hy, yc, x0, mult).then_inc(hy_ready, 1)

            def maxima(hd):
                o = 4 * (hd % 2)
                for b in range(4):
                    got(dve, "att", b, hd)
                    do(V.tensor_reduce(tiny[:, 16 + o + b:17 + o + b], ps[b][:, :], AXX, mx_op))
                settle()
                ts_(tiny[:, 16 + o:20 + o], tiny[:, 16 + o:20 + o], -0.125, None, mult).then_inc(nm_ready, 1)
            maxima(0)
            for hd in range(HEADS):
                o = 4 * (hd % 2)
                for b in range(4):
                    evacuated(dve, "att", b, hd)
                do(V.reciprocal(tiny[:, 24 + o:28 + o], tiny[:, 24 + o:28 + o]))
                settle()
                do(ts_(tiny[:, 26 + o:28 + o], tiny[:, 26 + o:28 + o], tiny[:, 4:5], None, mult))
                for qb in range(2):
                    do(ts_(prob[:, o + qb, :], prob[:, o + qb, :], tiny[:, 24 + o + qb:25 + o + qb], None, mult))
                settle()
                for qb in range(2):
                    ins = stt(prob[:, o + qb, :], prob[:, o + 2 + qb, :], tiny[:, 26 + o + qb:27 + o + qb],
                              prob[:, o + qb, :], mult, add)
                ins.then_inc(p_ready, 1)
                if hd + 1 < HEADS:
                    maxima(hd + 1)
                got(dve, "att", 6, hd)
                V.tensor_copy(pT[:, o:o + 4, P:2 * P], ps[6][:, :].rearrange("p (k n) -> p k n", n=P))\
                    .then_inc(evac[6], 1)
                if hd == 0:
                    for b in range(4):
                        evacuated(dve, "gates", b, 3)
                dve.wait_ge(full[4], 3 + hd + 1)
                tt_(mix[:, hd, :], ps[4][:, 0:T], gates[:, hd, :], mult).then_inc(evac[4], 1)
            do(ts_(tiny[:, 5:6], c("subg"), 1.0 - LAM_INIT, None, mult))
            evacuated(dve, "onorm", 5, 0)
            V.reciprocal(fh[0:HEADS, 0:T], fh[0:HEADS, T:2 * T]).then_inc(hr_ready, 1)
            settle()
            for j in range(HEADS):
                got(dve, "onorm", j // 2, 0)
                ins = stt(oT[:, j, :], oT[:, j, :], tiny[:, 5:6], ps[j // 2][:, (j % 2) * T:(j % 2) * T + T], mult, mult)
                if j % 2:
                    ins.then_inc(evac[j // 2], 1)
            def gated_add(stage, dst, gts):
                for t in range(KD):
                    got(dve, stage, t % 4, t // 4)
                    settle()
                    tt_(rt[:, 0:T], ps[t % 4][:, 0:T], gts[:, KD + t, :], mult).then_inc(evac[t % 4], 1)
                    evacuated(dve, stage, t % 4, t // 4)
                    ins = tt_(dst[:, t, :], dst[:, t, :], rt[:, 0:T], add)
                    if t < KD - 1:
                        do(ins)
                ins.then_inc(mix_ready, 1)
            dve.wait_ge(evac[4], norm_fill(3))
            gated_add("daout", mix, gates)
            do(tt_(gain_v[:, 2, :], mod(5, 0), g(3), mult))
            do(stt(gain_v[:, 0, :], mod(7, 0), 1.0, g(4), add, mult))
            inverse_root(3, T)
            residual(y2, [(0, T, gain_v[:, 2, :])], X, x, T)
            inverse_root(4, T)
            normalise(x, h, [(0, T, gain_v[:, 0, :], mod(6, 0))])
            ffn_in("ffn2", hid2, T, False)
            do(stt(gain_v[:, 2, :], mod(8, 0), 0.5, g(5), mult, mult))
            inverse_root(5, T)
            residual(y3, [(0, T, gain_v[:, 2, :])], x, x, T)
            do(tt_(rt[:, 256:271], c("mup", 0, 15), c("mun", 0, 15), add))
            settle()
            ts_(rt[:, 256:271], rt[:, 256:271], -1.0, 1.0, mult, add).then_inc(mu_ready, 1)
            inverse_root(6, T)
            normalise(x, h, [(0, T, c("nmix", 0, 8), None)])

            for t in range(15):
                b, dst = t % 4, US[:, t, :]
                dve.wait_ge(us_scaled, t + 1)
                do(stt(dst[:, 1:T], ps[b][:, 0:T - 1], c("mup", t), dst[:, 1:T], mult, add))
                settle()
                stt(dst[:, 0:T - 1], ps[b][:, 1:T], c("mun", t), dst[:, 0:T - 1], mult, add).then_inc(evac[b], 1)
            for b in range(4):
                dve.wait_ge(evac[b], FILLS["lora"][b])
            for j in range(3):
                do(ts_(kkr[:, j, :], US[:, US_K + j, :], c("kk", j), None, mult))
            ts_(kkr[:, 3, :], US[:, US_K + 3, :], c("kk", 3), None, mult).then_inc(kkr_ready, 1)
            for d in range(2):
                for half in range(2):
                    evacuated(dve, "lora", 2 * d + half, 0)
                for row in range(8 * d, 8 * d + 8):
                    do(V.tensor_tensor_scan(cum[:, row, :], ones, sig[:, row, :], 0.0, mult, add))
                settle()
                o = slice(8 * d, 8 * d + 8)
                do(tt_(D1[:, o, :], cum[:, o, :], cum[:, o, 63:64].to_broadcast([P, 8, P]), sub))
                cv = cum[:, o, :].rearrange("p (j c) n -> p j c n", c=2)
                sv = scl[:, 4 * d:4 * d + 4]
                do(tt_(sv, cv[:, :, 0, 127], cv[:, :, 0, 63], sub))
                settle()
                do(tt_(sv, sv, cv[:, :, 1, 63], add))
                if d == 0:
                    ins = tt_(D2[:, o, :], D1[:, o, :], sig[:, o, :], sub)
                else:
                    ins = tt_(D2[:, o, :], sig[:, o, :], D1[:, o, :], sub)
                ins.then_inc(logs_ready, 1)
            for i in range(2):
                got(dve, "kkn", 5 + i, 0)
                ts_(nrm[:, i * 512:i * 512 + 512], ps[5 + i][:, :], 1e-24, None, mx_op).then_inc(evac[5 + i], 1)
            evacuated(dve, "kkn", 5, 0)
            evacuated(dve, "kkn", 6, 0)
            V.tensor_copy(tiny[:, 0:1], nrm[:, 0:1]).then_inc(ss_ready, 1)
            do(ts_(tiny[:, 28:32], c("ka", 0, 4), -1.0, 1.0, mult, add))
            for b in range(4):
                evacuated(dve, "lora", b, 1)
            settle()
            kd256 = page(4, 2048, 256)
            for d in range(2):
                for j in range(4):
                    do(ts_(kd256[:, 4 * d + j, :], iclr[:, 4 * d + j, :], c("ka", j), tiny[:, 28 + j:29 + j], mult, add))
            settle()
            for d in range(2):
                do(tt_(kd256[:, 4 * d:4 * d + 4, :], kd256[:, 4 * d:4 * d + 4, :], US[:, US_K:US_K + 4, :], mult))
            settle()
            do(tt_(rkk, kd256[:, 0:4, :], kd256[:, 4:8, :], add))
            settle()
            for j in range(4):
                do(stt(US[:, US_K + j, :], US[:, US_K + j, :], c("rk", j), US[:, US_R + j, :], mult, mult))
            dve.wait_ge(nrm_ready, 1)
            do(V.reciprocal(nrm, nrm))
            settle()
            do(tt_(kkn256, kkr, nrm.rearrange("p (j n) -> p j n", n=T), mult))
            settle()
            r_rows = page(8, 15 * 256, P)[:, 2 * US_R:2 * US_R + 8, :]
            QQv = QQ.rearrange("p (a w) n -> p a w n", w=2)
            for d in range(2):
                dve.wait_ge(exps_ready, d + 1)
            for d in range(2):
                o = slice(8 * d, 8 * d + 8)
                do(tt_(BT[:, o, :], kkn, iclr128[:, o, :], mult))
                do(tt_(KT[:, o, :], kdir[:, o, :], Eneg[:, o, :], mult))
                do(tt_(QQv[:, o, 0, :], kkn, Eexc[:, o, :], mult))
                do(tt_(QQv[:, o, 1, :], r_rows, Einc[:, o, :], mult))
            settle()
            tt_(BT, BT, Eneg, mult).then_inc(qq_ready, 1)
            dve.wait_ge(am_zero, 1)
            dve.wait_ge(masks_in, 48)
            keep_bits = keep.bitcast(mybir.dt.uint32)
            for s in range(2):
                for d in range(2):
                    for hd in range(HEADS):
                        j, par = hd // 2, hd % 2
                        b = 2 * (j % 2) + par
                        got(dve, f"am{s}", b, 2 * d + j // 2)
                        V.copy_predicated(AM[:, 8 * d + hd, :], keep_bits[:, d, :], ps[b][:, :]).then_inc(evac[b], 1)
                for pair in range(2):
                    for d in range(2):
                        u0 = 8 * d + 4 * pair
                        eye4 = ident.unsqueeze(1).to_broadcast([P, 4, P])
                        if s:
                            got(dve, "tail0", 2, d)
                        if s or pair:
                            for b in ((1, 2), (5, 6))[d]:
                                evacuated(dve, f"inv{s if pair else 0}", b, 6 if pair else 13)
                        do(V.tensor_copy(Xw[:, 4 * d:4 * d + 4, :], eye4))
                        V.tensor_copy(XT[:, u0:u0 + 4, :], eye4).then_inc(x_init, 1)
                    for lv in range(7):
                        use = pair * 7 + lv
                        for d in range(2):
                            bx, bt = (1, 5)[d], (2, 6)[d]
                            u0 = 8 * d + 4 * pair
                            if lv == 0:
                                dve.wait_ge(x_init, (s * 2 + pair) * 2 + d + 1)
                            else:
                                evacuated(dve, f"inv{s}", bx, use - 1)
                                evacuated(dve, f"inv{s}", bt, use - 1)
                            for dst, b in ((Xw[:, 4 * d:4 * d + 4, :], bx), (XT[:, u0:u0 + 4, :], bt)):
                                got(dve, f"inv{s}", b, use)
                                tt_(dst, dst, ps[b][:, :].rearrange("p (i n) -> p i n", n=P), sub).then_inc(evac[b], 1)
                for d in range(2):
                    ch = d if s == 0 else 1 - d
                    w_c = wkv[:, :, ch * P:ch * P + P]
                    y_ps = ps[3][:, :].rearrange("p (j n) -> p j n", n=P)
                    got(dve, f"tail{s}", 3, d)
                    if s == 0:
                        V.tensor_copy(w_c, y_ps).then_inc(evac[3], 1)
                        got(dve, "tail0", 5, d)
                        tt_(state_v[:, d, :, :], ps[5][:, 0:256].rearrange("p (j n) -> p j n", n=64),
                            scl[:, 4 * d:4 * d + 4].unsqueeze(2).to_broadcast([P, 4, 64]), mult).then_inc(evac[5], 1)
                    else:
                        evacuated(dve, "tail0", 3, 1)
                        tt_(w_c, w_c, y_ps, add).then_inc(evac[3], 1)
            wkv_flat = page(5.5, 1024)
            evacuated(dve, "tail1", 3, 1)
            for i in range(2):
                o = slice(i * 512, i * 512 + 512)
                got(dve, "gn", i, 0)
                stt(dev[:, o], ps[i][:, :], -1.0 / 64, wkv_flat[:, o], mult, add).then_inc(evac[i], 1)
            US_flat = page(8, 15 * 256)
            bonus = page(21, 1024)
            for i in range(2):
                got(dve, "gn", 5 + i, 0)
                tt_(bonus[:, i * 512:i * 512 + 512], ps[5 + i][:, :],
                    US_flat[:, US_V * T + i * 512:US_V * T + i * 512 + 512], mult).then_inc(evac[5 + i], 1)
            for i in range(2):
                evacuated(dve, "gn", 2 + i, 0)
            do(V.reciprocal(grs, gsd))
            settle()
            do(tt_(dev, dev, grs, mult))
            settle()
            for j in range(4):
                do(ts_(dev[:, j * T:j * T + T], dev[:, j * T:j * T + T], c("lnw", j), c("lnb", j), mult, add))
            evacuated(dve, "gn", 5, 0)
            evacuated(dve, "gn", 6, 0)
            settle()
            do(tt_(dev, dev, bonus, add))
            settle()
            for i in range(2):
                o = slice(i * 512, i * 512 + 512)
                got(dve, "gn", i, 1)
                tt_(page(4, 1024)[:, o], dev[:, o], ps[i][:, :], mult).then_inc(evac[i], 1)

            def band_maxima(n):
                b, o, head = n % 2, 2 * (n % 2), n // 2 + 4 * (n % 2)
                got(dve, "batt", b, n // 2)
                stt(bs[:, o:o + 2, :], dist, 2.0 ** -(head + 1), ps[b][:, :].rearrange("p (q n) -> p q n", n=T), mult, add)\
                    .then_inc(evac[b], 1)
                evacuated(dve, "batt", b, n // 2)
                do(V.tensor_reduce(tiny[:, 16 + o:18 + o], bs[:, o:o + 2, :], AXX, mx_op))
                settle()
                ts_(tiny[:, 16 + o:18 + o], tiny[:, 16 + o:18 + o], c("sink", head), -1.0, mx_op, mult)\
                    .then_inc(nm_ready, 1)
            band_maxima(0)
            for n in range(HEADS):
                o = 2 * (n % 2)
                dve.wait_ge(es_ready, n + 1)
                do(tt_(tiny[:, 20 + o:22 + o], tiny[:, 20 + o:22 + o], tiny[:, 24 + o:26 + o], add))
                settle()
                do(V.reciprocal(tiny[:, 20 + o:22 + o], tiny[:, 20 + o:22 + o]))
                settle()
                for qb in range(2):
                    ins = ts_(bp[:, o + qb, :], bp[:, o + qb, :], tiny[:, 20 + o + qb:21 + o + qb], None, mult)
                ins.then_inc(p_ready, 1)
                if n + 1 < HEADS:
                    band_maxima(n + 1)
            for t in range(KD):
                got(dve, "projr", t % 4, t // 4)
                if t == 0:
                    dve.wait_ge(gates_ready, 2)
                tt_(mix2[:, t, :], ps[t % 4][:, 0:T], gates2[:, t, :], mult).then_inc(evac[t % 4], 1)
            for b in range(4):
                evacuated(dve, "projr", b, 1)
            gated_add("proja", mix2, gates2)
            for t in range(KD):
                got(dve, "wout", t % 4, t // 4)
                tt_(x[:, t, :], x[:, t, :], ps[t % 4][:, 0:T], add).then_inc(evac[t % 4], 1)
            for b in range(4):
                evacuated(dve, "wout", b, 1)
            inverse_root(7, T)
            normalise(x, h, [(0, T, c("nffn", 0, 8), None)])

            aff = tiny[:, 32:64].rearrange("p (t e) -> p t e", e=N_EXP)
            got(dve, "route", 0, 0)
            do(V.tensor_reduce(tiny[:, 16:18], ps[0][:, 0:2 * N_EXP].rearrange("p (t e) -> p t e", e=N_EXP), AXX, mx_op))
            settle()
            ts_(tiny[:, 16:18], tiny[:, 16:18], -1.0, None, mult).then_inc(nm_ready, 1)
            evacuated(dve, "route", 0, 0)
            do(V.reciprocal(tiny[:, 20:22], tiny[:, 20:22]))
            settle()
            for tt in range(2):
                ts_(aff[:, tt, :], aff[:, tt, :], tiny[:, 20 + tt:21 + tt], None, mult).then_inc(aexp, 1)
            E16 = slice(0, N_EXP)
            affT, work, slot = fh[E16, 2 * T:3 * T], fh[E16, 3 * T:4 * T], fh[E16, 0:T]
            gt, eq, run, sel = (sq[E16, i * T:i * T + T] for i in range(4))
            top, n_gt, room = rt[E16, 480:488], rt[E16, 488:489], rt[E16, 489:490]
            got(dve, "route", 1, 0)
            do(V.tensor_copy(affT, ps[1][E16, 0:T]))
            V.tensor_copy(work, ps[1][E16, 0:T]).then_inc(evac[1], 1)
            evacuated(dve, "route", 1, 0)
            settle()
            for i in range(CAP // 8):
                do(V.max(top, work))
                settle()
                if i + 1 < CAP // 8:
                    do(V.match_replace(work, top, work, -1.0))
                    settle()
            do(V.memset(ones2, 1.0))
            do(ts_(gt, affT, top[:, 7:8], 0.0, ALU.is_gt, add, accum_out=n_gt))
            do(ts_(eq, affT, top[:, 7:8], None, ALU.is_equal))
            settle()
            do(ts_(room, n_gt, -1.0, float(CAP), mult, add))
            do(V.tensor_tensor_scan(run, ones2, eq, 0.0, mult, add))
            settle()
            do(stt(eq, run, room, eq, ALU.is_le, mult))
            settle()
            do(tt_(sel, gt, eq, add))
            settle()
            do(V.tensor_tensor_scan(run, ones2, sel, 0.0, mult, add))
            settle()
            tt_(slot, run, sel, mult).then_inc(slot_ready, 1)
            got(dve, "route", 2, 0)
            V.tensor_copy(rt[:, 0:2 * N_EXP], ps[2][:, 0:2 * N_EXP]).then_inc(evac[2], 1)
            evacuated(dve, "route", 2, 0)
            for tt in range(2):
                do(tt_(OH[:, tt, :].rearrange("p (e r) -> p e r", r=CAP),
                       iota.unsqueeze(1).to_broadcast([P, N_EXP, CAP]),
                       rt[:, tt * N_EXP:tt * N_EXP + N_EXP].unsqueeze(2).to_broadcast([P, N_EXP, CAP]), ALU.is_equal))
            settle()
            for tt in range(2):
                tt_(OHW[:, tt, :].rearrange("p (e r) -> p e r", r=CAP), OH[:, tt, :].rearrange("p (e r) -> p e r", r=CAP),
                    aff[:, tt, :].unsqueeze(2).to_broadcast([P, N_EXP, CAP]), mult).then_inc(oh_ready, 1)
            for tt in range(2):
                got(dve, "oht", 5 + tt, 0)
                V.tensor_copy(OHT[:, :, tt * P:tt * P + P], ps[5 + tt][:, :].rearrange("p (g n) -> p g n", n=P))\
                    .then_inc(evac[5 + tt], 1)
            with dve.Fori(0, N_GROUPS) as i:
                got(dve, "moe", 6, i * 3)
                V.tensor_copy(xg[:, 4:8, :], ps[6][:, :].rearrange("p (k n) -> p k n", n=P)).then_inc(evac[6], 1)
                for half in range(2):
                    o = slice(half * 512, half * 512 + 512)
                    evacuated(dve, "moe", half, i * 2)
                    got(dve, "moe", 2 + half, i * 2)
                    tt_(hid[:, o], msil[:, o], ps[2 + half][:, :], mult).then_inc(evac[2 + half], 1)
                got(dve, "moe", 6, i * 3 + 1)
                V.tensor_copy(hidT[:, 4:8, :], ps[6][:, :].rearrange("p (k n) -> p k n", n=P)).then_inc(evac[6], 1)
                got(dve, "moe", 1, i * 2 + 1)
                V.tensor_copy(ys4[:, 512:1024], ps[1][:, :]).then_inc(evac[1], 1)
                for n, (b, k) in enumerate(((2, i * 2 + 1), (3, i * 2 + 1), (5, i * 3 + 2), (6, i * 3 + 2))):
                    got(dve, "moe", b, k)
                    tt_(x[:, 2 * n:2 * n + 2, :], x[:, 2 * n:2 * n + 2, :], ps[b][:, :].rearrange("p (j n) -> p j n", n=T),
                        add).then_inc(evac[b], 1)
            inverse_root(8, T)
            settle()
            for j in range(KD):
                ins = stt(outb[:, j, :], x[:, j, :], c("nfin", j), rstd[:, 0:T], mult, mult)
            ins.then_inc(out_ready, 1)


def kernel(**inputs):
    import concourse.bacc as bacc
    from concourse.bass_utils import run_bass_kernel_spmd

    nc = bacc.Bacc("TRN2", target_bir_lowering=False, num_devices=1)
    laid = lay_out(inputs)
    dram = {n: nc.dram_tensor(f"{n}_dram", laid[n].shape, mybir.dt.from_np(laid[n].dtype), kind="ExternalInput").ap()
            for n in _ARRAYS}
    out = nc.dram_tensor("out_dram", (P, KD * T), mybir.dt.float32, kind="ExternalOutput").ap()
    build(nc, dram, out)
    r = run_bass_kernel_spmd(nc, [{f"{n}_dram": laid[n] for n in _ARRAYS}], core_ids=[0])
    y = r.results[0]["out_dram"].reshape(P, KD, T)
    return np.ascontiguousarray(y.transpose(2, 1, 0).reshape(1, T, D))
```

```python
import math

import numpy as np
import concourse.bass as bass
from concourse import mybir
from contextlib import ExitStack

P = 128
D = 1024
T = 256
KD = D // P
D_FF = 2816
FT = D_FF // P
N_MOD = 9
HEADS = 8
N_EXP = 16
CAP = 2 * T // N_EXP
FFT = 2 * T
SLAB = 16 * P
RING = 4
EX_RING = 16
EX_EARLY = 3
GROUP = 4
N_GROUPS = N_EXP // GROUP
LAM_INIT = 0.8 - 0.6 * math.exp(-0.3 * 0)
DECAY_SCALE = math.exp(-0.5)
EPS = 1e-6
LNX_EPS = 64e-5
RW_TILES = [13, 14, 4, 5, 6, 7, 0, 1, 2, 3, 8, 9, 10, 11, 12]
US_K, US_R, US_V, US_G = 2, 6, 10, 14

COLS = [("b_ada", 72), ("g", 48), ("cw0", 24), ("cw1", 24), ("cw2", 24), ("cb", 24), ("hyb", 8), ("subg", 1),
        ("fb", 3), ("ffreq", 1), ("lam", 4), ("nmix", 8), ("mup", 15), ("mun", 15), ("w0", 8), ("a0", 8),
        ("kk", 4), ("ka", 4), ("rk", 4), ("lnw", 4), ("lnb", 4), ("nffn", 8), ("nfin", 8), ("sink", 8)]
COL0 = {}
_at = 0
for _n, _c in COLS:
    COL0[_n] = _at
    _at += _c
N_COLS = _at

DENSE = [("ffn1_in", FT + 20), ("ffn1_out", 11), ("z", 12 + 8), ("qk", 8), ("v", 4), ("gates", 8),
         ("hyout", 4), ("daout", 4), ("wo", 4), ("ffn2_in", FT), ("ffn2_out", 11), ("rwkv", 18.5 + 8)]
N_DENSE = int(math.ceil(sum(n for _, n in DENSE)))


def _rot(n, banks=(0, 1, 2, 3)):
    return {b: len(range(i, n, len(banks))) for i, b in enumerate(banks)}


STAGES = [("mlp", {5: 3}), ("lam", {7: 1}), 
          ("ada_head", {7: 2, 6: 2}), ("ffn1_in", {0: 11, 1: 11, 2: 11, 3: 11, 7: 5, 6: 5}),
          ("w4", _rot(8)), ("knorm", {5: 1}), ("ffn1_out", _rot(8)),
          ("kdft", _rot(10)), ("z", {**_rot(24), 7: 2, 6: 2}), ("qk", {**_rot(16), 5: 8, 6: 8}), ("ut", {5: 2, 6: 2}), ("v", _rot(12)),
          ("uspec", {0: 2, 1: 2, 2: 2, 3: 2}), ("v_end", _rot(4)), ("yinv", _rot(8)), ("gates", _rot(16)),
          ("att", {0: 8, 1: 8, 2: 8, 3: 8, 5: 8, 6: 8, 7: 8}), ("onorm", {5: 1, 0: 1, 1: 1, 2: 1, 3: 1}),
          ("daout", _rot(8)), ("wo", _rot(8)),
          ("ffn2_in", {0: 11, 1: 11, 2: 11, 3: 11}), ("ffn2_out", _rot(8)),
          ("shift", _rot(15)), ("lora", {0: 2, 1: 2, 2: 2, 3: 2}), ("kkn", {5: 1, 6: 1}),
          ("aq", _rot(6)), ("toks", {5: 3, 6: 3})]
for _s in range(2):
    STAGES += [(f"am{_s}", {0: 4, 1: 4, 2: 4, 3: 4}), (f"inv{_s}", {0: 12, 3: 12, 1: 12, 5: 12, 2: 12, 6: 12}),
               (f"tail{_s}", {0: 2, 5: 2, 1: 2 - _s, 6: 2 - _s, 2: 1, 3: 1})]
STAGES += [("gates2_start", {7: 3}), ("gn", {0: 1, 1: 1, 2: 1, 3: 1, 5: 2, 6: 2}), ("batt", {0: 4, 1: 4, 5: 4, 6: 4, 7: 4}),
           ("gates2", _rot(13, (2, 3))), ("proja", _rot(8)), ("projr", _rot(8)), ("wout", _rot(8)),
           ("route", {0: 1, 1: 1, 2: 1}), ("htok", {5: 2, 6: 2}), ("gather0", {5: 1, 6: 1}),
           ("moe", {0: 2 * N_GROUPS, 1: 2 * N_GROUPS, 2: 2 * N_GROUPS, 3: 2 * N_GROUPS,
                     5: 3 * N_GROUPS - 1, 6: 3 * N_GROUPS - 1, 7: N_GROUPS})]
FILLS = {}
_n = [0] * 8
for _name, _uses in STAGES:
    FILLS[_name] = list(_n)
    for _b, _c in _uses.items():
        _n[_b] += _c


def constants():
    f32 = np.float32
    out = {}
    t = np.linspace(0.0, 1.0, T, dtype=f32)[:, None]
    w = (f32(2.0 * math.pi) * np.arange(T, dtype=f32)[:, None] / f32(T)).astype(f32)
    f = np.linspace(1e-4, 15, 16, dtype=f32)[None, :]
    z = np.concatenate([t, np.cos(f * w), -np.sin(f * w)], axis=-1).astype(f32)
    out["zT"] = np.ascontiguousarray(z.T)
    deltas = np.linspace(math.log(1e-2) / 1.5, math.log(1e-2) / 0.3, D, dtype=f32)
    decay = np.exp(-t * np.abs(deltas)).astype(f32)
    out["decay"] = decay.reshape(2, P, D).transpose(1, 0, 2).reshape(P, 2 * D).copy()
    tt = np.arange(T)[:, None].astype(np.float64)
    ff = np.arange(T)[None, :].astype(np.float64)
    re = np.cos(2 * np.pi * tt * ff / FFT)
    im = -np.sin(2 * np.pi * tt * ff / FFT)
    last = (-1.0) ** np.arange(T)
    fu = np.concatenate([re, im], axis=1)
    fu[:, T] = last
    out["Fu"] = fu.reshape(2, P, 2 * T).transpose(1, 0, 2).reshape(P, 4 * T).astype(f32)
    alt = re[:, :P].copy()
    alt[:, 0] = last
    fwd = np.concatenate([re, im, alt], axis=1)
    bwd = np.concatenate([re, -im, alt], axis=1)
    bwd[0] = 0.0
    fk = np.concatenate([fwd, bwd], axis=0).reshape(4, P, 5 * P).transpose(1, 0, 2).astype(f32)
    out["FK"] = fk[:, :, :4 * P].reshape(P, 16 * P)
    out["FKalt"] = fk[:, :, 4 * P:].reshape(P, 4 * P)
    inv = np.concatenate([2 * re.T, 2 * im.T], axis=0) / FFT
    inv[0] = 1.0 / FFT
    inv[T] = last / FFT
    out["Finv"] = inv.reshape(4, P, T).transpose(1, 0, 2).reshape(P, 4 * T).astype(f32)
    p = np.arange(P)
    pos = np.arange(T)
    invf = (f32(10000.0) ** (-np.arange(0, 32, 2, dtype=f32) / f32(32))).astype(f32)
    rc = np.where(((p % 64) // 32 == 0)[:, None], (pos // 64)[None, :], (pos % 64)[None, :]).astype(f32)
    ang = (rc * invf[p % 16][:, None]).astype(f32)
    out["rope"] = np.concatenate([np.cos(ang), np.sin(ang)], axis=1).astype(f32)
    eye = np.eye(P, dtype=f32)
    blk = (p[:, None] // 64 == p[None, :] // 64).astype(f32)
    perm = np.zeros((P, P), f32)
    for m in range(P):
        if m % 32 < 16:
            perm[m + 16, m] = -1.0
        else:
            perm[m - 16, m] = 1.0
    nobwd0 = np.ones((P, 1), f32)
    nobwd0[0] = 0.0
    headsel = np.zeros((P, HEADS, HEADS), f32)
    headbc = np.zeros((HEADS, HEADS, P), f32)
    for j in range(HEADS):
        headsel[:, j, j] = 1.0
        headbc[j, j, :] = 1.0
    adasel = np.zeros((P, 4), f32)
    for half in range(2):
        for par in range(2):
            for r in range(2):
                adasel[32 * (2 * half + par) + r, 2 * half + r] = 1.0
    iota = np.broadcast_to(np.arange(1, CAP + 1, dtype=f32), (P, CAP))
    out["small"] = np.concatenate([eye, np.ones((P, P), f32), blk, perm, nobwd0, headsel.reshape(P, 64), iota, adasel], axis=1)
    out["headbc"] = headbc.reshape(HEADS, HEADS * P)
    s, u = p[:, None], p[None, :]
    keep = [np.concatenate([a, b, a, b], axis=1) for a, b in (((s < u), (s <= u)), ((s > u), (s >= u)))]
    lev = []
    for flip in (False, True):
        for lv in range(7):
            m = 1 << lv
            a, b = (u, s) if flip else (s, u)
            lev.append((a // (2 * m) == b // (2 * m)) & (a // m % 2 == 0) & (b // m % 2 == 1))
    q = np.arange(2)[None, :, None] * P + p[:, None, None]
    rel = np.abs(np.arange(T)[None, None, :] - q).astype(np.float64)
    dist = np.where(rel <= 128, -rel, -1e33)
    out["masks"] = np.concatenate([*keep, *lev, dist.reshape(P, 2 * T)], axis=1).astype(f32)
    return out


N_SMALL = 4 * P + 1 + 64 + CAP + 4
N_MASKS = 2 * 4 * P + 14 * P + 2 * T


def blocks(w):
    k, n = w.shape
    return w.reshape(k // P, P, n // P, P).transpose(2, 0, 1, 3)


def slabs(b):
    b = b.reshape(-1, P, P)
    pad = -len(b) % 16
    if pad:
        b = np.concatenate([b, np.zeros((pad, P, P), b.dtype)])
    return b.reshape(-1, 16, P, P).transpose(0, 2, 1, 3).reshape(-1, P, SLAB)


def wide(w, n=256):
    return w.reshape(KD, P, -1, n).transpose(2, 1, 0, 3).reshape(-1, P, KD * n)


def k_pairs(w):
    return w.reshape(KD // 2, 2, P, D).transpose(0, 2, 1, 3).reshape(KD // 2, P, SLAB)


def cols(v):
    return v.reshape(-1, P).T


def pad_rows(v):
    return np.concatenate([v, np.zeros((P - v.shape[0], v.shape[1]), v.dtype)], axis=0)


def lay_out(inp):
    g = {k: np.asarray(v) for k, v in inp.items()}
    ada = np.stack([k_pairs(g["w_ada"][0][:, m * D:m * D + D]) for m in range(N_MOD)])

    def ffn_in(w):
        b = blocks(w)
        return np.stack([b[:FT], b[FT:]], axis=1)

    f1 = ffn_in(g["w_ff_in"][0, 0])
    mixed = []
    for i in range(5):
        for q in range(4):
            mixed += [ada[2 + i][q:q + 1], slabs(f1[4 * i + q:4 * i + q + 1])]
    mixed += [slabs(f1[20:22])]
    w_in = g["w_in"][0]
    zs, late = slabs(blocks(w_in[:, :3 * D])), np.concatenate([ada[7], ada[8]])
    z = [a[i:i + 1] for i in range(12) for a in (zs, late) if i < len(a)]
    w2 = g["w_in_2"][0]
    b2 = blocks(w2)
    order = [h for j in range(4) for h in (j, 4 + j)]
    qcols = np.concatenate([np.arange(1920 + 64 * h, 1920 + 64 * h + 64) for h in order])
    arows = np.concatenate([np.arange(64 * h, 64 * h + 64) for h in order])
    bq = blocks(w2[:, qcols])
    second = np.concatenate([
        *(b2[i:i + 1].reshape(-1, P, P) for i in RW_TILES), bq.reshape(-1, P, P), b2[19:37].reshape(-1, P, P),
        blocks(g["w_proj_attn_2"][0][arows]).reshape(-1, P, P), blocks(g["w_proj_rwkv_2"][0]).reshape(-1, P, P),
        blocks(g["w_out_2"][0]).reshape(-1, P, P)])
    dense = np.concatenate([
        *mixed, slabs(blocks(g["w_ff_out"][0, 0])), *z, slabs(blocks(w_in[:, 3 * D:5 * D])),
        wide(w_in[:, 5 * D:6 * D]), slabs(blocks(w_in[:, 6 * D:])), slabs(blocks(g["w_hy_out"][0])),
        slabs(blocks(g["w_da_out"][0])), slabs(blocks(g["w_o"][0])), slabs(ffn_in(g["w_ff_in"][0, 1])),
        slabs(blocks(g["w_ff_out"][0, 1])), slabs(second)])
    assert dense.shape == (N_DENSE, P, SLAB), dense.shape
    gate, up, down = (np.stack([k_pairs(w) for w in g[n][0]]).reshape(N_GROUPS, GROUP, KD // 2, P, SLAB).swapaxes(1, 2)
                      for n in ("exp_w_gate_2", "exp_w_up_2", "exp_w_down_2"))
    gate_up = np.stack([gate, up], axis=2).reshape(N_GROUPS, -1, P, SLAB)
    experts = np.concatenate([gate_up, down.reshape(N_GROUPS, -1, P, SLAB)], axis=1).reshape(-1, P, SLAB)
    xT = g["x"][0].T.reshape(KD, P, T)
    cT = g["ctx"][0].T.reshape(KD, P, T)
    tokens = np.concatenate([xT, cT], axis=2).transpose(1, 0, 2).reshape(P, KD * 2 * T)
    cond = np.stack([cols(g["c"][0]), cols(g["c_ctx"])], axis=2).reshape(P, KD * 2)

    def mu(v):
        return v.reshape(15, P)[RW_TILES].T

    cw = g["hy_conv_w"][0]
    parts = {
        "b_ada": cols(g["b_ada"][0]), "g": cols(g["norm_g"][0]), "cw0": cols(cw[0]), "cw1": cols(cw[1]),
        "cw2": cols(cw[2]), "cb": cols(g["hy_conv_b"][0]), "hyb": cols(g["hy_bias"][0]), "subg": cols(g["subln_g"][0]),
        "fb": pad_rows(np.stack([g["filt_b1"][0], g["filt_b2"][0], g["filt_b3"][0]], axis=1)),
        "ffreq": pad_rows(g["filt_freq"][0][:, None]),
        "lam": pad_rows(np.stack([g["lambda_q1"][0], g["lambda_q2"][0], g["lambda_k1"][0], g["lambda_k2"][0]], axis=1)),
        "nmix": cols(g["norm_mix_g_2"][0]), "mup": mu(g["mu_prev_2"][0]), "mun": mu(g["mu_next_2"][0]),
        "w0": np.concatenate([cols(g["w0_f_2"][0]), cols(g["w0_b_2"][0])], axis=1),
        "a0": np.concatenate([cols(g["a0_f_2"][0]), cols(g["a0_b_2"][0])], axis=1),
        "kk": cols(g["k_k_2"][0]), "ka": cols(g["k_a_2"][0]), "rk": cols(g["r_k_2"][0].reshape(-1)),
        "lnw": cols(g["ln_x_w_2"][0]), "lnb": cols(g["ln_x_b_2"][0]), "nffn": cols(g["norm_ffn_g_2"][0]),
        "nfin": cols(g["norm_final_g_2"]), "sink": np.broadcast_to(g["attn_sink_2"][0][None, :], (P, HEADS))}
    cc = np.concatenate([parts[n] for n, _ in COLS], axis=1)
    assert cc.shape == (P, N_COLS)
    w1 = np.concatenate([g["filt_w1"][0], np.zeros((64 - 33, 64), np.float32)], axis=0)
    filt = np.concatenate([w1, g["filt_w2"][0], g["filt_w3"][0]], axis=1)
    lora = np.concatenate([
        np.concatenate([g["w_up_f_2"][0], g["w_up_b_2"][0]], axis=0),
        np.concatenate([g["a_up_f_2"][0], g["a_up_b_2"][0]], axis=0), g["g_up_2"][0]], axis=1)
    router = g["w_router_2"][0].reshape(KD, P, N_EXP).transpose(1, 0, 2).reshape(P, KD * N_EXP)
    out = {"ada_head": np.concatenate([ada[0], ada[1]]), "dense": dense, "experts": experts, "tokens": tokens, "cond": cond, "cols": cc, "filt": filt,
           "w4": g["filt_w4"][0], "lora": lora, "router": router}
    out.update(constants())
    return {k: np.ascontiguousarray(v) for k, v in out.items()}


_ARRAYS = ["ada_head", "dense", "experts", "tokens", "cond", "cols", "filt", "w4", "lora", "router", "zT", "decay", "Fu", "FK", "FKalt",
           "Finv", "rope", "small", "headbc", "masks"]


def build(nc, dram, out_dram):
    fp32 = mybir.dt.float32
    ALU = mybir.AluOpType
    ACT = mybir.ActivationFunctionType
    AXX = mybir.AxisListType.X
    mult, add, sub, mx_op, mn_op = ALU.mult, ALU.add, ALU.subtract, ALU.max, ALU.min
    ds = bass.ds

    ctx = ExitStack()
    with ctx:
        def sb(name, shape):
            return ctx.enter_context(nc.sbuf_tensor(name, shape, fp32))

        def sem(name):
            return ctx.enter_context(nc.semaphore(name))

        PAGE = 2048
        N_PAGES = 23
        arena = sb("arena", [P, N_PAGES * PAGE])

        def page(at, words, a=None):
            lo = int(at * PAGE)
            v = arena[:, lo:lo + words]
            return v if a is None else v.rearrange("p (n a) -> p n a", a=a)

        ring = [page(i, SLAB, P) for i in range(RING)]
        ring_wide = [page(i, SLAB, 256) for i in range(RING)]
        ring_flat = [page(i, SLAB) for i in range(RING)]
        head_flat = [page(i, SLAB) for i in (6, 7, 8, 9, 10, 11, 12, 14)]
        EX_PAGES = [*range(11, 23), *range(RING)]
        ex_flat = [page(i, SLAB) for i in EX_PAGES]
        ex_early = [[page(5, SLAB // 2), page(5.5, SLAB // 2)], [page(6, SLAB // 2), page(6.5, SLAB // 2)],
                    [page(4.5, SLAB // 2), page(8.5, SLAB // 2)]]

        col_sb = sb("col_sb", [P, N_COLS])
        small = sb("small", [P, N_SMALL])
        router = sb("router", [P, KD * N_EXP])
        mods = sb("mods", [P, N_MOD * KD * 2])
        cond = sb("cond", [P, KD * 2])
        cond_s = sb("cond_s", [P, KD * 32])
        sil = sb("sil", [P, 2 * 512])
        sq = sb("sq", [P, 2 * 512])
        sd = sb("sd", [P, 512])
        rstd = sb("rstd", [P, 512])
        eps = sb("eps", [P, 2])
        gain = sb("gain", [P, 4 * KD])
        filt = page(20, 3 * 64)[0:64]
        zT = page(20.25, T)[0:33]
        fh = sb("fh", [64, 4 * T])
        tiny = sb("tiny", [P, 64])

        def c(name, j=0, n=1):
            return col_sb[:, COL0[name] + j:COL0[name] + j + n]

        ident = small[:, 0:P]
        ones = small[:, P:2 * P]
        ones2 = fh[0:N_EXP, T:2 * T]
        blk = small[:, 2 * P:3 * P]
        perm = small[:, 3 * P:4 * P]
        nobwd0 = small[:, 4 * P:4 * P + 1]
        headsel = small[:, 4 * P + 1:4 * P + 65].rearrange("p (h m) -> p h m", m=HEADS)
        headbc = page(19, HEADS * P, P)[0:HEADS]
        iota = small[:, 4 * P + 65:N_SMALL - 4]
        adasel = small[:, N_SMALL - 4:N_SMALL]
        ada_rows = sd
        mods_v = mods[:, :].rearrange("p (m j r) -> p m j r", m=N_MOD, r=2)
        cond_v = cond_s[:, :].rearrange("p (k r) -> p k r", r=32)
        sil_v = sil[:, :].rearrange("p (s n) -> p s n", n=512)
        sq_v = sq[:, :].rearrange("p (s n) -> p s n", n=512)
        gain_v = gain[:, :].rearrange("p (s j) -> p s j", j=KD)
        router_v = router[:, :].rearrange("p (k e) -> p k e", e=N_EXP)

        def mod(m, r):
            return mods_v[:, m, :, r]

        def g(i):
            return c("g", 8 * i, 8)

        X = page(4, 4096, 512)
        h1 = page(6, 4096, 512)
        hid1 = page(8, FT * 512, 512)
        y1 = page(14, 4096, 512)
        hfil = page(20, 4096, 1024)
        habs = page(14, 4096, 1024)
        FK = page(22, 16 * P, 4 * P)
        FK_alt = page(13.5, 4 * P, P)
        decay = page(16, 2048, 1024)
        w4 = page(17, 2048)
        Kspec = page(16, 5 * 1024, 1024)
        Fu = page(18.5, 1024, 512)
        Finv = page(19, 1024, 256)
        rope = page(19.5, 512, 256)
        x0 = page(8, 2048, 256)
        u = page(9, 2048, 256)
        zv = page(10, 2048, 256)
        hy = page(10, 2048, 256)
        utok = page(11, 2048, 1024)
        yc = page(11, 2048, 256)
        Y = page(12, 4096, 1024)
        q_sb = page(22, 2048, 256)
        kT = page(20, 4096, 512)
        vtok = page(14, 4096, 1024)
        gates = page(12, 4096, 256)
        prob = page(8, 4096, 512)
        pT = page(16, 2048, 256)
        osq = page(17, 2048, 256)
        oT = page(11, 2048, 256)
        mix = page(18, 2048, 256)
        y2 = page(19, 2048, 256)
        x = page(7, 2048, 256)
        h = page(6, 2048, 256)
        hid2 = page(8, FT * 256, 256)
        y3 = page(15, 2048, 256)
        masks = page(13, N_MASKS)
        lora = page(17, 1024)
        g_up = page(13 + N_MASKS / PAGE, 512)
        keep = masks[:, 0:1024].rearrange("p (d n) -> p d n", n=512)
        level = masks[:, 1024:1024 + 14 * P].rearrange("p (l n) -> p l n", n=P)
        dist = masks[:, 1024 + 14 * P:N_MASKS].rearrange("p (q n) -> p q n", n=T)
        US = page(8, 15 * 256, 256)
        sig = page(10, 2048, 128)
        iclr = page(11, 2048, 256)
        cum = page(12, 2048, 128)
        D1 = page(15, 2048, 128)
        D2 = page(16, 2048, 128)
        Eneg = page(19, 2048, 128)
        Einc = page(20, 2048, 128)
        Eexc = page(21, 2048, 128)
        kkn = page(22, 1024, 128)
        kkr = page(22.5, 1024, 256)
        kdir = page(4, 2048, 128)
        nrm = page(5, 1024)
        gsq_kk = page(5.5, 1024)
        kkr_flat = page(22.5, 1024)
        kkn256 = page(22, 1024, 256)
        sig256 = page(10, 2048, 256)
        iclr128 = page(11, 2048, 128)
        QQw = page(15, 4096, 256)
        QQ = page(15, 4096, 128)
        KT = page(17, 2048, 128)
        BT = page(18, 2048, 128)
        AM = page(19, 8192, 512)
        XT = page(4, 2048, 128)
        Vtok = page(5, 1024, 512)
        wkv = page(5.5, 1024, 256)
        Xw = page(10, 1024, 128)
        NL = page(10.5, 1024, 128)
        Pw = page(11, 1024, 128)
        Wsb = [page(11.5, 512, 64), page(11, 512, 64)]
        nU = [page(11.75, 512, 64), page(11.25, 512, 64)]
        toks = page(12, 2048, 512)
        rkk = US[:, US_K:US_K + 4, :]
        gsq = page(19, 1024)
        dev = page(19.5, 1024)
        g_out = page(21.5, 1024)
        gsd = page(22, 1024)
        bonus = page(22.5, 1024)
        yr = page(4, 1024, 256)
        qa = sil[:, :].rearrange("p (n a) -> p n a", a=256)
        ka = sq[:, 512:768]
        va = sq[:, 768:1024].rearrange("p (n a) -> p n a", a=128)
        oa = page(16, 1024, 256)
        gates2 = page(17, 4096, 256)
        bs = page(20, 1024, 256)
        bp = page(20.5, 1024, 256)
        bpT = page(21, 1024, 256)
        mix2 = page(8, 2048, 256)
        htok = page(9, 2048, 1024)
        OH = page(10, 1024, 512)
        OHW = page(8, 1024, 512)
        OHW_g = page(10.5, 256, P)
        OHT = page(10.625, 256)
        xg = page(4, 1024, P)
        msil = page(4.5, 1024)
        hid = page(5, 1024)
        hidT = page(5.5, 1024, P)
        ys4 = page(8.5, 1024)
        outb = page(8, 2048, 256)
        state_v = sq[:, 0:512].rearrange("p (d j n) -> p d j n", d=2, n=64)
        scl = sb("scl", [P, 8])
        raw = sil[:, 0:512]
        rt = sil[:, 512:1024]
        raw_v = raw[:, :].rearrange("p (s n) -> p s n", n=256)

        ps = [ctx.enter_context(nc.psum_tensor(f"bank{i}", [P, 512], fp32)) for i in range(8)]

        slab_loaded = [sem(f"slab_loaded{i}") for i in range(RING)]
        slab_started = sem("slab_started")
        ex_loaded = [sem(f"ex_loaded{i}") for i in range(EX_RING)]
        ex_early_in = [sem(f"ex_early_in{i}") for i in range(EX_EARLY)]
        ex_started = sem("ex_started")
        full = [sem(f"full{i}") for i in range(8)]
        evac = [sem(f"evac{i}") for i in range(8)]
        head_in = [sem(f"head_in{k}") for k in range(2)]
        consts_in = sem("consts_in")
        filters_in = sem("filters_in")
        tokens_in = sem("tokens_in")
        decay_in = sem("decay_in")
        spectra_in = sem("spectra_in")
        masks_in = sem("masks_in")
        eps_set = sem("eps_set")
        cond_zero = sem("cond_zero")
        cond_ready = sem("cond_ready")
        sq_ready = sem("sq_ready")
        acc_ready = sem("acc_ready")
        sq_used = sem("sq_used")
        h_ready = sem("h_ready")
        x_ready = sem("x_ready")
        group_choice = sem("group_choice")
        dve_step = sem("dve_step")
        act_step = sem("act_step")
        router_in = sem("router_in")
        headbc_in = sem("headbc_in")
        kn_ready = sem("kn_ready")
        mu_ready = sem("mu_ready")
        es_ready = sem("es_ready")
        arg_ready = sem("arg_ready")
        sin_ready = sem("sin_ready")
        prod_ready = sem("prod_ready")
        habs_ready = sem("habs_ready")
        z_scaled = sem("z_scaled")
        u_ready = sem("u_ready")
        y_ready = sem("y_ready")
        hy_ready = sem("hy_ready")
        nm_ready = sem("nm_ready")
        p_ready = sem("p_ready")
        osq_ready = sem("osq_ready")
        hr_ready = sem("hr_ready")
        mix_ready = sem("mix_ready")
        us_scaled = sem("us_scaled")
        act_us = sem("act_us")
        kkr_ready = sem("kkr_ready")
        kksq_ready = sem("kksq_ready")
        ss_ready = sem("ss_ready")
        nrm_ready = sem("nrm_ready")
        logs_ready = sem("logs_ready")
        exps_ready = sem("exps_ready")
        qq_ready = sem("qq_ready")
        am_zero = sem("am_zero")
        x_init = sem("x_init")
        nl_ready = sem("nl_ready")
        gsq_ready = sem("gsq_ready")
        g_ready = sem("g_ready")
        gates_ready = sem("gates_ready")
        yr_ready = sem("yr_ready")
        aexp = sem("aexp")
        slot_ready = sem("slot_ready")
        oh_ready = sem("oh_ready")
        out_ready = sem("out_ready")
        out_stored = sem("out_stored")

        block = ctx.enter_context(nc.Block())

        def norm_fill(r):
            return r + (KD if r >= 3 else 0)

        SCATTER = (2, 3, 5, 6)

        def take(pe, stage, b, k):
            v = FILLS[stage][b] + k
            if not (isinstance(v, int) and v == 0):
                pe.wait_ge(evac[b], v)

        def got(eng, stage, b, k):
            eng.wait_ge(full[b], FILLS[stage][b] + k + 1)

        def evacuated(eng, stage, b, k):
            eng.wait_ge(evac[b], FILLS[stage][b] + k + 1)

        class Steps:

            def __init__(self, eng, s):
                self.eng, self.s, self.n = eng, s, 0

            def do(self, ins):
                self.n += 1
                ins.then_inc(self.s, 1)

            def settle(self):
                self.eng.wait_ge(self.s, self.n)

        class Stream:

            def __init__(self, eng, loaded, started, slots, n):
                self.eng, self.loaded, self.started, self.slots, self.n = eng, loaded, started, slots, n
                self.slab, self.at, self.turn = 0, 0, 0

            def block(self):
                first = self.at == 0
                if first:
                    s = self.slab % self.n
                    self.eng.wait_ge(self.loaded[s], 16 * (self.slab // self.n + 1) + self.turn)
                blk_ap = self.slots[self.slab % self.n][:, self.at, :]
                self.at = (self.at + 1) % 16
                if self.at == 0:
                    self.slab += 1
                return blk_ap, first

            def whole(self, slots):
                assert self.at == 0
                s = self.slab % self.n
                self.eng.wait_ge(self.loaded[s], 16 * (self.slab // self.n + 1) + self.turn)
                self.slab += 1
                return slots[s]

            def loop(self, i, per):
                assert self.at == 0 and per % self.n == 0
                self.turn = i * (16 * per // self.n)

            def end_loop(self, per, turns):
                self.turn = 0
                self.slab += per * (turns - 1)

        def scatter_fills(i, last):
            k = i * 3 + (1 if last else 2)
            return (2, i * 2 + 1), (3, i * 2 + 1), (5, k), (6, k)

        @block.sync
        def _(sp):
            sp.dma_start(cond[:, :], dram["cond"]).then_inc(consts_in, 16)
            sp.dma_start(col_sb[:, :], dram["cols"]).then_inc(consts_in, 16)
            sp.dma_start(small[:, :], dram["small"]).then_inc(consts_in, 16)
            for j in range(KD):
                sp.dma_start(head_flat[j], dram["ada_head"][j]).then_inc(head_in[j // 4], 16)
            for j in range(RING):
                sp.dma_start(ring_flat[j], dram["dense"][j]).then_inc(slab_loaded[j], 16)
            with sp.Fori(1, N_DENSE // RING) as i:
                for j in range(RING):
                    sp.wait_ge(slab_started, i * RING + (j - RING + 2))
                    sp.dma_start(ring_flat[j], dram["dense"][ds(i * RING + j, 1), :, :].rearrange("s p n -> (s p) n"))\
                        .then_inc(slab_loaded[j], 16)
            for m in range(N_DENSE - N_DENSE % RING, N_DENSE):
                sp.wait_ge(slab_started, m - RING + 2)
                sp.dma_start(ring_flat[m % RING], dram["dense"][m]).then_inc(slab_loaded[m % RING], 16)
            sp.wait_ge(mix_ready, 2)
            def early(s):
                for par in range(2):
                    sp.dma_start(ex_early[s][par], dram["experts"][s][:, par * D:par * D + D]).then_inc(ex_early_in[s], 16)
            early(0)
            for j in range(EX_RING):
                if j == EX_RING - RING:
                    sp.wait_ge(h_ready, 5 * KD)
                elif j == EX_RING - RING // 2:
                    early(2)
                    for half in range(2):
                        got(sp, "htok", 5 + half, 1)
                    early(1)
                sp.dma_start(ex_flat[j], dram["experts"][EX_EARLY + j]).then_inc(ex_loaded[j], 16)

            def ring_slab(i, j, slab):
                sp.wait_ge(ex_started, i * EX_RING + ((j + EX_EARLY) // GROUP * GROUP - EX_RING + 2 * GROUP))
                sp.dma_start(ex_flat[j], slab).then_inc(ex_loaded[j], 16)
            rounds, rest = divmod(12 * N_EXP - EX_EARLY, EX_RING)
            with sp.Fori(1, rounds) as i:
                for j in range(EX_RING):
                    ring_slab(i, j, dram["experts"][ds(i * EX_RING + EX_EARLY + j, 1), :, :].rearrange("s p n -> (s p) n"))
            for j in range(rest):
                ring_slab(rounds, j, dram["experts"][rounds * EX_RING + EX_EARLY + j])
            for q_ in range(4):
                sp.wait_ge(out_ready, q_ + 1)
                sp.dma_start(out_dram[:, 512 * q_:512 * q_ + 512], page(8 + q_ / 4, 512)).then_inc(out_stored, 16)
            sp.wait_ge(out_stored, 64)

        @block.gpsimd
        def _(pool):
            nc.gpsimd.memset(cond_s[:, :], 0.0).then_inc(cond_zero, 1)
            nc.gpsimd.memset(eps[:, 0:1], EPS).then_inc(eps_set, 1)
            nc.gpsimd.memset(eps[:, 1:2], LNX_EPS).then_inc(eps_set, 1)
            pool.wait_ge(qq_ready, 1)
            nc.gpsimd.memset(page(19, 8192), 0.0).then_inc(am_zero, 1)
            for s in range(2):
                for pair in range(2):
                    for lv in range(7):
                        for d in range(2):
                            if lv == 0:
                                for b in range(4):
                                    evacuated(pool, f"am{s}", b, 2 * d + 1)
                                if s or pair:
                                    got(pool, f"inv{s if pair else 0}", 3 * d, 5 if pair else 11)
                            elif lv == 1:
                                got(pool, f"inv{s}", (1, 5)[d], 6 * pair)
                                pool.wait_ge(x_init, (s * 2 + pair) * 2 + d + 1)
                            else:
                                got(pool, f"inv{s}", 3 * d, 6 * pair + lv - 2)
                            u0 = 8 * d + 4 * pair
                            nc.gpsimd.tensor_tensor(NL[:, 4 * d:4 * d + 4, :], AM[:, u0:u0 + 4, 0:P],
                                                    level[:, 7 * d + lv:7 * d + lv + 1, :].to_broadcast([P, 4, P]), mult)\
                                .then_inc(nl_ready, 1)

        @block.tensor
        def _(pe):
            mm = nc.tensor.matmul
            st = Stream(pe, slab_loaded, slab_started, ring, RING)

            def product(out, k_tiles, rhs, last_sem=None, norm=None):
                for k in range(k_tiles):
                    if norm is not None:
                        pe.wait_ge(h_ready, KD * norm + k + 1)
                    w, first = st.block()
                    ins = mm(out, lhsT=w, rhs=rhs(k), start=k == 0, stop=k == k_tiles - 1)
                    if first:
                        ins.then_inc(slab_started, 1)
                if last_sem is not None:
                    ins.then_inc(last_sem, 1)

            def stat(r, j, n):
                pe.wait_ge(sq_ready, 8 * r + j + 1)
                if j == 0 and r > 0:
                    pe.wait_ge(evac[4], norm_fill(r))
                mm(ps[4][:, 0:n], lhsT=ones, rhs=sq_v[:, j % 2, 0:n], start=j == 0, stop=j == 7)\
                    .then_inc(sq_used if j < 7 else full[4], 1)

            def stat_of_sum(r, n):
                pe.wait_ge(acc_ready, (r + 1) // 2)
                pe.wait_ge(evac[4], norm_fill(r))
                mm(ps[4][:, 0:n], lhsT=ones, rhs=rstd[:, 0:n], start=True, stop=True).then_inc(full[4], 1)

            def tiles(stage, count, k_tiles, rhs, n=T, after=None, norm=None):
                for t in range(count):
                    b = t % 4
                    take(pe, stage, b, t // 4)
                    product(ps[b][:, 0:n], k_tiles, rhs, full[b], norm if t == 0 else None)
                    if after:
                        after(t)

            def ada_sums(stage, k, kp):
                if kp == 0:
                    take(pe, stage, 7, k)
                head = stage == "ada_head"
                if head and kp == 0:
                    pe.wait_ge(head_in[k], 64)
                slab = head_flat[4 * k + kp] if head else st.whole(ring_flat)
                for q_ in range(4):
                    half, par = q_ // 2, q_ % 2
                    ins = mm(ps[7][32 * q_:32 * q_ + 32, :], lhsT=cond_v[:, 2 * kp + par, :],
                             rhs=slab[:, par * D + half * 512:par * D + half * 512 + 512],
                             start=kp == 0, stop=kp == KD // 2 - 1)
                    if q_ == 0 and not head:
                        ins.then_inc(slab_started, 1)
                if kp == KD // 2 - 1:
                    ins.then_inc(full[7], 1)

            def ada_columns(stage, k, k_rows):
                evacuated(pe, stage, 7, k_rows)
                take(pe, stage, 6, k)
                for j in range(4):
                    ins = mm(ps[6][:, 4 * j:4 * j + 4], lhsT=ada_rows[:, j * P:j * P + P], rhs=adasel,
                             start=True, stop=True)
                ins.then_inc(full[6], 1)

            pe.wait_ge(filters_in, 32)
            for n in range(3):
                take(pe, "mlp", 5, n)
                if n == 0:
                    mm(ps[5][0:64, 0:T], lhsT=filt[0:33, 0:64], rhs=zT[0:33, :], start=True, stop=True)\
                        .then_inc(full[5], 1)
                else:
                    pe.wait_ge(sin_ready, n)
                    mm(ps[5][0:64, 0:T], lhsT=filt[:, 64 * n:64 * n + 64], rhs=fh[:, 0:T], start=True, stop=True)\
                        .then_inc(full[5], 1)
            pe.wait_ge(consts_in, 48)
            pe.wait_ge(prod_ready, 1)
            mm(ps[7][:, 0:2], lhsT=ones[0:64, :], rhs=tiny[0:64, 0:2], start=True, stop=True).then_inc(full[7], 1)
            pe.wait_ge(cond_ready, 1)
            for kp in range(KD // 2):
                ada_sums("ada_head", 0, kp)
            for j in range(KD):
                if j == KD // 2:
                    ada_columns("ada_head", 0, 0)
                stat(0, j, 512)
            for kp in range(KD // 2):
                ada_sums("ada_head", 1, kp)
            ada_columns("ada_head", 1, 1)

            def filter_in_time():
                pe.wait_ge(sin_ready, 3)
                pe.wait_ge(decay_in, 32)
                for n in range(8):
                    tt, qq = n % 2, n // 2
                    take(pe, "w4", n % 4, n // 4)
                    mm(ps[n % 4][:, :], lhsT=fh[:, tt * P:tt * P + P], rhs=w4[0:64, qq * 512:qq * 512 + 512],
                       start=True, stop=True).then_inc(full[n % 4], 1)
                pe.wait_ge(habs_ready, 8)
                take(pe, "knorm", 5, 0)
                for ct in range(KD):
                    for kt in range(4):
                        ins = mm(ps[5][:, ct:ct + 1], lhsT=habs[:, kt, ct * P:ct * P + P],
                                 rhs=nobwd0 if kt == 2 else ones[:, 0:1], start=kt == 0, stop=kt == 3)
                ins.then_inc(full[5], 1)

            def filter_spectrum(tiles_):
                for n in tiles_:
                    take(pe, "kdft", n % 4, n // 4)
                    for kt in range(4):
                        part = FK_alt[:, kt, :] if n // 2 == 4 else FK[:, kt, (n // 2) * P:(n // 2) * P + P]
                        ins = mm(ps[n % 4][:, :], lhsT=part, rhs=hfil[:, kt, (n % 2) * 512:(n % 2) * 512 + 512],
                                 start=kt == 0, stop=kt == 3)
                    ins.then_inc(full[n % 4], 1)

            def ffn(stage, r, src, hid, n, with_ada, norm, between=None):
                def pair(q_, use):
                    for b in (2 * (q_ % 2), 2 * (q_ % 2) + 1):
                        take(pe, stage + "_in", b, use)
                        product(ps[b][:, 0:n], KD, lambda k: src[:, k, 0:n], full[b], norm if b == 0 else None)
                per = 8 if with_ada else 4
                with pe.Fori(0, 5) as i:
                    st.loop(i, per)
                    for q_ in range(4):
                        if with_ada:
                            ada_sums(stage + "_in", i, q_)
                        pair(q_, i * 2 + q_ // 2)
                    if with_ada:
                        ada_columns(stage + "_in", i, i)
                st.end_loop(per, 5)
                pair(0, 10)
                pair(1, 10)
                if between:
                    between()
                evacuated(pe, stage + "_in", 1, 10)
                evacuated(pe, stage + "_in", 3, 10)
                tiles(stage + "_out", KD, FT, lambda k: hid[:, k, 0:n], n)
                stat_of_sum(r, n)

            ffn("ffn1", 1, h1, hid1, 512, True, 0, filter_in_time)
            pe.wait_ge(spectra_in, 16 * 5)
            filter_spectrum(range(4))
            for j in range(KD):
                stat(2, j, 512)
            filter_spectrum(range(4, 10))

            def late_ada(t):
                if t % 2 and t < 16:
                    ada_sums("z", t // 8, t // 2 % 4)
                if t in (9, 17):
                    ada_columns("z", t // 16, t // 16)
            tiles("z", 24, KD, lambda k: h1[:, k, 0:T], T, late_ada, 1)

            def rotate(n):
                evacuated(pe, "qk", n % 4, n // 4)
                take(pe, "qk", 5 + n % 2, n // 2)
                mm(ps[5 + n % 2][:, 0:T], lhsT=perm, rhs=raw_v[:, n % 2, :], start=True, stop=True)\
                    .then_inc(full[5 + n % 2], 1)
            for n in range(16):
                w_n = T if n < 8 else 512
                take(pe, "qk", n % 4, n // 4)
                product(ps[n % 4][:, 0:w_n], KD, lambda k: h1[:, k, 0:w_n], full[n % 4])
                if n:
                    rotate(n - 1)
            rotate(15)
            pe.wait_ge(u_ready, 8)
            for n in range(4):
                kt, half = n // 2, n % 2
                take(pe, "ut", 5 + half, n // 2)
                for q_ in range(4):
                    ins = nc.tensor.transpose(ps[5 + half][:, q_ * P:q_ * P + P],
                                              u[:, half * 4 + q_, kt * P:kt * P + P], ident)
                ins.then_inc(full[5 + half], 1)
            def values(stage, s):
                slot = st.slab % RING
                pe.wait_ge(slab_loaded[slot], 16 * (st.slab // RING + 1))
                for tt in range(4):
                    take(pe, stage, tt, s)
                    for k in range(KD):
                        ins = mm(ps[tt][:, 0:256], lhsT=h1[:, k, tt * P:tt * P + P], rhs=ring_wide[slot][:, k, :],
                                 start=k == 0, stop=k == KD - 1)
                        if tt == 0 and k == 0:
                            ins.then_inc(slab_started, 1)
                    ins.then_inc(full[tt], 1)
                st.slab += 1
            for s in range(3):
                values("v", s)
            evacuated(pe, "ut", 5, 1)
            evacuated(pe, "ut", 6, 1)
            for i in range(4):
                j, half = i // 2, i % 2
                for im in range(2):
                    b = 2 * half + im
                    take(pe, "uspec", b, j)
                    for kt in range(2):
                        ins = mm(ps[b][:, :], lhsT=Fu[:, kt, im * T + j * P:im * T + j * P + P],
                                 rhs=utok[:, kt, half * 512:half * 512 + 512], start=kt == 0, stop=kt == 1)
                    ins.then_inc(full[b], 1)
            values("v_end", 0)
            pe.wait_ge(y_ready, 4)
            for ct in range(KD):
                take(pe, "yinv", ct % 4, ct // 4)
                for f in range(4):
                    ins = mm(ps[ct % 4][:, 0:T], lhsT=Y[:, f, ct * P:ct * P + P], rhs=Finv[:, f, :],
                             start=f == 0, stop=f == 3)
                ins.then_inc(full[ct % 4], 1)
            tiles("gates", 16, KD, lambda k: h1[:, k, 0:T])

            def scores(hd):
                for qb in range(2):
                    for m in range(2):
                        b = 2 * m + qb
                        take(pe, "att", b, hd)
                        mm(ps[b][:, :], lhsT=q_sb[64 * m:64 * m + 64, hd, qb * P:qb * P + P],
                           rhs=kT[64 * m:64 * m + 64, hd, :], start=True, stop=True).then_inc(full[b], 1)

            def hyena_out(ks):
                for k in ks:
                    w, first = st.block()
                    ins = mm(ps[4][:, 0:T], lhsT=w, rhs=hy[:, k, :], start=k == 0, stop=k == KD - 1)
                    if first:
                        ins.then_inc(slab_started, 1)
                return ins
            evacuated(pe, "qk", 5, 7)
            evacuated(pe, "qk", 6, 7)
            for b in range(4):
                evacuated(pe, "v_end", b, 0)
            scores(0)
            for hd in range(HEADS):
                if hd + 1 < HEADS:
                    scores(hd + 1)
                if hd == 0:
                    pe.wait_ge(hy_ready, 1)
                pe.wait_ge(evac[4], 3 + hd)
                hyena_out(range(5))
                pe.wait_ge(p_ready, hd + 1)
                for qb in range(2):
                    take(pe, "att", 5 + qb, hd)
                    for kt in range(4):
                        ins = nc.tensor.transpose(ps[5 + qb][:, kt * P:kt * P + P],
                                                  prob[:, 4 * (hd % 2) + qb, kt * P:kt * P + P], ident)
                    ins.then_inc(full[5 + qb], 1)
                hyena_out(range(5, KD)).then_inc(full[4], 1)
                evacuated(pe, "att", 5, hd)
                evacuated(pe, "att", 6, hd)
                take(pe, "att", 7, hd)
                for kt in range(4):
                    ins = mm(ps[7][:, 0:T], lhsT=vtok[:, kt, hd * P:hd * P + P], rhs=pT[:, 4 * (hd % 2) + kt, :],
                             start=kt == 0, stop=kt == 3)
                ins.then_inc(full[7], 1)
            pe.wait_ge(osq_ready, 8)
            take(pe, "onorm", 5, 0)
            for j in range(HEADS):
                ins = mm(ps[5][0:HEADS, 0:T], lhsT=headsel[:, j, :], rhs=osq[:, j, :], start=j == 0, stop=j == 7)
            ins.then_inc(full[5], 1)
            pe.wait_ge(hr_ready, 1)
            pe.wait_ge(headbc_in, 16)
            for j in range(HEADS):
                b = j // 2
                if j % 2 == 0:
                    take(pe, "onorm", b, 0)
                ins = mm(ps[b][:, (j % 2) * T:(j % 2) * T + T], lhsT=headbc[:, j, :], rhs=fh[0:HEADS, 0:T],
                         start=True, stop=True)
                if j % 2:
                    ins.then_inc(full[b], 1)
            for b in range(4):
                evacuated(pe, "onorm", b, 0)
            tiles("daout", KD, KD, lambda k: oT[:, k, :])
            pe.wait_ge(mix_ready, 1)
            tiles("wo", KD, KD, lambda k: mix[:, k, :])
            stat_of_sum(3, T)
            for j in range(KD):
                stat(4, j, T)
            ffn("ffn2", 5, h, hid2, T, False, 2)
            for j in range(KD):
                stat(6, j, T)

            tiles("shift", 15, KD, lambda k: h[:, k, :], norm=3)
            pe.wait_ge(masks_in, 48)
            evacuated(pe, "shift", 1, 0)
            for which in range(2):
                if which == 0:
                    pe.wait_ge(act_us, 1)
                for half in range(2):
                    for d in range(2):
                        b = 2 * d + half
                        take(pe, "lora", b, which)
                        for q_ in range(2):
                            j = 2 * half + q_
                            ins = mm(ps[b][:, q_ * T:q_ * T + T],
                                     lhsT=lora[64 * d:64 * d + 64, which * 512 + j * P:which * 512 + j * P + P],
                                     rhs=US[64 * d:64 * d + 64, which, :], start=True, stop=True)
                        ins.then_inc(full[b], 1)
            pe.wait_ge(kksq_ready, 1)
            for i in range(2):
                take(pe, "kkn", 5 + i, 0)
                mm(ps[5 + i][:, :], lhsT=blk, rhs=gsq_kk[:, i * 512:i * 512 + 512], start=True, stop=True)\
                    .then_inc(full[5 + i], 1)
            tiles("aq", 5, KD, lambda k: h[:, k, :])
            bl = [st.block() for _ in range(KD)]
            take(pe, "aq", 1, 1)
            for tt in range(2):
                for k in range(KD):
                    ins = mm(ps[1][:, tt * P:tt * P + P], lhsT=h[:, k, tt * P:tt * P + P], rhs=bl[k][0],
                             start=k == 0, stop=k == KD - 1)
                    if tt == 0 and bl[k][1]:
                        ins.then_inc(slab_started, 1)
            ins.then_inc(full[1], 1)

            def to_tokens(b, k, src):
                take(pe, "toks", b, k)
                for j in range(4):
                    ins = nc.tensor.transpose(ps[b][:, j * P:j * P + P], src(j), ident)
                ins.then_inc(full[b], 1)
            evacuated(pe, "shift", 1, 3)
            for ch in range(2):
                to_tokens(5 + ch, 0, lambda j: US[:, US_V + j, ch * P:ch * P + P])
            pe.wait_ge(qq_ready, 1)
            for d in range(2):
                to_tokens(5, 1 + d, lambda j: KT[:, 8 * d + 2 * j + d, :])
                to_tokens(6, 1 + d, lambda j: BT[:, 8 * d + 2 * j + d, :])

            def gate2(t):
                b = 7 if t < 3 else 2 + (t - 3) % 2
                if t < 3:
                    take(pe, "gates2_start", b, t)
                else:
                    take(pe, "gates2", b, (t - 3) // 2)
                product(ps[b][:, 0:T], KD, lambda k: h[:, k, :], full[b])

            for s in range(2):
                for d in range(2):
                    ch = d if s == 0 else 1 - d
                    for j in range(4):
                        row = 8 * d + 2 * j + ch
                        for half, keys in enumerate((BT, KT)):
                            for par in range(2):
                                b, r0 = 2 * (j % 2) + par, 64 * par
                                if half == 0:
                                    take(pe, f"am{s}", b, 2 * d + j // 2)
                                ins = mm(ps[b][:, half * T:half * T + T], lhsT=keys[r0:r0 + 64, row, :],
                                         rhs=QQw[r0:r0 + 64, row, :], start=True, stop=True)
                                if half:
                                    ins.then_inc(full[b], 1)
                for pair in range(2):
                    for d in range(2):
                        bx = (1, 5)[d]
                        pe.wait_ge(nl_ready, (s * 2 + pair) * 14 + d + 1)
                        take(pe, f"inv{s}", bx, 6 * pair)
                        for i in range(4):
                            ins = nc.tensor.transpose(ps[bx][:, i * P:i * P + P], NL[:, 4 * d + i, :], ident)
                        ins.then_inc(full[bx], 1)
                    for lv in range(1, 7):
                        use = pair * 6 + lv - 1
                        for d in range(2):
                            b = 3 * d
                            pe.wait_ge(nl_ready, (s * 2 + pair) * 14 + lv * 2 + d + 1)
                            evacuated(pe, f"inv{s}", (1, 5)[d], use)
                            take(pe, f"inv{s}", b, use)
                            for i in range(4):
                                ins = mm(ps[b][:, i * P:i * P + P], lhsT=NL[:, 4 * d + i, :], rhs=Xw[:, 4 * d + i, :],
                                         start=True, stop=True)
                            ins.then_inc(full[b], 1)
                        for d in range(2):
                            b, bx, bt = 3 * d, (1, 5)[d], (2, 6)[d]
                            u0 = 8 * d + 4 * pair
                            evacuated(pe, f"inv{s}", b, use)
                            if lv == 1:
                                pe.wait_ge(x_init, (s * 2 + pair) * 2 + d + 1)
                            else:
                                evacuated(pe, f"inv{s}", bt, use - 1)
                            if lv < 6:
                                take(pe, f"inv{s}", bx, use + 1)
                                for i in range(4):
                                    ins = mm(ps[bx][:, i * P:i * P + P], lhsT=XT[:, u0 + i, :], rhs=Pw[:, 4 * d + i, :],
                                             start=True, stop=True)
                                ins.then_inc(full[bx], 1)
                            take(pe, f"inv{s}", bt, use)
                            for i in range(4):
                                ins = mm(ps[bt][:, i * P:i * P + P], lhsT=Pw[:, 4 * d + i, :], rhs=XT[:, u0 + i, :],
                                         start=True, stop=True)
                            ins.then_inc(full[bt], 1)
                if s:
                    gate2(0)
                for d in range(2):
                    ch = d if s == 0 else 1 - d
                    if s == 0:
                        evacuated(pe, "toks", 5, 2)
                        evacuated(pe, "toks", 6, 2)
                    else:
                        evacuated(pe, "tail0", (1, 6)[d], 1)
                    for par in range(2):
                        b = 5 * d + par
                        take(pe, f"tail{s}", b, 0)
                        for j in range(4):
                            hd = 2 * j + par
                            row = 8 * d + 2 * j + ch
                            o = ps[b][:, 64 * j:64 * j + 64]
                            ins = mm(o, lhsT=AM[:, 8 * d + hd, 256:384], rhs=Vtok[:, ch, 64 * hd:64 * hd + 64],
                                     start=True, stop=s == 0)
                            if s:
                                ins = mm(o, lhsT=QQ[64 * par:64 * par + 64, 2 * row, :],
                                         rhs=state_v[64 * par:64 * par + 64, d, j, :], start=False, stop=True)
                        ins.then_inc(full[b], 1)
                if s:
                    gate2(1)
                for d in range(2):
                    evacuated(pe, f"tail{s}", 5 * d, 0)
                    evacuated(pe, f"tail{s}", 5 * d + 1, 0)
                    evacuated(pe, f"inv{s}", (2, 6)[d], 11)
                    take(pe, f"tail{s}", 2 + d, 0)
                    for hd in range(HEADS):
                        ins = mm(ps[2 + d][:, 64 * hd:64 * hd + 64], lhsT=XT[:, 8 * d + hd, :], rhs=Wsb[d][:, hd, :],
                                 start=True, stop=True)
                    ins.then_inc(full[2 + d], 1)
                if s:
                    gate2(2)
                for d in range(2):
                    ch = d if s == 0 else 1 - d
                    evacuated(pe, f"tail{s}", 2 + d, 0)
                    take(pe, f"tail{s}", 5 * d, 1)
                    for j in range(4):
                        for par in range(2):
                            hd = 2 * j + par
                            row = 8 * d + 2 * j + ch
                            o = ps[5 * d][64 * par:64 * par + 64, j * P:j * P + P]
                            mm(o, lhsT=Vtok[:, ch, 64 * hd:64 * hd + 64], rhs=AM[:, 8 * d + hd, 384:512],
                               start=True, stop=False)
                            ins = mm(o, lhsT=nU[d][:, hd, :], rhs=AM[:, 8 * d + hd, 128:256], start=False, stop=s == 0)
                            if s:
                                ins = mm(o, lhsT=state_v[64 * par:64 * par + 64, d, j, :],
                                         rhs=QQ[64 * par:64 * par + 64, 2 * row + 1, :], start=False, stop=True)
                    ins.then_inc(full[5 * d], 1)
                    if s == 0:
                        b = 5 * d + 1
                        take(pe, "tail0", b, 1)
                        for j in range(4):
                            for par in range(2):
                                hd = 2 * j + par
                                o = ps[b][64 * par:64 * par + 64, 64 * j:64 * j + 64]
                                mm(o, lhsT=toks[:, 2 * d, 64 * hd:64 * hd + 64],
                                   rhs=Vtok[:, ch, 64 * hd:64 * hd + 64], start=True, stop=False)
                                ins = mm(o, lhsT=toks[:, 2 * d + 1, 64 * hd:64 * hd + 64], rhs=nU[d][:, hd, :],
                                         start=False, stop=True)
                        ins.then_inc(full[b], 1)
            def band_scores(n):
                j, par = n // 2, n % 2
                b = n % 2
                take(pe, "batt", b, n // 2)
                for qb in range(2):
                    ins = mm(ps[b][:, qb * T:qb * T + T], lhsT=qa[64 * par:64 * par + 64, j, qb * P:qb * P + P],
                             rhs=ka[64 * par:64 * par + 64, :], start=True, stop=True)
                ins.then_inc(full[b], 1)
            pe.wait_ge(g_ready, 1)
            for i in range(2):
                take(pe, "gn", 2 + i, 0)
                for q_ in range(2):
                    j = 2 * i + q_
                    ins = mm(ps[2 + i][:, q_ * T:q_ * T + T], lhsT=g_up[:, j * P:j * P + P],
                             rhs=US[:, US_G, :], start=True, stop=True)
                ins.then_inc(full[2 + i], 1)
            evacuated(pe, "tail1", 0, 1)
            evacuated(pe, "tail1", 5, 1)
            for i in range(2):
                take(pe, "gn", i, 0)
                mm(ps[i][:, :], lhsT=blk, rhs=page(5.5 + 0.25 * i, 512), start=True, stop=True).then_inc(full[i], 1)
            for i in range(2):
                take(pe, "gn", 5 + i, 0)
                mm(ps[5 + i][:, :], lhsT=blk, rhs=page(8, 15 * 256)[:, (US_K + 2 * i) * T:(US_K + 2 * i + 2) * T],
                   start=True, stop=True).then_inc(full[5 + i], 1)
            for b, k in ((0, 1), (1, 0), (2, 0), (3, 0), (1, 1)):
                evacuated(pe, "aq", b, k)
            band_scores(0)
            pe.wait_ge(gsq_ready, 1)
            for i in range(2):
                take(pe, "gn", 5 + i, 1)
                mm(ps[5 + i][:, :], lhsT=blk, rhs=gsq[:, i * 512:i * 512 + 512], start=True, stop=True)\
                    .then_inc(full[5 + i], 1)
            for n in range(HEADS):
                j, par = n // 2, n % 2
                if n + 1 < HEADS:
                    band_scores(n + 1)
                gate2(min(2 * n, HEADS - 3 + n) + 3)
                pe.wait_ge(p_ready, HEADS + n + 1)
                b = 5 + n % 2
                take(pe, "batt", b, n // 2)
                for qb in range(2):
                    for kt in range(2):
                        ins = nc.tensor.transpose(ps[b][:, kt * T + qb * P:kt * T + qb * P + P],
                                                  bp[:, 2 * (n % 2) + qb, kt * P:kt * P + P], ident)
                ins.then_inc(full[b], 1)
                if n < HEADS - 3:
                    gate2(2 * n + 4)
                evacuated(pe, "batt", b, n // 2)
                if par == 0:
                    take(pe, "batt", 7, j)
                for kt in range(2):
                    ins = mm(ps[7][64 * par:64 * par + 64, 0:T], lhsT=va[:, kt, 64 * par:64 * par + 64],
                             rhs=bpT[:, 2 * (n % 2) + kt, :], start=kt == 0, stop=kt == 1)
                if par:
                    ins.then_inc(full[7], 1)
            evacuated(pe, "batt", 7, 3)
            tiles("proja", KD, 4, lambda k: oa[:, k, :])
            pe.wait_ge(yr_ready, 1)
            tiles("projr", KD, 4, lambda k: yr[:, k, :])
            pe.wait_ge(mix_ready, 2)
            tiles("wout", KD, KD, lambda k: mix2[:, k, :])
            for j in range(KD):
                stat(7, j, T)
            pe.wait_ge(router_in, 16)
            take(pe, "route", 0, 0)
            for tt in range(2):
                for k in range(KD):
                    if tt == 0:
                        pe.wait_ge(h_ready, 4 * KD + k + 1)
                    ins = mm(ps[0][:, tt * N_EXP:tt * N_EXP + N_EXP], lhsT=h[:, k, tt * P:tt * P + P],
                             rhs=router_v[:, k, :], start=k == 0, stop=k == KD - 1)
            ins.then_inc(full[0], 1)
            for n in range(4):
                tt, half = n // 2, n % 2
                if n == 2:
                    pe.wait_ge(aexp, 2)
                    take(pe, "route", 1, 0)
                    for t2 in range(2):
                        ins = nc.tensor.transpose(ps[1][0:N_EXP, t2 * P:t2 * P + P], tiny[:, 32 + 16 * t2:48 + 16 * t2],
                                                  ident)
                    ins.then_inc(full[1], 1)
                take(pe, "htok", 5 + half, tt)
                for q_ in range(4):
                    ins = nc.tensor.transpose(ps[5 + half][:, q_ * P:q_ * P + P],
                                              h[:, half * 4 + q_, tt * P:tt * P + P], ident)
                ins.then_inc(full[5 + half], 1)
            pe.wait_ge(slot_ready, 1)
            take(pe, "route", 2, 0)
            for tt in range(2):
                ins = nc.tensor.transpose(ps[2][:, tt * N_EXP:tt * N_EXP + N_EXP], fh[0:N_EXP, tt * P:tt * P + P],
                                          ident[0:N_EXP, 0:N_EXP])
            ins.then_inc(full[2], 1)

            def gather(stage, k, i):
                for half in range(2):
                    take(pe, stage, 5 + half, k)
                    for q_ in range(4):
                        f = 4 * half + q_
                        for tt in range(2):
                            ins = mm(ps[5 + half][:, q_ * P:q_ * P + P], lhsT=htok[:, tt, f * P:f * P + P],
                                     rhs=OH[:, tt, ds(i * P, P)], start=tt == 0, stop=tt == 1)
                    ins.then_inc(full[5 + half], 1)
            pe.wait_ge(oh_ready, 2)
            evacuated(pe, "htok", 5, 1)
            evacuated(pe, "htok", 6, 1)
            gather("gather0", 0, 0)
            ex = Stream(pe, ex_loaded, ex_started, ex_flat, EX_RING)

            def group_product(banks, kp, lhs, early=()):
                slab = list(early)
                for _ in range(GROUP - len(slab)):
                    s = ex.whole(ex_flat)
                    slab.append([s[:, 0:D], s[:, D:2 * D]])
                for par in range(2):
                    for half in range(2):
                        for e in range(GROUP):
                            ins = mm(ps[banks[half]][32 * e:32 * e + 32, :], lhsT=lhs[:, 2 * kp + par, CAP * e:CAP * e + CAP],
                                     rhs=slab[e][par][:, half * 512:half * 512 + 512],
                                     start=kp == 0 and par == 0, stop=kp == KD // 2 - 1 and par == 1)
                            if par == half == e == 0:
                                ins.then_inc(ex_started, GROUP)
                        if kp == KD // 2 - 1 and par == 1:
                            ins.then_inc(full[banks[half]], 1)

            def group(i, last=False):
                take(pe, "moe", 2, i * 2)
                take(pe, "moe", 3, i * 2)
                for kp in range(KD // 2):
                    if kp == 2:
                        pe.wait_ge(evac[6], FILLS["moe"][6] + i * 3)
                    if kp > 0:
                        group_product((0, 1), kp, xg)
                    group_product((2, 3), kp, xg)
                pe.wait_ge(group_choice, i + 1)
                take(pe, "moe", 7, i)
                for tt in range(2):
                    ins = nc.tensor.transpose(ps[7][:, tt * P:tt * P + P], OHW_g[:, tt, :], ident)
                ins.then_inc(full[7], 1)
                for half in range(2):
                    evacuated(pe, "moe", 2 + half, i * 2)
                    take(pe, "moe", 5 + half, i * 3)
                    for q_ in range(4):
                        f = 4 * half + q_
                        ins = nc.tensor.transpose(ps[5 + half][:, q_ * P:q_ * P + P], hid[:, f * P:f * P + P], ident)
                    ins.then_inc(full[5 + half], 1)
                take(pe, "moe", 0, i * 2 + 1)
                take(pe, "moe", 1, i * 2 + 1)
                for kp in range(KD // 2):
                    if kp % 2 == 0:
                        evacuated(pe, "moe", 5 + kp // 2, i * 3)
                    group_product((0, 1), kp, hidT)
                if not last:
                    gather("moe", i * 3 + 1, i + 1)
                evacuated(pe, "moe", 0, i * 2 + 1)
                evacuated(pe, "moe", 1, i * 2 + 1)
                evacuated(pe, "moe", 7, i)
                for n, (b, k) in enumerate(scatter_fills(i, last)):
                    take(pe, "moe", b, k)
                    for q_ in range(2):
                        dt = 2 * n + q_
                        ins = mm(ps[b][:, q_ * T:q_ * T + T], lhsT=ys4[:, dt * P:dt * P + P],
                                 rhs=OHT, start=True, stop=True)
                    ins.then_inc(full[b], 1)

            def gate_start(i, early=()):
                take(pe, "moe", 0, i * 2)
                take(pe, "moe", 1, i * 2)
                group_product((0, 1), 0, xg, early)

            evacuated(pe, "gather0", 5, 0)
            for s in range(EX_EARLY):
                pe.wait_ge(ex_early_in[s], 32)
            gate_start(0, ex_early)
            with pe.Fori(0, N_GROUPS - 1) as i:
                ex.loop(i, 12 * GROUP)
                group(i)
                evacuated(pe, "moe", 5, i * 3 + 1)
                gate_start(i + 1)
            ex.end_loop(12 * GROUP, N_GROUPS - 1)
            group(N_GROUPS - 1, last=True)
            for j in range(KD):
                stat(8, j, T)

        @block.scalar
        def _(act):
            A = nc.scalar.activation
            act.dma_start(filt, dram["filt"]).then_inc(filters_in, 16)
            act.dma_start(zT, dram["zT"]).then_inc(filters_in, 16)
            act.dma_start(arena[:, 4 * PAGE:6 * PAGE], dram["tokens"]).then_inc(tokens_in, 16)

            def square(r, j, src, n):
                if j >= 2:
                    act.wait_ge(sq_used, 7 * r + j - 1)
                elif r:
                    act.wait_ge(full[4], norm_fill(r))
                A(sq_v[:, j % 2, 0:n], src, ACT.Square).then_inc(sq_ready, 1)

            def root(r, n):
                act.wait_ge(full[4], norm_fill(r) + 1)
                A(sd[:, 0:n], ps[4][:, 0:n], ACT.Sqrt, bias=eps[:, 0:1], scale=1.0 / D).then_inc(evac[4], 1)

            act.wait_ge(consts_in, 48)
            act.wait_ge(cond_zero, 1)
            A(cond_v[:, :, 0:2], cond[:, :].rearrange("p (k r) -> p k r", r=2), ACT.Silu).then_inc(cond_ready, 1)
            for n in range(3):
                act.wait_ge(arg_ready, n + 1)
                A(fh[:, 0:T], fh[:, T:2 * T], ACT.Sin).then_inc(sin_ready, 1)
            got(act, "lam", 7, 0)
            A(tiny[:, 2:4], ps[7][:, 0:2], ACT.Exp).then_inc(evac[7], 1)
            act.wait_ge(tokens_in, 16)
            for j in range(KD):
                square(0, j, X[:, j, :], 512)
            act.wait_ge(eps_set, 2)
            root(0, 512)
            act.dma_start(w4[0:64, :], dram["w4"]).then_inc(decay_in, 16)
            act.dma_start(page(16, 2048), dram["decay"]).then_inc(decay_in, 16)
            act.dma_start(page(22, 16 * P), dram["FK"]).then_inc(spectra_in, 16)
            act.dma_start(page(13.5, 4 * P), dram["FKalt"]).then_inc(spectra_in, 16)
            act.dma_start(page(18.5, 1024), dram["Fu"]).then_inc(spectra_in, 16)
            act.dma_start(page(19, 1024), dram["Finv"]).then_inc(spectra_in, 16)
            act.dma_start(page(19.5, 512), dram["rope"]).then_inc(spectra_in, 16)
            act.dma_start(router[:, :], dram["router"]).then_inc(router_in, 16)

            def magnitudes():
                for n in range(8):
                    tt, qq = n % 2, n // 2
                    kt, lo = (qq // 2) * 2 + tt, (qq % 2) * 512
                    evacuated(act, "w4", n % 4, n // 4)
                    A(habs[:, kt, lo:lo + 512], hfil[:, kt, lo:lo + 512], ACT.Abs).then_inc(habs_ready, 1)

            def filter_spectrum(tiles_):
                for n in tiles_:
                    got(act, "kdft", n % 4, n // 4)
                    A(Kspec[:, n // 2, (n % 2) * 512:(n % 2) * 512 + 512], ps[n % 4][:, :], ACT.Copy)\
                        .then_inc(evac[n % 4], 1)

            def ffn(stage, r, y, n, between=None):
                def gate(q_, use):
                    b = 2 * (q_ % 2)
                    got(act, stage + "_in", b, use)
                    act.wait_ge(evac[b + 1], FILLS[stage + "_in"][b + 1] + use)
                    A(sil_v[:, q_ % 2, 0:n], ps[b][:, 0:n], ACT.Silu).then_inc(evac[b], 1)
                with act.Fori(0, 5) as i:
                    for q_ in range(4):
                        gate(q_, i * 2 + q_ // 2)
                gate(0, 10)
                gate(1, 10)
                if between:
                    between()
                leave(stage + "_out", r, y, n)

            def leave(stage, r, y, n):
                for t in range(KD):
                    got(act, stage, t % 4, t // 4)
                    square(r, t, ps[t % 4][:, 0:n], n)
                    A(y[:, t, 0:n], ps[t % 4][:, 0:n], ACT.Copy).then_inc(evac[t % 4], 1)
                root(r, n)

            ffn("ffn1", 1, y1, 512, magnitudes)
            filter_spectrum(range(4))
            for j in range(KD):
                act.wait_ge(x_ready, j + 1)
                square(2, j, X[:, j, :], 512)
            root(2, 512)
            filter_spectrum(range(4, 10))
            for n in range(24):
                got(act, "z", n % 4, n // 4)
                A((x0, u, zv)[n // 8][:, n % 8, :], ps[n % 4][:, 0:T], ACT.Identity, bias=c("cb", n),
                  scale=c("cw1", n)).then_inc(z_scaled, 1)
            for n in range(16):
                got(act, "qk", n % 4, n // 4)
                if n >= 2:
                    evacuated(act, "qk", 5 + n % 2, n // 2 - 1)
                if n >= 8:
                    A(kT[:, n - 8, T:2 * T], ps[n % 4][:, T:2 * T], ACT.Copy)
                A(raw_v[:, n % 2, :], ps[n % 4][:, 0:T], ACT.Copy).then_inc(evac[n % 4], 1)
            for n in range(16):
                s, tt = n // 4, n % 4
                got(act, *(("v", tt, s) if s < 3 else ("v_end", tt, 0)))
                A(vtok[:, tt, s * 256:s * 256 + 256], ps[tt][:, 0:256], ACT.Copy).then_inc(evac[tt], 1)
            act.wait_ge(kn_ready, 1)
            for ct in range(KD):
                got(act, "yinv", ct % 4, ct // 4)
                A(yc[:, ct, :], ps[ct % 4][:, 0:T], ACT.Copy, scale=tiny[:, 8 + ct:9 + ct]).then_inc(evac[ct % 4], 1)
            act.dma_start(page(19, HEADS * P)[0:HEADS], dram["headbc"]).then_inc(headbc_in, 16)
            for n in range(16):
                got(act, "gates", n % 4, n // 4)
                A(gates[:, n, :], ps[n % 4][:, 0:T], ACT.Sigmoid).then_inc(evac[n % 4], 1)

            def exps(hd):
                act.wait_ge(nm_ready, hd + 1)
                o = 4 * (hd % 2)
                for b in range(4):
                    A(prob[:, o + b, :], ps[b][:, :], ACT.Exp, bias=tiny[:, 16 + o + b:17 + o + b],
                      scale=0.125, accum_out=tiny[:, 24 + o + b:25 + o + b]).then_inc(evac[b], 1)
            exps(0)
            for hd in range(HEADS):
                if hd + 1 < HEADS:
                    exps(hd + 1)
                got(act, "att", 5, hd)
                A(pT[:, 4 * (hd % 2):4 * (hd % 2) + 4, 0:P], ps[5][:, :].rearrange("p (k n) -> p k n", n=P), ACT.Copy)\
                    .then_inc(evac[5], 1)
                got(act, "att", 7, hd)
                A(oT[:, hd, :], ps[7][:, 0:T], ACT.Copy).then_inc(evac[7], 1)
                evacuated(act, "att", 7, hd)
                A(osq[:, hd, :], oT[:, hd, :], ACT.Square).then_inc(osq_ready, 1)
            got(act, "onorm", 5, 0)
            A(fh[0:HEADS, T:2 * T], ps[5][0:HEADS, 0:T], ACT.Sqrt, bias=eps[0:HEADS, 0:1], scale=1.0 / P)\
                .then_inc(evac[5], 1)
            leave("wo", 3, y2, T)
            act.wait_ge(mix_ready, 1)
            act.dma_start(masks, dram["masks"]).then_inc(masks_in, 16)
            act.dma_start(lora, dram["lora"][:, 0:1024]).then_inc(masks_in, 16)
            act.dma_start(g_up, dram["lora"][:, 1024:1536]).then_inc(masks_in, 16)
            for j in range(KD):
                act.wait_ge(x_ready, KD + j + 1)
                square(4, j, x[:, j, :], T)
            root(4, T)
            ffn("ffn2", 5, y3, T)
            for j in range(KD):
                act.wait_ge(x_ready, 2 * KD + j + 1)
                square(6, j, x[:, j, :], T)
            root(6, T)

            act.wait_ge(mu_ready, 1)
            for t in range(15):
                got(act, "shift", t % 4, t // 4)
                A(US[:, t, :], ps[t % 4][:, 0:T], ACT.Copy, scale=rt[:, 256 + t:257 + t]).then_inc(us_scaled, 1)
            evacuated(act, "shift", 0, 0)
            A(US[:, 0, :], US[:, 0, :], ACT.Tanh).then_inc(act_us, 1)
            evacuated(act, "shift", 14 % 4, 14 // 4)
            A(US[:, US_G, :], US[:, US_G, :], ACT.Sigmoid).then_inc(g_ready, 1)
            for which in range(2):
                dst = (sig256, iclr)[which]
                for half in range(2):
                    for d in range(2):
                        b = 2 * d + half
                        got(act, "lora", b, which)
                        for q_ in range(2):
                            j = 4 * d + 2 * half + q_
                            ins = A(dst[:, j, :], ps[b][:, q_ * T:q_ * T + T], ACT.Sigmoid,
                                    bias=c(("w0", "a0")[which], j))
                        ins.then_inc(evac[b], 1)
            act.wait_ge(kkr_ready, 1)
            A(gsq_kk, kkr_flat, ACT.Square).then_inc(kksq_ready, 1)
            act.wait_ge(ss_ready, 1)
            A(nrm, nrm, ACT.Sqrt).then_inc(nrm_ready, 1)
            for d in range(2):
                act.wait_ge(logs_ready, d + 1)
                o = slice(8 * d, 8 * d + 8)
                inc = (D1, D2)[d]
                A(Einc[:, o, :], inc[:, o, :], ACT.Exp, scale=-DECAY_SCALE)
                A(Eneg[:, o, :], inc[:, o, :], ACT.Exp, scale=DECAY_SCALE)
                A(Eexc[:, o, :], (D2, D1)[d][:, o, :], ACT.Exp, scale=(-DECAY_SCALE, DECAY_SCALE)[d])
                A(scl[:, 4 * d:4 * d + 4], scl[:, 4 * d:4 * d + 4], ACT.Exp, scale=-DECAY_SCALE).then_inc(exps_ready, 1)
            for t in range(5):
                got(act, "aq", t % 4, t // 4)
                A(qa[:, t, :] if t < 4 else ka, ps[t % 4][:, 0:T], ACT.Copy, scale=0.125 if t < 4 else 1.0).then_inc(evac[t % 4], 1)
            got(act, "aq", 1, 1)
            A(va, ps[1][:, 0:T].rearrange("p (k n) -> p k n", n=P), ACT.Copy).then_inc(evac[1], 1)
            act.wait_ge(qq_ready, 1)
            for k in range(3):
                for b in (5, 6):
                    got(act, "toks", b, k)
                    dst = Vtok[:, b - 5, :] if k == 0 else toks[:, 2 * (k - 1) + b - 5, :]
                    A(dst, ps[b][:, :], ACT.Copy).then_inc(evac[b], 1)

            def gate2(t):
                b = 7 if t < 3 else 2 + (t - 3) % 2
                if t < 3:
                    got(act, "gates2_start", b, t)
                else:
                    got(act, "gates2", b, (t - 3) // 2)
                A(gates2[:, t, :], ps[b][:, 0:T], ACT.Copy).then_inc(evac[b], 1)
            for s in range(2):
                for use in range(12):
                    for d in range(2):
                        got(act, f"inv{s}", 3 * d, use)
                        A(Pw[:, 4 * d:4 * d + 4, :], ps[3 * d][:, :].rearrange("p (i n) -> p i n", n=P), ACT.Copy)\
                            .then_inc(evac[3 * d], 1)
                if s:
                    gate2(0)
                for d in range(2):
                    for par in range(2):
                        b = 5 * d + par
                        got(act, f"tail{s}", b, 0)
                        A(Wsb[d].rearrange("p (j r) n -> p j r n", r=2)[:, :, par, :],
                          ps[b][:, 0:256].rearrange("p (j n) -> p j n", n=64), ACT.Copy).then_inc(evac[b], 1)
                if s:
                    gate2(1)
                for d in range(2):
                    got(act, f"tail{s}", 2 + d, 0)
                    A(nU[d], ps[2 + d][:, :].rearrange("p (h n) -> p h n", n=64), ACT.Copy, scale=-1.0).then_inc(evac[2 + d], 1)
                if s:
                    gate2(2)
            for i in range(2):
                got(act, "gn", 2 + i, 0)
                A(g_out[:, i * 512:i * 512 + 512], ps[2 + i][:, :], ACT.Copy).then_inc(evac[2 + i], 1)
            for i in range(2):
                evacuated(act, "gn", i, 0)
            A(gsq, dev, ACT.Square).then_inc(gsq_ready, 1)
            for i in range(2):
                got(act, "gn", 5 + i, 1)
                A(gsd[:, i * 512:i * 512 + 512], ps[5 + i][:, :], ACT.Sqrt, bias=eps[:, 1:2], scale=1.0 / 64)\
                    .then_inc(evac[5 + i], 1)

            def band_exps(n):
                act.wait_ge(nm_ready, HEADS + n + 1)
                o, head = 2 * (n % 2), n // 2 + 4 * (n % 2)
                for qb in range(2):
                    A(bp[:, o + qb, :], bs[:, o + qb, :], ACT.Exp, bias=tiny[:, 16 + o + qb:17 + o + qb],
                      accum_out=tiny[:, 20 + o + qb:21 + o + qb])
                A(tiny[:, 24 + o:26 + o], tiny[:, 16 + o:18 + o], ACT.Exp, bias=c("sink", head)).then_inc(es_ready, 1)

            band_exps(0)
            for n in range(HEADS):
                if n + 1 < HEADS:
                    band_exps(n + 1)
                gate2(min(2 * n, HEADS - 3 + n) + 3)
                b = 5 + n % 2
                got(act, "batt", b, n // 2)
                A(bpT[:, 2 * (n % 2):2 * (n % 2) + 2, :], ps[b][:, :].rearrange("p (k n) -> p k n", n=T), ACT.Copy)\
                    .then_inc(evac[b], 1)
                if n < HEADS - 3:
                    gate2(2 * n + 4)
                if n % 2:
                    got(act, "batt", 7, n // 2)
                    A(oa[:, n // 2, :], ps[7][:, 0:T], ACT.Copy).then_inc(evac[7], 1)
            evacuated(act, "gates2_start", 7, 2)
            for b in (2, 3):
                evacuated(act, "gates2", b, 8 - b)
            for half in range(2):
                A(gates2[:, 8 * half:8 * half + 8, :], gates2[:, 8 * half:8 * half + 8, :], ACT.Sigmoid).then_inc(gates_ready, 1)
            for j in range(KD):
                evacuated(act, "wout", j % 4, j // 4)
                square(7, j, x[:, j, :], T)
            root(7, T)
            act.wait_ge(nm_ready, 2 * HEADS + 1)
            for tt in range(2):
                ins = A(tiny[:, 32 + 16 * tt:48 + 16 * tt], ps[0][:, 16 * tt:16 * tt + 16], ACT.Exp,
                        bias=tiny[:, 16 + tt:17 + tt], accum_out=tiny[:, 20 + tt:21 + tt])
            ins.then_inc(evac[0], 1)
            for n in range(4):
                tt, half = n // 2, n % 2
                got(act, "htok", 5 + half, tt)
                A(htok[:, tt, half * 512:half * 512 + 512], ps[5 + half][:, :], ACT.Copy).then_inc(evac[5 + half], 1)
            got(act, "gather0", 5, 0)
            A(xg[:, 0:4, :], ps[5][:, :].rearrange("p (k n) -> p k n", n=P), ACT.Copy).then_inc(evac[5], 1)

            def group(i, last=False):
                for half in range(2):
                    o = slice(half * 512, half * 512 + 512)
                    got(act, "moe", half, i * 2)
                    A(msil[:, o], ps[half][:, :], ACT.Silu).then_inc(evac[half], 1)
                got(act, "moe", 5, i * 3)
                A(hidT[:, 0:4, :], ps[5][:, :].rearrange("p (k n) -> p k n", n=P), ACT.Copy).then_inc(evac[5], 1)
                got(act, "moe", 0, i * 2 + 1)
                A(ys4[:, 0:512], ps[0][:, :], ACT.Copy).then_inc(evac[0], 1)
                if last:
                    return
                got(act, "moe", 5, i * 3 + 1)
                A(xg[:, 0:4, :], ps[5][:, :].rearrange("p (k n) -> p k n", n=P), ACT.Copy).then_inc(evac[5], 1)
            with act.Fori(0, N_GROUPS - 1) as i:
                group(i)
            group(N_GROUPS - 1, last=True)
            for j in range(KD):
                b = SCATTER[j // 2]
                evacuated(act, "moe", b, 3 * N_GROUPS - 2 if b > 4 else 2 * N_GROUPS - 1)
                square(8, j, x[:, j, :], T)
            root(8, T)

        @block.vector
        def _(dve):
            V = nc.vector
            tt_, ts_, stt = V.tensor_tensor, V.tensor_scalar, V.scalar_tensor_tensor
            steps = Steps(dve, dve_step)
            do, settle = steps.do, steps.settle

            def inverse_root(r, n):
                dve.wait_ge(evac[4], norm_fill(r) + 1)
                do(V.reciprocal(rstd[:, 0:n], sd[:, 0:n]))

            def sum_squares(r, n):
                for j in range(1, KD):
                    dve.wait_ge(sq_ready, KD * r + j + 1)
                    if j > 1:
                        dve.wait_ge(sq_used, 7 * r + j)
                    ins = tt_(rstd[:, 0:n], sq_v[:, 0, 0:n] if j == 1 else rstd[:, 0:n], sq_v[:, j % 2, 0:n], add)
                    if j < KD - 1:
                        ins.then_inc(sq_used, 2 if j == 1 else 1)
                    else:
                        ins.then_inc(acc_ready, 1)

            def normalise(src, dst, parts):
                settle()
                if parts[0][3] is None:
                    for j in range(KD):
                        for lo, hi, gn_, _ in parts:
                            ins = stt(dst[:, j, lo:hi], src[:, j, lo:hi], gn_[:, j:j + 1], rstd[:, lo:hi], mult, mult)
                        ins.then_inc(h_ready, 1)
                    return
                scaled = []
                for j in range(KD + 1):
                    if j < KD:
                        for lo, hi, gn_, _ in parts:
                            do(stt(dst[:, j, lo:hi], src[:, j, lo:hi], gn_[:, j:j + 1], rstd[:, lo:hi], mult, mult))
                        scaled.append(steps.n)
                    if j:
                        dve.wait_ge(dve_step, scaled[j - 1])
                        for lo, hi, _, shift in parts:
                            ins = ts_(dst[:, j - 1, lo:hi], dst[:, j - 1, lo:hi], shift[:, j - 1:j], None, add)
                        ins.then_inc(h_ready, 1)

            def residual(stage, y, parts, src, dst, n):
                settle()
                for b in range(4):
                    evacuated(dve, stage, b, 1)
                scaled = []
                for j in range(KD + 1):
                    if j < KD:
                        for lo, hi, gn_ in parts:
                            do(stt(y[:, j, lo:hi], y[:, j, lo:hi], gn_[:, j:j + 1], rstd[:, lo:hi], mult, mult))
                        scaled.append(steps.n)
                    if j:
                        dve.wait_ge(dve_step, scaled[j - 1])
                        tt_(dst[:, j - 1, 0:n], src[:, j - 1, 0:n], y[:, j - 1, 0:n], add).then_inc(x_ready, 1)

            TWO_PI_HI, TWO_PI_LO = 6.28125, 2 * math.pi - 6.28125
            ROUND = 1.5 * 2.0 ** 23
            PI = 3.1415925
            dve.wait_ge(consts_in, 48)
            for n in range(3):
                got(dve, "mlp", 5, n)
                a, k1, k2 = fh[:, T:2 * T], fh[:, 2 * T:3 * T], fh[:, 3 * T:4 * T]
                ts_(a, ps[5][0:64, 0:T], c("fb", n)[0:64], c("ffreq")[0:64], add, mult).then_inc(evac[5], 1)
                evacuated(dve, "mlp", 5, n)
                do(ts_(k1, a, 1.0 / (2 * math.pi), ROUND, mult, add))
                settle()
                do(ts_(k1, k1, ROUND, None, sub))
                settle()
                do(stt(a, k1, -TWO_PI_HI, a, mult, add))
                settle()
                do(stt(a, k1, -TWO_PI_LO, a, mult, add))
                settle()
                ts_(a, a, PI, -PI, mn_op, mx_op).then_inc(arg_ready, 1)
            tt_(tiny[0:64, 0:2], c("lam", 0, 2)[0:64], c("lam", 2, 2)[0:64], mult).then_inc(prod_ready, 1)
            evacuated(dve, "lam", 7, 0)
            do(stt(tiny[:, 4:5], tiny[:, 3:4], LAM_INIT, tiny[:, 2:3], sub, sub))
            def ada_sums(stage, k):
                got(dve, stage, 7, k)
                V.tensor_copy(ada_rows[:, :], ps[7][:, :]).then_inc(evac[7], 1)

            def ada_columns(stage, k, m):
                got(dve, stage, 6, k)
                tt_(mods[:, :].rearrange("p (m h j r) -> p m j h r", m=N_MOD, h=2, r=2)[:, m, :, :, :],
                    ps[6][:, 0:16].rearrange("p (m j h r) -> p m j h r", m=1, h=2, r=2),
                    c("b_ada", 0, 72).rearrange("p (m h j) -> p m j h", m=N_MOD, h=2)[:, m, :, :].unsqueeze(4)
                    .to_broadcast([P, 1, 4, 2, 2]), add).then_inc(evac[6], 1)
            for k in range(2):
                ada_sums("ada_head", k)
                ada_columns("ada_head", k, slice(k, k + 1))
                if k == 0:
                    inverse_root(0, 512)
                    settle()
            evacuated(dve, "ada_head", 6, 1)
            for r in range(2):
                do(stt(gain_v[:, r, :], mod(1, r), 1.0, g(0), add, mult))
            normalise(X, h1, [(0, T, gain_v[:, 0, :], mod(0, 0)), (T, 2 * T, gain_v[:, 1, :], mod(0, 1))])

            def filter_in_time():
                dve.wait_ge(decay_in, 32)
                for n in range(8):
                    tt, qq = n % 2, n // 2
                    kt, lo = (qq // 2) * 2 + tt, (qq % 2) * 512
                    got(dve, "w4", n % 4, n // 4)
                    tt_(hfil[:, kt, lo:lo + 512], ps[n % 4][:, :], decay[:, tt, lo:lo + 512], mult).then_inc(evac[n % 4], 1)

            def ffn_in(stage, hid, n, with_ada):
                def up(q_, use, at):
                    b = 2 * (q_ % 2)
                    dve.wait_ge(evac[b], FILLS[stage + "_in"][b] + use + 1)
                    got(dve, stage + "_in", b + 1, use)
                    tt_(hid[:, at, 0:n], sil_v[:, q_ % 2:q_ % 2 + 1, 0:n], ps[b + 1][:, 0:n].unsqueeze(1), mult)\
                        .then_inc(evac[b + 1], 1)
                with dve.Fori(0, 5) as i:
                    for q_ in range(4):
                        if with_ada and q_ == 3:
                            ada_sums(stage + "_in", i)
                        up(q_, i * 2 + q_ // 2, ds(i * 4 + q_, 1))
                    if with_ada:
                        ada_columns(stage + "_in", i, ds(i + 2, 1))
                up(0, 10, slice(20, 21))
                up(1, 10, slice(21, 22))

            ffn_in("ffn1", hid1, 512, True)
            filter_in_time()
            got(dve, "knorm", 5, 0)
            ts_(tiny[:, 8:16], ps[5][:, 0:KD], EPS, None, add).then_inc(evac[5], 1)
            evacuated(dve, "knorm", 5, 0)
            V.reciprocal(tiny[:, 8:16], tiny[:, 8:16]).then_inc(kn_ready, 1)
            evacuated(dve, "ffn1_in", 6, 4)
            for r in range(2):
                do(stt(gain_v[:, 2 + r, :], mod(2, r), 0.5, g(1), mult, mult))
                do(stt(gain_v[:, r, :], mod(4, r), 1.0, g(2), add, mult))
            sum_squares(1, 512)
            inverse_root(1, 512)
            residual("ffn1_out", y1, [(0, T, gain_v[:, 2, :]), (T, 2 * T, gain_v[:, 3, :])], X, X, 512)
            inverse_root(2, 512)
            normalise(X, h1, [(0, T, gain_v[:, 0, :], mod(3, 0)), (T, 2 * T, gain_v[:, 1, :], mod(3, 1))])
            for n in range(24):
                b, dst = n % 4, (x0, u, zv)[n // 8][:, n % 8, :]
                dve.wait_ge(z_scaled, n + 1)
                do(stt(dst[:, 1:T], ps[b][:, 0:T - 1], c("cw0", n), dst[:, 1:T], mult, add))
                settle()
                stt(dst[:, 0:T - 1], ps[b][:, 1:T], c("cw2", n), dst[:, 0:T - 1], mult, add).then_inc(evac[b], 1)
                if n >= 16:
                    evacuated(dve, "z", b, n // 4)
                    tt_(u[:, n - 16, :], u[:, n - 16, :], dst, mult).then_inc(u_ready, 1)
                if n in (7, 15):
                    ada_sums("z", n // 8)
                if n in (9, 17):
                    ada_columns("z", n // 16, slice(7 + n // 16, 8 + n // 16))
            for n in range(16):
                b = 5 + n % 2
                dst = q_sb[:, n, :] if n < 8 else kT[:, n - 8, 0:T]
                got(dve, "qk", b, n // 2)
                if n >= 2:
                    evacuated(dve, "qk", b, n // 2 - 1)
                r = rt[:, (n % 2) * T:(n % 2) * T + T]
                do(tt_(r, ps[b][:, 0:T], rope[:, 1, :], mult))
                do(tt_(dst, raw_v[:, n % 2, :], rope[:, 0, :], mult))
                settle()
                tt_(dst, dst, r, add).then_inc(evac[b], 1)
            for n in range(4):
                kt, half = n // 2, n % 2
                got(dve, "ut", 5 + half, kt)
                V.tensor_copy(utok[:, kt, half * 512:half * 512 + 512], ps[5 + half][:, :]).then_inc(evac[5 + half], 1)
            for i in range(4):
                j, half = i // 2, i % 2
                o = slice(half * 512, half * 512 + 512)
                br, bi = 2 * half, 2 * half + 1
                k_alt = Kspec[:, 4, o] if j == 0 else Kspec[:, 1, o]
                if i:
                    settle()
                    dve.wait_ge(y_ready, i)
                got(dve, "uspec", br, j)
                do(tt_(Y[:, j, o], ps[br][:, :], Kspec[:, j, o], mult))
                tt_(Y[:, 2 + j, o], ps[br][:, :], Kspec[:, 2 + j, o], mult).then_inc(evac[br], 1)
                got(dve, "uspec", bi, j)
                do(tt_(rt, ps[bi][:, :], Kspec[:, 2 + j, o], mult))
                tt_(raw, ps[bi][:, :], k_alt, mult).then_inc(evac[bi], 1)
                settle()
                do(tt_(Y[:, j, o], Y[:, j, o], rt, sub))
                evacuated(dve, "uspec", bi, j)
                evacuated(dve, "uspec", br, j)
                tt_(Y[:, 2 + j, o], Y[:, 2 + j, o], raw, add).then_inc(y_ready, 1)
            for ct in range(KD):
                evacuated(dve, "yinv", ct % 4, ct // 4)
                do(stt(yc[:, ct, :], u[:, ct, :], c("hyb", ct), yc[:, ct, :], mult, add))
            settle()
            tt_(hy, yc, x0, mult).then_inc(hy_ready, 1)

            def maxima(hd):
                o = 4 * (hd % 2)
                for b in range(4):
                    got(dve, "att", b, hd)
                    do(V.tensor_reduce(tiny[:, 16 + o + b:17 + o + b], ps[b][:, :], AXX, mx_op))
                settle()
                ts_(tiny[:, 16 + o:20 + o], tiny[:, 16 + o:20 + o], -0.125, None, mult).then_inc(nm_ready, 1)
            maxima(0)
            for hd in range(HEADS):
                o = 4 * (hd % 2)
                for b in range(4):
                    evacuated(dve, "att", b, hd)
                do(V.reciprocal(tiny[:, 24 + o:28 + o], tiny[:, 24 + o:28 + o]))
                settle()
                do(ts_(tiny[:, 26 + o:28 + o], tiny[:, 26 + o:28 + o], tiny[:, 4:5], None, mult))
                for qb in range(2):
                    do(ts_(prob[:, o + qb, :], prob[:, o + qb, :], tiny[:, 24 + o + qb:25 + o + qb], None, mult))
                settle()
                for qb in range(2):
                    ins = stt(prob[:, o + qb, :], prob[:, o + 2 + qb, :], tiny[:, 26 + o + qb:27 + o + qb],
                              prob[:, o + qb, :], mult, add)
                ins.then_inc(p_ready, 1)
                if hd + 1 < HEADS:
                    maxima(hd + 1)
                got(dve, "att", 6, hd)
                V.tensor_copy(pT[:, o:o + 4, P:2 * P], ps[6][:, :].rearrange("p (k n) -> p k n", n=P))\
                    .then_inc(evac[6], 1)
                if hd == 0:
                    for b in range(4):
                        evacuated(dve, "gates", b, 3)
                dve.wait_ge(full[4], 3 + hd + 1)
                tt_(mix[:, hd, :], ps[4][:, 0:T], gates[:, hd, :], mult).then_inc(evac[4], 1)
            do(ts_(tiny[:, 5:6], c("subg"), 1.0 - LAM_INIT, None, mult))
            evacuated(dve, "onorm", 5, 0)
            V.reciprocal(fh[0:HEADS, 0:T], fh[0:HEADS, T:2 * T]).then_inc(hr_ready, 1)
            settle()
            for j in range(HEADS):
                got(dve, "onorm", j // 2, 0)
                ins = stt(oT[:, j, :], oT[:, j, :], tiny[:, 5:6], ps[j // 2][:, (j % 2) * T:(j % 2) * T + T], mult, mult)
                if j % 2:
                    ins.then_inc(evac[j // 2], 1)
            def gated_add(stage, dst, gts, first):
                for t in range(KD):
                    got(dve, stage, t % 4, t // 4)
                    settle()
                    tt_(rt[:, 0:T], ps[t % 4][:, 0:T], gts[:, first + t, :], mult).then_inc(evac[t % 4], 1)
                    evacuated(dve, stage, t % 4, t // 4)
                    ins = tt_(dst[:, t, :], dst[:, t, :], rt[:, 0:T], add)
                    if t < KD - 1:
                        do(ins)
                ins.then_inc(mix_ready, 1)
            dve.wait_ge(evac[4], norm_fill(3))
            gated_add("daout", mix, gates, KD)
            do(tt_(gain_v[:, 2, :], mod(5, 0), g(3), mult))
            do(stt(gain_v[:, 0, :], mod(7, 0), 1.0, g(4), add, mult))
            sum_squares(3, T)
            inverse_root(3, T)
            residual("wo", y2, [(0, T, gain_v[:, 2, :])], X, x, T)
            inverse_root(4, T)
            normalise(x, h, [(0, T, gain_v[:, 0, :], mod(6, 0))])
            ffn_in("ffn2", hid2, T, False)
            do(stt(gain_v[:, 2, :], mod(8, 0), 0.5, g(5), mult, mult))
            sum_squares(5, T)
            inverse_root(5, T)
            residual("ffn2_out", y3, [(0, T, gain_v[:, 2, :])], x, x, T)
            do(tt_(rt[:, 256:271], c("mup", 0, 15), c("mun", 0, 15), add))
            settle()
            ts_(rt[:, 256:271], rt[:, 256:271], -1.0, 1.0, mult, add).then_inc(mu_ready, 1)
            inverse_root(6, T)
            normalise(x, h, [(0, T, c("nmix", 0, 8), None)])

            for t in range(15):
                b, dst = t % 4, US[:, t, :]
                dve.wait_ge(us_scaled, t + 1)
                do(stt(dst[:, 1:T], ps[b][:, 0:T - 1], c("mup", t), dst[:, 1:T], mult, add))
                settle()
                stt(dst[:, 0:T - 1], ps[b][:, 1:T], c("mun", t), dst[:, 0:T - 1], mult, add).then_inc(evac[b], 1)
            for b in range(4):
                dve.wait_ge(evac[b], FILLS["lora"][b])
            for j in range(3):
                do(ts_(kkr[:, j, :], US[:, US_K + j, :], c("kk", j), None, mult))
            ts_(kkr[:, 3, :], US[:, US_K + 3, :], c("kk", 3), None, mult).then_inc(kkr_ready, 1)
            for d in range(2):
                for half in range(2):
                    evacuated(dve, "lora", 2 * d + half, 0)
                for row in range(8 * d, 8 * d + 8):
                    do(V.tensor_tensor_scan(cum[:, row, :], ones, sig[:, row, :], 0.0, mult, add))
                settle()
                o = slice(8 * d, 8 * d + 8)
                do(tt_(D1[:, o, :], cum[:, o, :], cum[:, o, 63:64].to_broadcast([P, 8, P]), sub))
                cv = cum[:, o, :].rearrange("p (j c) n -> p j c n", c=2)
                sv = scl[:, 4 * d:4 * d + 4]
                do(tt_(sv, cv[:, :, 0, 127], cv[:, :, 0, 63], sub))
                settle()
                do(tt_(sv, sv, cv[:, :, 1, 63], add))
                if d == 0:
                    ins = tt_(D2[:, o, :], D1[:, o, :], sig[:, o, :], sub)
                else:
                    ins = tt_(D2[:, o, :], sig[:, o, :], D1[:, o, :], sub)
                ins.then_inc(logs_ready, 1)
            for i in range(2):
                got(dve, "kkn", 5 + i, 0)
                ts_(nrm[:, i * 512:i * 512 + 512], ps[5 + i][:, :], 1e-24, None, mx_op).then_inc(evac[5 + i], 1)
            evacuated(dve, "kkn", 5, 0)
            evacuated(dve, "kkn", 6, 0)
            V.tensor_copy(tiny[:, 0:1], nrm[:, 0:1]).then_inc(ss_ready, 1)
            do(ts_(tiny[:, 28:32], c("ka", 0, 4), -1.0, 1.0, mult, add))
            for b in range(4):
                evacuated(dve, "lora", b, 1)
            settle()
            kd256 = page(4, 2048, 256)
            for d in range(2):
                for j in range(4):
                    do(ts_(kd256[:, 4 * d + j, :], iclr[:, 4 * d + j, :], c("ka", j), tiny[:, 28 + j:29 + j], mult, add))
            settle()
            for d in range(2):
                do(tt_(kd256[:, 4 * d:4 * d + 4, :], kd256[:, 4 * d:4 * d + 4, :], US[:, US_K:US_K + 4, :], mult))
            settle()
            dve.wait_ge(nrm_ready, 1)
            do(V.reciprocal(nrm, nrm))
            settle()
            do(tt_(kkn256, kkr, nrm.rearrange("p (j n) -> p j n", n=T), mult))
            settle()
            r_rows = page(8, 15 * 256, P)[:, 2 * US_R:2 * US_R + 8, :]
            QQv = QQ.rearrange("p (a w) n -> p a w n", w=2)
            for d in range(2):
                dve.wait_ge(exps_ready, d + 1)
            for d in range(2):
                o = slice(8 * d, 8 * d + 8)
                do(tt_(BT[:, o, :], kkn, iclr128[:, o, :], mult))
                do(tt_(KT[:, o, :], kdir[:, o, :], Eneg[:, o, :], mult))
                do(tt_(QQv[:, o, 0, :], kkn, Eexc[:, o, :], mult))
                do(tt_(QQv[:, o, 1, :], r_rows, Einc[:, o, :], mult))
            settle()
            tt_(BT, BT, Eneg, mult).then_inc(qq_ready, 1)
            do(tt_(rkk, kd256[:, 0:4, :], kd256[:, 4:8, :], add))
            settle()
            for j in range(4):
                do(stt(US[:, US_K + j, :], US[:, US_K + j, :], c("rk", j), US[:, US_R + j, :], mult, mult))
            dve.wait_ge(am_zero, 1)
            dve.wait_ge(masks_in, 48)
            keep_bits = keep.bitcast(mybir.dt.uint32)
            for s in range(2):
                for d in range(2):
                    for hd in range(HEADS):
                        j, par = hd // 2, hd % 2
                        b = 2 * (j % 2) + par
                        got(dve, f"am{s}", b, 2 * d + j // 2)
                        V.copy_predicated(AM[:, 8 * d + hd, :], keep_bits[:, d, :], ps[b][:, :]).then_inc(evac[b], 1)
                for pair in range(2):
                    for d in range(2):
                        u0 = 8 * d + 4 * pair
                        bx, bt = (1, 5)[d], (2, 6)[d]
                        eye4 = ident.unsqueeze(1).to_broadcast([P, 4, P])
                        dve.wait_ge(nl_ready, (s * 2 + pair) * 14 + d + 1)
                        if s:
                            got(dve, "tail0", 2 + d, 0)
                        if s or pair:
                            evacuated(dve, f"inv{s if pair else 0}", bx, 5 if pair else 11)
                            evacuated(dve, f"inv{s if pair else 0}", bt, 5 if pair else 11)
                        tt_(XT[:, u0:u0 + 4, :], eye4, NL[:, 4 * d:4 * d + 4, :], sub).then_inc(x_init, 1)
                    for d in range(2):
                        bx = (1, 5)[d]
                        got(dve, f"inv{s}", bx, 6 * pair)
                        tt_(Xw[:, 4 * d:4 * d + 4, :], eye4, ps[bx][:, :].rearrange("p (i n) -> p i n", n=P), sub)\
                            .then_inc(evac[bx], 1)
                    for lv in range(1, 7):
                        use = pair * 6 + lv - 1
                        for d in range(2):
                            bx, bt = (1, 5)[d], (2, 6)[d]
                            u0 = 8 * d + 4 * pair
                            evacuated(dve, f"inv{s}", bx, use)
                            if lv == 1:
                                dve.wait_ge(x_init, (s * 2 + pair) * 2 + d + 1)
                            else:
                                evacuated(dve, f"inv{s}", bt, use - 1)
                            for dst, b, k in ((Xw[:, 4 * d:4 * d + 4, :], bx, use + 1), (XT[:, u0:u0 + 4, :], bt, use)):
                                if lv == 6 and b == bx:
                                    continue
                                got(dve, f"inv{s}", b, k)
                                tt_(dst, dst, ps[b][:, :].rearrange("p (i n) -> p i n", n=P), sub).then_inc(evac[b], 1)
                for d in range(2):
                    ch = d if s == 0 else 1 - d
                    w_c = wkv[:, :, ch * P:ch * P + P]
                    y_ps = ps[5 * d][:, :].rearrange("p (j n) -> p j n", n=P)
                    got(dve, f"tail{s}", 5 * d, 1)
                    if s == 0:
                        b = 5 * d + 1
                        V.tensor_copy(w_c, y_ps).then_inc(evac[5 * d], 1)
                        got(dve, "tail0", b, 1)
                        tt_(state_v[:, d, :, :], ps[b][:, 0:256].rearrange("p (j n) -> p j n", n=64),
                            scl[:, 4 * d:4 * d + 4].unsqueeze(2).to_broadcast([P, 4, 64]), mult).then_inc(evac[b], 1)
                    else:
                        evacuated(dve, "tail0", 5 - 5 * d, 1)
                        tt_(w_c, w_c, y_ps, add).then_inc(evac[5 * d], 1)
            wkv_flat = page(5.5, 1024)
            evacuated(dve, "tail1", 0, 1)
            evacuated(dve, "tail1", 5, 1)
            for i in range(2):
                o = slice(i * 512, i * 512 + 512)
                got(dve, "gn", i, 0)
                stt(dev[:, o], ps[i][:, :], -1.0 / 64, wkv_flat[:, o], mult, add).then_inc(evac[i], 1)
            US_flat = page(8, 15 * 256)
            for i in range(2):
                got(dve, "gn", 5 + i, 0)
                tt_(bonus[:, i * 512:i * 512 + 512], ps[5 + i][:, :],
                    US_flat[:, US_V * T + i * 512:US_V * T + i * 512 + 512], mult).then_inc(evac[5 + i], 1)

            def heads_out(step):
                o = slice(step % 2 * 512, step % 2 * 512 + 512)
                if step < 2:
                    evacuated(dve, "gn", 5 + step, 1)
                    do(V.reciprocal(gsd[:, o], gsd[:, o]))
                elif step < 4:
                    settle()
                    do(tt_(dev[:, o], dev[:, o], gsd[:, o], mult))
                elif step == 4:
                    settle()
                    for j in range(4):
                        do(ts_(dev[:, j * T:j * T + T], dev[:, j * T:j * T + T], c("lnw", j), c("lnb", j), mult, add))
                elif step == 5:
                    evacuated(dve, "gn", 5, 0)
                    evacuated(dve, "gn", 6, 0)
                    settle()
                    do(tt_(dev, dev, bonus, add))
                elif step == 6:
                    for i in range(2):
                        evacuated(dve, "gn", 2 + i, 0)
                    settle()
                    tt_(page(4, 1024), dev, g_out, mult).then_inc(yr_ready, 1)

            def band_maxima(n):
                b, o, head = n % 2, 2 * (n % 2), n // 2 + 4 * (n % 2)
                got(dve, "batt", b, n // 2)
                stt(bs[:, o:o + 2, :], dist, 2.0 ** -(head + 1), ps[b][:, :].rearrange("p (q n) -> p q n", n=T), mult, add)\
                    .then_inc(evac[b], 1)
                evacuated(dve, "batt", b, n // 2)
                do(V.tensor_reduce(tiny[:, 16 + o:18 + o], bs[:, o:o + 2, :], AXX, mx_op))
                settle()
                ts_(tiny[:, 16 + o:18 + o], tiny[:, 16 + o:18 + o], c("sink", head), -1.0, mx_op, mult)\
                    .then_inc(nm_ready, 1)
            band_maxima(0)
            for n in range(HEADS):
                o = 2 * (n % 2)
                dve.wait_ge(es_ready, n + 1)
                do(tt_(tiny[:, 20 + o:22 + o], tiny[:, 20 + o:22 + o], tiny[:, 24 + o:26 + o], add))
                settle()
                do(V.reciprocal(tiny[:, 20 + o:22 + o], tiny[:, 20 + o:22 + o]))
                settle()
                for qb in range(2):
                    ins = ts_(bp[:, o + qb, :], bp[:, o + qb, :], tiny[:, 20 + o + qb:21 + o + qb], None, mult)
                ins.then_inc(p_ready, 1)
                if n + 1 < HEADS:
                    band_maxima(n + 1)
                heads_out(n)
            for t in range(KD):
                got(dve, "proja", t % 4, t // 4)
                if t == 0:
                    dve.wait_ge(gates_ready, 2)
                tt_(mix2[:, t, :], ps[t % 4][:, 0:T], gates2[:, KD + t, :], mult).then_inc(evac[t % 4], 1)
            for b in range(4):
                evacuated(dve, "proja", b, 1)
            gated_add("projr", mix2, gates2, 0)
            for t in range(KD):
                got(dve, "wout", t % 4, t // 4)
                tt_(x[:, t, :], x[:, t, :], ps[t % 4][:, 0:T], add).then_inc(evac[t % 4], 1)
            for b in range(4):
                evacuated(dve, "wout", b, 1)
            inverse_root(7, T)
            normalise(x, h, [(0, T, c("nffn", 0, 8), None)])

            aff = tiny[:, 32:64].rearrange("p (t e) -> p t e", e=N_EXP)
            got(dve, "route", 0, 0)
            do(V.tensor_reduce(tiny[:, 16:18], ps[0][:, 0:2 * N_EXP].rearrange("p (t e) -> p t e", e=N_EXP), AXX, mx_op))
            settle()
            ts_(tiny[:, 16:18], tiny[:, 16:18], -1.0, None, mult).then_inc(nm_ready, 1)
            evacuated(dve, "route", 0, 0)
            do(V.reciprocal(tiny[:, 20:22], tiny[:, 20:22]))
            settle()
            for tt in range(2):
                ts_(aff[:, tt, :], aff[:, tt, :], tiny[:, 20 + tt:21 + tt], None, mult).then_inc(aexp, 1)
            E16 = slice(0, N_EXP)
            affT, work, slot = fh[E16, 2 * T:3 * T], fh[E16, 3 * T:4 * T], fh[E16, 0:T]
            gt, eq, run, sel = (sq[E16, i * T:i * T + T] for i in range(4))
            top, n_gt, room = rt[E16, 480:488], rt[E16, 488:489], rt[E16, 489:490]
            got(dve, "route", 1, 0)
            do(V.tensor_copy(affT, ps[1][E16, 0:T]))
            V.tensor_copy(work, ps[1][E16, 0:T]).then_inc(evac[1], 1)
            evacuated(dve, "route", 1, 0)
            settle()
            for i in range(CAP // 8):
                do(V.max(top, work))
                settle()
                if i + 1 < CAP // 8:
                    do(V.match_replace(work, top, work, -1.0))
                    settle()
            do(V.memset(ones2, 1.0))
            do(ts_(gt, affT, top[:, 7:8], 0.0, ALU.is_gt, add, accum_out=n_gt))
            do(ts_(eq, affT, top[:, 7:8], None, ALU.is_equal))
            settle()
            do(ts_(room, n_gt, -1.0, float(CAP), mult, add))
            do(V.tensor_tensor_scan(run, ones2, eq, 0.0, mult, add))
            settle()
            do(stt(eq, run, room, eq, ALU.is_le, mult))
            settle()
            do(tt_(sel, gt, eq, add))
            settle()
            do(V.tensor_tensor_scan(run, ones2, sel, 0.0, mult, add))
            settle()
            tt_(slot, run, sel, mult).then_inc(slot_ready, 1)
            got(dve, "route", 2, 0)
            V.tensor_copy(rt[:, 0:2 * N_EXP], ps[2][:, 0:2 * N_EXP]).then_inc(evac[2], 1)
            evacuated(dve, "route", 2, 0)
            per_expert = [OH[:, tt, :].rearrange("p (e r) -> p e r", r=CAP) for tt in range(2)]
            for lo, hi in ((0, GROUP), (GROUP, N_EXP)):
                for tt in range(2):
                    tt_(per_expert[tt][:, lo:hi, :], iota.unsqueeze(1).to_broadcast([P, hi - lo, CAP]),
                        rt[:, tt * N_EXP + lo:tt * N_EXP + hi].unsqueeze(2).to_broadcast([P, hi - lo, CAP]), ALU.is_equal)\
                        .then_inc(oh_ready, 1)
            got(dve, "gather0", 6, 0)
            V.tensor_copy(xg[:, 4:8, :], ps[6][:, :].rearrange("p (k n) -> p k n", n=P)).then_inc(evac[6], 1)
            dve.wait_ge(oh_ready, 4)
            for tt in range(2):
                tt_(OHW[:, tt, :].rearrange("p (e r) -> p e r", r=CAP), per_expert[tt],
                    aff[:, tt, :].unsqueeze(2).to_broadcast([P, N_EXP, CAP]), mult).then_inc(oh_ready, 1)
            dve.wait_ge(oh_ready, 6)

            def group(i, last=False):
                V.tensor_copy(OHW_g, OHW[:, :, ds(i * P, P)]).then_inc(group_choice, 1)
                for half in range(2):
                    o = slice(half * 512, half * 512 + 512)
                    evacuated(dve, "moe", half, i * 2)
                    got(dve, "moe", 2 + half, i * 2)
                    tt_(hid[:, o], msil[:, o], ps[2 + half][:, :], mult).then_inc(evac[2 + half], 1)
                got(dve, "moe", 7, i)
                V.tensor_copy(OHT, ps[7][:, 0:T]).then_inc(evac[7], 1)
                got(dve, "moe", 6, i * 3)
                V.tensor_copy(hidT[:, 4:8, :], ps[6][:, :].rearrange("p (k n) -> p k n", n=P)).then_inc(evac[6], 1)
                got(dve, "moe", 1, i * 2 + 1)
                V.tensor_copy(ys4[:, 512:1024], ps[1][:, :]).then_inc(evac[1], 1)
                if not last:
                    got(dve, "moe", 6, i * 3 + 1)
                    V.tensor_copy(xg[:, 4:8, :], ps[6][:, :].rearrange("p (k n) -> p k n", n=P)).then_inc(evac[6], 1)
                for n, (b, k) in enumerate(scatter_fills(i, last)):
                    got(dve, "moe", b, k)
                    tt_(x[:, 2 * n:2 * n + 2, :], x[:, 2 * n:2 * n + 2, :], ps[b][:, :].rearrange("p (j n) -> p j n", n=T),
                        add).then_inc(evac[b], 1)
            with dve.Fori(0, N_GROUPS - 1) as i:
                group(i)
            group(N_GROUPS - 1, last=True)
            inverse_root(8, T)
            settle()
            for j in range(KD):
                ins = stt(outb[:, j, :], x[:, j, :], c("nfin", j), rstd[:, 0:T], mult, mult)
                if j % 2:
                    ins.then_inc(out_ready, 1)


def kernel(**inputs):
    import concourse.bacc as bacc
    from concourse.bass_utils import run_bass_kernel_spmd

    nc = bacc.Bacc("TRN2", target_bir_lowering=False, num_devices=1)
    laid = lay_out(inputs)
    dram = {n: nc.dram_tensor(f"{n}_dram", laid[n].shape, mybir.dt.from_np(laid[n].dtype), kind="ExternalInput").ap()
            for n in _ARRAYS}
    out = nc.dram_tensor("out_dram", (P, KD * T), mybir.dt.float32, kind="ExternalOutput").ap()
    build(nc, dram, out)
    r = run_bass_kernel_spmd(nc, [{f"{n}_dram": laid[n] for n in _ARRAYS}], core_ids=[0])
    y = r.results[0]["out_dram"].reshape(P, KD, T)
    return np.ascontiguousarray(y.transpose(2, 1, 0).reshape(1, T, D))
```
